# Optimizing a Trainium2 kernel written in Bass

```python
import math
import jax, jax.numpy as jnp
from jax import lax
import numpy as np
import jax
import jax.numpy as jnp

D_MODEL = 1024
BATCH = 1
SEQ = 256
DEPTH = 2

N_EVEN = (DEPTH + 1) // 2
N_ODD = DEPTH // 2
D_FF = 2816
N_MOD = 9
EPS = 1e-6

ATT_HEADS = 4
ATT_QK_DIM = 64
ATT_V_DIM = 2 * ATT_QK_DIM
QK_COLS = ATT_HEADS * 2 * ATT_QK_DIM
ATT_WIDTH = ATT_HEADS * ATT_V_DIM
Q_BLOCK = 128

POOL_WINDOWS = (2, 4, 8, 16)
POOL_GROUPS = len(POOL_WINDOWS)
POOL_WIDTH = D_MODEL // 2
POOL_GROUP_DIM = POOL_WIDTH // POOL_GROUPS

AB_IN_WIDTH = 2 * QK_COLS + ATT_WIDTH + POOL_WIDTH
MIX_WIDTH = ATT_WIDTH + POOL_WIDTH

CONV_WIDTH = D_MODEL
CONV_K = 3


def rmsnorm(x, g):
    xf = x.astype(jnp.float32)
    y = xf * lax.rsqrt(jnp.mean(xf * xf, axis=-1, keepdims=True) + EPS)
    return (y * g.astype(jnp.float32)).astype(x.dtype)

def modulated_norm(x, g, shift, scale):
    return rmsnorm(x, g) * (1 + scale) + shift

def swiglu(h, wg, wu, wd):
    return (jax.nn.silu(h @ wg) * (h @ wu)) @ wd

def diff_attention(q1, q2, k1, k2, v, lam):
    b, h, s, _ = q1.shape
    nb = s // Q_BLOCK
    scale = ATT_QK_DIM ** -0.5
    kpos = jnp.arange(s)

    def blocks(q):
        return q.reshape(b, h, nb, Q_BLOCK, q.shape[-1]).transpose(2, 0, 1, 3, 4)

    def one_block(args):
        qa, qb, i = args
        qpos = i * Q_BLOCK + jnp.arange(Q_BLOCK)
        mask = kpos[None, :] <= qpos[:, None]

        def probs(q, k):
            sc = jnp.einsum('bhqd,bhkd->bhqk', q, k).astype(jnp.float32) * scale
            sc = jnp.where(mask, sc, -jnp.inf)
            return jax.nn.softmax(sc, axis=-1)

        w = probs(qa, k1) - lam * probs(qb, k2)
        return jnp.einsum('bhqk,bhkd->bhqd', w.astype(v.dtype), v)

    out = lax.map(one_block, (blocks(q1), blocks(q2), jnp.arange(nb)))
    return out.transpose(1, 2, 0, 3, 4).reshape(b, h, s, v.shape[-1])

def multiscale_pool(u, pool_w, pool_scale):
    b, s, _ = u.shape
    uf = u.astype(jnp.float32).reshape(b, s, POOL_GROUPS, POOL_GROUP_DIM)
    cs = jnp.cumsum(uf, axis=1)
    t = jnp.arange(s)
    outs = []
    for g, w in enumerate(POOL_WINDOWS):
        csg = cs[:, :, g]
        lagged = jnp.pad(csg, ((0, 0), (w, 0), (0, 0)))[:, :s]
        cnt = jnp.minimum(t + 1, w).astype(jnp.float32)[None, :, None]
        outs.append((csg - lagged) / cnt - uf[:, :, g])
    d = jnp.stack(outs, axis=2)
    y = jnp.einsum('bsgc,gcd->bsgd', d, pool_w.astype(jnp.float32))
    y = y.reshape(b, s, POOL_WIDTH) * pool_scale.astype(jnp.float32)
    return y.astype(u.dtype)

def attn_pool_mixer(h, layer_idx, w_in, qk_g, lq1, lk1, lq2, lk2, subln_g, pool_w, pool_scale, w_out):
    b, s, _ = h.shape
    proj = h @ w_in
    q, k, v, u = jnp.split(proj, [QK_COLS, 2 * QK_COLS, 2 * QK_COLS + ATT_WIDTH], axis=-1)
    q = rmsnorm(q.reshape(b, s, ATT_HEADS, 2, ATT_QK_DIM), qk_g[0]).transpose(0, 2, 3, 1, 4)
    k = rmsnorm(k.reshape(b, s, ATT_HEADS, 2, ATT_QK_DIM), qk_g[1]).transpose(0, 2, 3, 1, 4)
    v = v.reshape(b, s, ATT_HEADS, ATT_V_DIM).transpose(0, 2, 1, 3)
    lam_init = 0.8 - 0.6 * math.exp(-0.3 * layer_idx)
    f32 = jnp.float32
    lam = (jnp.exp(jnp.sum(lq1.astype(f32) * lk1.astype(f32)))
           - jnp.exp(jnp.sum(lq2.astype(f32) * lk2.astype(f32))) + lam_init)
    o = diff_attention(q[:, :, 0], q[:, :, 1], k[:, :, 0], k[:, :, 1], v, lam)
    o = rmsnorm(o, subln_g) * (1 - lam_init)
    o = o.transpose(0, 2, 1, 3).reshape(b, s, ATT_WIDTH)
    p = multiscale_pool(u, pool_w, pool_scale)
    return jnp.concatenate([o, p], axis=-1) @ w_out

def short_conv_mixer(h, w_in, conv_w, w_out):
    b_gate, c_gate, xin = jnp.split(h @ w_in, 3, axis=-1)
    v = c_gate * xin
    s = v.shape[1]
    vp = jnp.pad(v, ((0, 0), (CONV_K - 1, 0), (0, 0)))
    y = conv_w[0] * vp[:, 0:s]
    for j in range(1, CONV_K):
        y = y + conv_w[j] * vp[:, j:j + s]
    return (b_gate * y) @ w_out

def first_inputs(seed: int = 0) -> dict:
    key = jax.random.key(seed)
    ks = jax.random.split(key, 24)
    f32 = jnp.float32

    def nrm(k, shape, scale):
        return jax.random.normal(k, shape, f32) * scale

    D = D_MODEL
    return {
        "x": nrm(ks[0], (BATCH, SEQ, D), 1.0),
        "c": nrm(ks[1], (BATCH, D), 1.0),
        "norm_g": 1.0 + nrm(ks[2], (DEPTH, 3, D), 0.05),
        "w_ada": nrm(ks[3], (DEPTH, D, N_MOD * D), D ** -0.5),
        "b_ada": nrm(ks[4], (DEPTH, N_MOD * D), 0.02),
        "ffn_wg": nrm(ks[5], (DEPTH, 2, D, D_FF), D ** -0.5),
        "ffn_wu": nrm(ks[6], (DEPTH, 2, D, D_FF), D ** -0.5),
        "ffn_wd": nrm(ks[7], (DEPTH, 2, D_FF, D), D_FF ** -0.5),
        "w_in_ab": nrm(ks[8], (N_EVEN, D, AB_IN_WIDTH), D ** -0.5),
        "qk_norm_g": 1.0 + nrm(ks[9], (N_EVEN, 2, ATT_QK_DIM), 0.05),
        "lambda_q1": nrm(ks[10], (N_EVEN, ATT_QK_DIM), 0.1),
        "lambda_k1": nrm(ks[11], (N_EVEN, ATT_QK_DIM), 0.1),
        "lambda_q2": nrm(ks[12], (N_EVEN, ATT_QK_DIM), 0.1),
        "lambda_k2": nrm(ks[13], (N_EVEN, ATT_QK_DIM), 0.1),
        "subln_g": 1.0 + nrm(ks[14], (N_EVEN, ATT_V_DIM), 0.05),
        "pool_w": nrm(ks[15], (N_EVEN, POOL_GROUPS, POOL_GROUP_DIM, POOL_GROUP_DIM), POOL_GROUP_DIM ** -0.5),
        "pool_scale": 1.0 + nrm(ks[16], (N_EVEN, POOL_WIDTH), 0.1),
        "w_out_ab": nrm(ks[17], (N_EVEN, MIX_WIDTH, D), MIX_WIDTH ** -0.5),
        "w_in_c": nrm(ks[18], (N_ODD, D, 3 * CONV_WIDTH), D ** -0.5),
        "conv_w": nrm(ks[19], (N_ODD, CONV_K, CONV_WIDTH), CONV_K ** -0.5),
        "w_out_c": nrm(ks[20], (N_ODD, CONV_WIDTH, D), CONV_WIDTH ** -0.5),
    }

def first_block(x, c, norm_g, w_ada, b_ada, ffn_wg, ffn_wu, ffn_wd, w_in_ab, qk_norm_g,
              lambda_q1, lambda_k1, lambda_q2, lambda_k2, subln_g, pool_w, pool_scale,
              w_out_ab, w_in_c, conv_w, w_out_c):
    b = x.shape[0]
    c_act = jax.nn.silu(c)
    for l in range(DEPTH):
        mod = (c_act @ w_ada[l] + b_ada[l]).reshape(b, N_MOD, 1, D_MODEL)
        sh1, sc1, g1, sh2, sc2, g2, sh3, sc3, g3 = [mod[:, i] for i in range(N_MOD)]
        h = modulated_norm(x, norm_g[l, 0], sh1, sc1)
        x = x + 0.5 * g1 * swiglu(h, ffn_wg[l, 0], ffn_wu[l, 0], ffn_wd[l, 0])
        h = modulated_norm(x, norm_g[l, 1], sh2, sc2)
        if l % 2 == 0:
            e = l // 2
            m = attn_pool_mixer(h, l, w_in_ab[e], qk_norm_g[e], lambda_q1[e], lambda_k1[e],
                                lambda_q2[e], lambda_k2[e], subln_g[e], pool_w[e],
                                pool_scale[e], w_out_ab[e])
        else:
            o = l // 2
            m = short_conv_mixer(h, w_in_c[o], conv_w[o], w_out_c[o])
        x = x + g2 * m
        h = modulated_norm(x, norm_g[l, 2], sh3, sc3)
        x = x + 0.5 * g3 * swiglu(h, ffn_wg[l, 1], ffn_wu[l, 1], ffn_wd[l, 1])
    return x


DEPTH_2 = 1

ROPE_THETA = 500000.0
NORM_EPS = 1e-6
MLA_HEADS = 8
MLA_NOPE = 64
MLA_ROPE = 32
MLA_V = 64
KV_LORA = 4 * MLA_V
Q_LORA = 3 * KV_LORA
ATTN_Q_BLOCK = 128
MOBA_HEADS = 8
MOBA_HD = 64
MOBA_ROT = MOBA_HD // 4
MOBA_BLOCK = 256
MOBA_TOPK = 3
MOBA_Q_CHUNK = 32
N_GROUPS = 4
EXPERTS_PER_GROUP = 8
N_EXPERTS = N_GROUPS * EXPERTS_PER_GROUP
EXPERT_TOPK = 2
EXPERT_FF = 256
EXPERT_BLOCK = 256
IN_SPLITS = (Q_LORA, KV_LORA, MLA_ROPE,
             MOBA_HEADS * MOBA_HD, MOBA_HEADS * MOBA_HD, MOBA_HEADS * MOBA_HD,
             D_MODEL, D_MODEL)
IN_WIDTH = sum(IN_SPLITS)


def rmsnorm_2(x, g):
    xf = x.astype(jnp.float32)
    y = xf * lax.rsqrt(jnp.mean(xf * xf, axis=-1, keepdims=True) + NORM_EPS)
    return (y * g.astype(jnp.float32)).astype(x.dtype)

def rope_tables(seq, rot_dim):
    half = rot_dim // 2
    inv_freq = jnp.power(ROPE_THETA, -jnp.arange(half, dtype=jnp.float32) / half)
    ang = jnp.arange(seq, dtype=jnp.float32)[:, None] * inv_freq[None, :]
    return jnp.cos(ang), jnp.sin(ang)

def apply_rope(x, cos, sin):
    half = x.shape[-1] // 2
    xf = x.astype(jnp.float32)
    x1, x2 = xf[..., :half], xf[..., half:]
    c = cos[None, :, None, :]
    s = sin[None, :, None, :]
    return jnp.concatenate([x1 * c - x2 * s, x2 * c + x1 * s], axis=-1).astype(x.dtype)

def causal_dense_attention(q, k, v):
    B, S, H, Dq = q.shape
    Dv = v.shape[-1]
    scale = Dq ** -0.5
    nqb = S // ATTN_Q_BLOCK
    q_blocks = q.reshape(B, nqb, ATTN_Q_BLOCK, H, Dq).transpose(1, 0, 2, 3, 4)
    kpos = jnp.arange(S)

    def block(args):
        qi, i = args
        s = jnp.einsum('bqhd,bkhd->bhqk', qi, k).astype(jnp.float32) * scale
        qpos = i * ATTN_Q_BLOCK + jnp.arange(ATTN_Q_BLOCK)
        s = jnp.where(kpos[None, :] <= qpos[:, None], s, -jnp.inf)
        p = jax.nn.softmax(s, axis=-1).astype(v.dtype)
        return jnp.einsum('bhqk,bkhd->bqhd', p, v)

    o = lax.map(block, (q_blocks, jnp.arange(nqb)))
    return o.transpose(1, 0, 2, 3, 4).reshape(B, S, H * Dv)

def mla_attention(c_q, c_kv, k_r, q_norm, w_uq, kv_norm, w_ukv, cos, sin):
    B, S, _ = c_q.shape
    q = (rmsnorm_2(c_q, q_norm) @ w_uq).reshape(B, S, MLA_HEADS, MLA_NOPE + MLA_ROPE)
    q = jnp.concatenate([q[..., :MLA_NOPE], apply_rope(q[..., MLA_NOPE:], cos, sin)], axis=-1)
    kv = (rmsnorm_2(c_kv, kv_norm) @ w_ukv).reshape(B, S, MLA_HEADS, MLA_NOPE + MLA_V)
    k_nope, v = kv[..., :MLA_NOPE], kv[..., MLA_NOPE:]
    k_rope = apply_rope(k_r[:, :, None, :], cos, sin)
    k = jnp.concatenate([k_nope, jnp.broadcast_to(k_rope, (B, S, MLA_HEADS, MLA_ROPE))], axis=-1)
    return causal_dense_attention(q, k, v)

def moba_attention(q, k, v, cos, sin):
    B, S, H, dh = q.shape
    scale = dh ** -0.5
    q = jnp.concatenate([apply_rope(q[..., :MOBA_ROT], cos, sin), q[..., MOBA_ROT:]], axis=-1)
    k = jnp.concatenate([apply_rope(k[..., :MOBA_ROT], cos, sin), k[..., MOBA_ROT:]], axis=-1)
    nb = -(-S // MOBA_BLOCK)
    pad = nb * MOBA_BLOCK - S
    kp = jnp.pad(k, ((0, 0), (0, pad), (0, 0), (0, 0)))
    vp = jnp.pad(v, ((0, 0), (0, pad), (0, 0), (0, 0)))
    k_blocks = kp.reshape(B, nb, MOBA_BLOCK, H, dh).transpose(0, 3, 1, 2, 4)
    v_blocks = vp.reshape(B, nb, MOBA_BLOCK, H, dh).transpose(0, 3, 1, 2, 4)
    k_mean = jnp.mean(k_blocks.astype(jnp.float32), axis=3)
    n_sel = min(MOBA_TOPK, nb)
    gather = jax.vmap(jax.vmap(lambda blocks, idx: blocks[idx]))
    nqc = S // MOBA_Q_CHUNK
    q_chunks = q.reshape(B, nqc, MOBA_Q_CHUNK, H, dh).transpose(1, 0, 3, 2, 4)
    blk_ids = jnp.arange(nb)
    sel_ids = jnp.arange(n_sel)

    def chunk(args):
        qc, c = args
        q0 = c * MOBA_Q_CHUNK
        own = q0 // MOBA_BLOCK
        qpos = q0 + jnp.arange(MOBA_Q_CHUNK)
        gate = jnp.einsum('bhqd,bhnd->bhqn', qc.astype(jnp.float32), k_mean)
        gate = jnp.where(blk_ids < own, gate, -jnp.inf)
        _, idx = lax.top_k(gate, n_sel)
        valid = sel_ids < own
        k_sel = gather(k_blocks, idx)
        v_sel = gather(v_blocks, idx)
        s_sel = jnp.einsum('bhqd,bhqjkd->bhqjk', qc, k_sel).astype(jnp.float32) * scale
        s_sel = jnp.where(valid[:, None], s_sel, -jnp.inf).reshape(B, H, MOBA_Q_CHUNK, n_sel * MOBA_BLOCK)
        k_own = lax.dynamic_index_in_dim(k_blocks, own, axis=2, keepdims=False)
        v_own = lax.dynamic_index_in_dim(v_blocks, own, axis=2, keepdims=False)
        kpos = own * MOBA_BLOCK + jnp.arange(MOBA_BLOCK)
        s_own = jnp.einsum('bhqd,bhkd->bhqk', qc, k_own).astype(jnp.float32) * scale
        s_own = jnp.where(kpos[None, :] <= qpos[:, None], s_own, -jnp.inf)
        p = jax.nn.softmax(jnp.concatenate([s_own, s_sel], axis=-1), axis=-1).astype(v.dtype)
        p_own = p[..., :MOBA_BLOCK]
        p_sel = p[..., MOBA_BLOCK:].reshape(B, H, MOBA_Q_CHUNK, n_sel, MOBA_BLOCK)
        return (jnp.einsum('bhqk,bhkd->bhqd', p_own, v_own)
                + jnp.einsum('bhqjk,bhqjkd->bhqd', p_sel, v_sel))

    o = lax.map(chunk, (q_chunks, jnp.arange(nqc)))
    return o.transpose(1, 0, 3, 2, 4).reshape(B, S, H * dh)

def hierarchical_moe(h, w_rg, b_rg, w_re, b_re, w_g, w_u, w_d):
    B, S, D = h.shape
    T = B * S
    hf = h.reshape(T, D)
    g_logits = (hf @ w_rg + b_rg).astype(jnp.float32)
    g_sel = jnp.argmax(g_logits, axis=-1).astype(jnp.int32)
    p_group = jnp.take_along_axis(jax.nn.softmax(g_logits, axis=-1), g_sel[:, None], axis=1)
    e_logits = (jnp.einsum('td,gde->tge', hf, w_re) + b_re).astype(jnp.float32)
    e_in = jnp.take_along_axis(e_logits, g_sel[:, None, None], axis=1)[:, 0]
    top_vals, top_idx = lax.top_k(e_in, EXPERT_TOPK)
    weight = p_group * jax.nn.softmax(top_vals, axis=-1)
    expert_id = g_sel[:, None] * EXPERTS_PER_GROUP + top_idx.astype(jnp.int32)

    A = T * EXPERT_TOPK
    eid = expert_id.reshape(A)
    w_flat = weight.reshape(A)
    tok = jnp.repeat(jnp.arange(T, dtype=jnp.int32), EXPERT_TOPK)
    order = jnp.argsort(eid, stable=True)
    se = eid[order]
    counts = jnp.bincount(eid, length=N_EXPERTS).astype(jnp.int32)
    padded = (counts + EXPERT_BLOCK - 1) // EXPERT_BLOCK * EXPERT_BLOCK
    start = jnp.cumsum(counts) - counts
    pend = jnp.cumsum(padded)
    pstart = pend - padded
    dest = pstart[se] + jnp.arange(A, dtype=jnp.int32) - start[se]
    n_slots = (-(-A // EXPERT_BLOCK) + N_EXPERTS) * EXPERT_BLOCK
    slot_tok = jnp.zeros((n_slots,), jnp.int32).at[dest].set(tok[order])
    slot_w = jnp.zeros((n_slots,), h.dtype).at[dest].set(w_flat[order].astype(h.dtype))
    n_blocks = n_slots // EXPERT_BLOCK
    blk_e = jnp.minimum(jnp.searchsorted(pend, jnp.arange(n_blocks, dtype=jnp.int32) * EXPERT_BLOCK,
                                         side='right'), N_EXPERTS - 1)
    xs = hf[slot_tok].reshape(n_blocks, EXPERT_BLOCK, D)

    def expert_block(args):
        xb, e = args
        return (jax.nn.silu(xb @ w_g[e]) * (xb @ w_u[e])) @ w_d[e]

    ys = lax.map(expert_block, (xs, blk_e)).reshape(n_slots, D)
    out = jnp.zeros((T, D), h.dtype).at[slot_tok].add(ys * slot_w[:, None])
    return out.reshape(B, S, D)

def second_inputs(seed: int = 0) -> dict:
    key = jax.random.key(seed)
    ks = jax.random.split(key, 20)
    f32 = jnp.float32
    L = DEPTH_2

    def dense(k, shape, fan_in):
        return jax.random.normal(k, shape, f32) * fan_in ** -0.5

    def gain(k, shape):
        return 1.0 + 0.02 * jax.random.normal(k, shape, f32)

    return {
        'x': jax.random.normal(ks[0], (BATCH, SEQ, D_MODEL), f32),
        'attn_norm': gain(ks[1], (L, D_MODEL)),
        'w_in': dense(ks[2], (L, D_MODEL, IN_WIDTH), D_MODEL),
        'q_norm': gain(ks[3], (L, Q_LORA)),
        'w_uq': dense(ks[4], (L, Q_LORA, MLA_HEADS * (MLA_NOPE + MLA_ROPE)), Q_LORA),
        'kv_norm': gain(ks[5], (L, KV_LORA)),
        'w_ukv': dense(ks[6], (L, KV_LORA, MLA_HEADS * (MLA_NOPE + MLA_V)), KV_LORA),
        'w_o_mla': dense(ks[7], (L, MLA_HEADS * MLA_V, D_MODEL), MLA_HEADS * MLA_V),
        'w_o_moba': dense(ks[8], (L, MOBA_HEADS * MOBA_HD, D_MODEL), MOBA_HEADS * MOBA_HD),
        'w_out': dense(ks[9], (L, D_MODEL, D_MODEL), D_MODEL),
        'ffn_norm': gain(ks[10], (L, D_MODEL)),
        'w_router_group': dense(ks[11], (L, D_MODEL, N_GROUPS), D_MODEL),
        'b_router_group': 0.01 * jax.random.normal(ks[12], (L, N_GROUPS), f32),
        'w_router_expert': dense(ks[13], (L, N_GROUPS, D_MODEL, EXPERTS_PER_GROUP), D_MODEL),
        'b_router_expert': 0.01 * jax.random.normal(ks[14], (L, N_GROUPS, EXPERTS_PER_GROUP), f32),
        'w_exp_gate': dense(ks[15], (L, N_EXPERTS, D_MODEL, EXPERT_FF), D_MODEL),
        'w_exp_up': dense(ks[16], (L, N_EXPERTS, D_MODEL, EXPERT_FF), D_MODEL),
        'w_exp_down': dense(ks[17], (L, N_EXPERTS, EXPERT_FF, D_MODEL), EXPERT_FF),
        'final_norm': gain(ks[18], (D_MODEL,)),
    }

def second_block(x, attn_norm, w_in, q_norm, w_uq, kv_norm, w_ukv, w_o_mla, w_o_moba, w_out,
              ffn_norm, w_router_group, b_router_group, w_router_expert, b_router_expert,
              w_exp_gate, w_exp_up, w_exp_down, final_norm):
    B, S, _ = x.shape
    cos_mla, sin_mla = rope_tables(S, MLA_ROPE)
    cos_moba, sin_moba = rope_tables(S, MOBA_ROT)
    split_at = [int(i) for i in np.cumsum(IN_SPLITS)[:-1]]
    for l in range(DEPTH_2):
        h = rmsnorm_2(x, attn_norm[l])
        proj = h @ w_in[l]
        c_q, c_kv, k_r, q_b, k_b, v_b, gate_a, gate_b = jnp.split(proj, split_at, axis=-1)
        o_a = mla_attention(c_q, c_kv, k_r, q_norm[l], w_uq[l], kv_norm[l], w_ukv[l], cos_mla, sin_mla)
        o_b = moba_attention(q_b.reshape(B, S, MOBA_HEADS, MOBA_HD),
                             k_b.reshape(B, S, MOBA_HEADS, MOBA_HD),
                             v_b.reshape(B, S, MOBA_HEADS, MOBA_HD), cos_moba, sin_moba)
        mixed = (jax.nn.sigmoid(gate_a) * (o_a @ w_o_mla[l])
                 + jax.nn.sigmoid(gate_b) * (o_b @ w_o_moba[l]))
        x = x + mixed @ w_out[l]
        x = x + hierarchical_moe(rmsnorm_2(x, ffn_norm[l]), w_router_group[l], b_router_group[l],
                                 w_router_expert[l], b_router_expert[l],
                                 w_exp_gate[l], w_exp_up[l], w_exp_down[l])
    return rmsnorm_2(x, final_norm)


def setup_inputs(seed=0):
    out = dict(first_inputs(seed))
    for name, value in second_inputs(seed + 1).items():
        if name != "x":
            out[name + "_2"] = value
    return out


def reference(
    x, c, norm_g, w_ada, b_ada, ffn_wg, ffn_wu, ffn_wd, w_in_ab, qk_norm_g, lambda_q1,
    lambda_k1, lambda_q2, lambda_k2, subln_g, pool_w, pool_scale, w_out_ab, w_in_c, conv_w,
    w_out_c, attn_norm_2, w_in_2, q_norm_2, w_uq_2, kv_norm_2, w_ukv_2, w_o_mla_2, w_o_moba_2,
    w_out_2, ffn_norm_2, w_router_group_2, b_router_group_2, w_router_expert_2,
    b_router_expert_2, w_exp_gate_2, w_exp_up_2, w_exp_down_2, final_norm_2,
):
    x = first_block(
        x, c, norm_g, w_ada, b_ada, ffn_wg, ffn_wu, ffn_wd, w_in_ab, qk_norm_g, lambda_q1,
        lambda_k1, lambda_q2, lambda_k2, subln_g, pool_w, pool_scale, w_out_ab, w_in_c, conv_w,
        w_out_c,
    )
    return second_block(
        x, attn_norm_2, w_in_2, q_norm_2, w_uq_2, kv_norm_2, w_ukv_2, w_o_mla_2, w_o_moba_2,
        w_out_2, ffn_norm_2, w_router_group_2, b_router_group_2, w_router_expert_2,
        b_router_expert_2, w_exp_gate_2, w_exp_up_2, w_exp_down_2, final_norm_2,
    )


_drawn_inputs = setup_inputs


def setup_inputs(seed=0):
    import zlib

    import numpy as np

    out = dict(_drawn_inputs(seed))
    spreads = {}
    factors = {'qk_norm_g': 3.026,
     'lambda_q1': 8.0,
     'attn_norm_2': 8.0,
     'q_norm_2': 8.0,
     'kv_norm_2': 8.0,
     'ffn_norm_2': 4.344,
     'b_router_group_2': 7.728,
     'b_router_expert_2': 8.0,
     'final_norm_2': 2.805}
    for name, (base, spread) in spreads.items():
        noise = np.random.default_rng([zlib.crc32(name.encode()), seed]).standard_normal(out[name].shape)
        drawn = base * np.exp(spread * noise) if base else spread * noise
        out[name] = jnp.asarray(drawn.astype(out[name].dtype))
    for name, factor in factors.items():
        out[name] = (out[name] * factor).astype(out[name].dtype)
    return out
```

```python
from contextlib import ExitStack

import numpy as np

import concourse.bass as bass
from concourse import mybir

F32 = mybir.dt.float32
F32R = mybir.dt.float32r
ALU = mybir.AluOpType
ACT = mybir.ActivationFunctionType
AX_X = mybir.AxisListType.X

P = 128
T = 256
D = 1024
KT = D // P
F = 2816
CH = 256
NCH = F // CH
NE = 32
NG = 4
EG = NE // NG
NMOD = 9
EPS = 1e-6
BIG = -3.0e38
LAM_INIT = 0.8 - 0.6 * 1.0
UW = 2048

MLA_H, MLA_NOPE, MLA_ROPE, MLA_V = 8, 64, 32, 64
MLA_Q = MLA_NOPE + MLA_ROPE
MOBA_H, MOBA_HD, MOBA_ROT = 8, 64, 16
QL, KVL = 768, 256
C_Q, C_KV, C_KR = 0, QL, QL + KVL
C_QB = C_KR + MLA_ROPE
C_KB, C_VB = C_QB + 512, C_QB + 1024
C_GA, C_GB = C_QB + 1536, C_QB + 1536 + D

STAGES = [
    ("ffn0", NCH), ("mix0", 12), ("ffn1", NCH), ("ffn2", NCH), ("mix1", 16), ("ffn3", NCH),
    ("blk2", 32), ("moe", NE),
]
CHUNKED = ("ffn0", "ffn1", "ffn2", "ffn3", "moe")
KR_UNIT, UQ_UNITS = 4, (12, 13, 14, 15)


def unit_width(stage, u):
    if stage == "blk2" and u == KR_UNIT:
        return KT * MLA_Q
    if stage == "blk2" and u in UQ_UNITS:
        return (QL // P) * 2 * MLA_Q
    return UW


def slot_plan():
    first, widths, chunks, n = {}, [[], [], []], {}, 0
    for stage, units in STAGES:
        first[stage] = [len(w) for w in widths]
        chunks[stage] = n
        if stage in CHUNKED:
            n += units
            for s in range(3):
                widths[s] += [UW] * units
        else:
            for u in range(units):
                widths[u % 3].append(unit_width(stage, u))
    return first, widths, chunks


def constants():
    parts, at = [], {}

    def put(name, a):
        a = np.asarray(a, np.float32)
        full = np.zeros((P, a.shape[1]), np.float32)
        full[: a.shape[0]] = a
        at[name] = (sum(x.shape[1] for x in parts), a.shape[1])
        parts.append(full)

    i = np.arange(P)
    put("ident", np.eye(P))
    put("ones", np.ones((P, P)))
    put("halves", (i[:, None] // 64 == i[None, :] // 64))
    moba = np.zeros((P, P))
    for o in (0, MOBA_HD):
        for r in range(MOBA_ROT // 2):
            moba[o + r + MOBA_ROT // 2, o + r] = -1
            moba[o + r, o + r + MOBA_ROT // 2] = 1
    put("swap_moba", moba)
    mla = np.zeros((P, MLA_ROPE))
    for r in range(MLA_ROPE // 2):
        mla[MLA_NOPE + r + MLA_ROPE // 2, r] = -1
        mla[MLA_NOPE + r, r + MLA_ROPE // 2] = 1
    put("swap_mla", mla)
    put("causal", np.where(i[None, :] <= i[:, None], 0.0, BIG))

    def rope(rot):
        half = rot // 2
        freq = np.power(np.float32(500000.0), -np.arange(half, dtype=np.float32) / np.float32(half)).astype(np.float32)
        ang = (np.arange(T, dtype=np.float32)[:, None] * freq[None, :]).astype(np.float32)
        return np.cos(ang).T, np.sin(ang).T

    cos, sin = rope(MOBA_ROT)
    c, s = np.ones((P, T)), np.zeros((P, T))
    for o in (0, MOBA_HD):
        c[o:o + MOBA_ROT] = np.concatenate([cos, cos])
        s[o:o + MOBA_ROT] = np.concatenate([sin, sin])
    put("cos_moba", c)
    put("sin_moba", s)
    cos, sin = rope(MLA_ROPE)
    c, s = np.ones((P, T)), np.zeros((P, T))
    c[MLA_NOPE:MLA_Q] = np.concatenate([cos, cos])
    s[MLA_NOPE:MLA_Q] = np.concatenate([sin, sin])
    put("cos_mla", c)
    put("sin_mla", s)
    t = np.arange(16)
    put("inv_count", np.tile(np.concatenate([1.0 / np.minimum(t + 1, w) for w in (2, 4, 8, 16)]).astype(np.float32), (P, 1)))
    put("rank", np.tile(np.arange(8, 0, -1), (P, 1)))
    return np.concatenate(parts, axis=1), at


ROWS = {}
_n = 0
for _name, _k in (("c", 8), ("norm_g", 48), ("conv_w", 24), ("pool_scale", 4), ("attn_norm", 8), ("q_norm", 6),
                  ("kv_norm", 2), ("ffn_norm", 8), ("final_norm", 8), ("subln", 1), ("qk_g", 2), ("lam", 4)):
    ROWS[_name] = (_n, _k)
    _n += _k
NROWS = _n


def build(nc, a, const_dram, out):
    first, widths, chunk0 = slot_plan()
    const_np, const_at = constants()

    ctx = ExitStack()
    with ctx:
        def sb(name, shape, dt=F32):
            return ctx.enter_context(nc.sbuf_tensor(name, shape, dt))

        sem_of = {}

        def sem(name):
            if name not in sem_of:
                sem_of[name] = ctx.enter_context(nc.semaphore(name))
            return sem_of[name]

        raw = [sb(f"raw{s}", [P, UW]) for s in range(3)]
        whi = [sb(f"whi{s}", [P, UW], F32R) for s in range(3)]
        wlo = [sb(f"wlo{s}", [P, UW], F32R) for s in range(3)]
        ada_raw = sb("ada_raw", [P, 2, UW])
        xT = sb("xT", [P, KT, T])
        hf = sb("hf", [P, KT, T])
        hhi = sb("hhi", [P, KT, T], F32R)
        hlo = sb("hlo", [P, KT, T], F32R)
        mhi = sb("mhi", [P, KT, T], F32R)
        mlo = sb("mlo", [P, KT, T], F32R)
        act_tile = sb("act_tile", [P, 4 * T])
        silu, hid = act_tile[:, 0:2 * T], act_tile[:, 2 * T:4 * T]
        sq = act_tile[:, :].rearrange("p (i n) -> p i n", i=2)
        hidhi = [sb(f"hidhi{i}", [P, 2, T], F32R) for i in range(2)]
        hidlo = [sb(f"hidlo{i}", [P, 2, T], F32R) for i in range(2)]
        arena = sb("arena", [P, 8192])
        exps = sb("exps", [P, 4, 384])
        probsT = sb("probsT", [P, 2, 384])
        root = sb("root", [P, 2 * T])
        rstd = sb("rstd", [P, 2 * T])
        swapped = exps[:, 0:2, 0:T]
        cst = sb("cst", [P, const_np.shape[1]])
        zeros = sb("zeros", [P, P], F32R)
        vcols = sb("vcols", [P, NROWS])
        bada = sb("bada", [P, 2 * NMOD * KT])
        modv = sb("modv", [P, 2 * NMOD * KT])
        adarow = sb("adarow", [P, T])
        cact = sb("cact", [P, KT])
        gmod = sb("gmod", [P, KT])
        ghalf = sb("ghalf", [P, KT])
        lam = sb("lam", [P, 8])
        negmax = sb("negmax", [P, 4, 2])
        zsum = sb("zsum", [P, 4, 2])
        zinv = sb("zinv", [P, 4, 2])
        wrout = sb("wrout", [P, KT, NG + NE])
        brout = sb("brout", [1, NG + NE])

        def c_(name, rows=slice(0, P)):
            o, n = const_at[name]
            return cst[rows, o:o + n]

        def col(name, k=0, n=1):
            o, _ = ROWS[name]
            return vcols[:, o + k:o + k + n]

        def mod(layer, v, k=None):
            o = (layer * NMOD + v) * KT
            return modv[:, o:o + KT] if k is None else modv[:, o + k:o + k + 1]

        ident, ones = c_("ident"), c_("ones")
        ar = lambda o, n: arena[:, o:o + n]
        xin = ar(0, 2048).rearrange("p (t d) -> p t d", t=2)
        q0 = ar(0, 1024).rearrange("p (h t) -> p h t", h=4)
        k0 = ar(1024, 1024).rearrange("p (h t) -> p h t", h=4)
        v0 = ar(2048, 1024).rearrange("p (t n) -> p t n", t=2)
        PADT = T + 16
        pool_in = ar(3072, 4 * PADT).rearrange("p (g t) -> p g t", g=4)
        pool_a = ar(3072 + 4 * PADT, 4 * PADT).rearrange("p (g t) -> p g t", g=4)
        pool_b = ar(3072 + 8 * PADT, 4 * PADT).rearrange("p (g t) -> p g t", g=4)
        pool_d = ar(3072 + 12 * PADT, 4 * T).rearrange("p (g t) -> p g t", g=4)
        cgate = ar(0, 2 * T)
        vconv = ar(512, 2 * (T + 2)).rearrange("p (g t) -> p g t", g=2)
        yconv = ar(1040, 2 * T).rearrange("p (g t) -> p g t", g=2)
        vA = ar(3072, 1024).rearrange("p (t n) -> p t n", t=2)
        qA = ar(4096, 2048).rearrange("p (h t) -> p h t", h=8)
        kA = ar(6144, 2048).rearrange("p (h t) -> p h t", h=8)
        krope = adarow[:, :]
        poolw = ar(7424, 4 * P).rearrange("p (g n) -> p g n", g=4)
        vrows = ar(2048, P)
        brows = arena[0:72, 2048 + P:2048 + 3 * P].rearrange("p (l n) -> p l n", l=2)
        cbuf = ar(2048, 2 * T).rearrange("p (i t) -> p i t", i=2)
        rt = ar(2560, 256)
        logit = ar(2816, 2 * (NG + NE)).rearrange("p (t n) -> p t n", t=2)
        comb = ar(2888, 2 * NE).rearrange("p (t n) -> p t n", t=2)
        combT = arena[0:NE, 2952:2952 + T]
        gates = ada_raw[:, :, :].rearrange("p g (k t) -> p g k t", k=KT)
        xout = xin

        ps = ctx.enter_context(nc.psum_tensor("ps", [P, 8, 512], F32))
        scratch = nc.dram_tensor("comb_rows", [NE, T], F32, kind="Internal").ap()

        landed = [sem(f"landed{s}") for s in range(3)]
        high = [sem(f"high{s}") for s in range(3)]
        split = [sem(f"split{s}") for s in range(3)]
        used = [sem(f"used{s}") for s in range(3)]
        ada_landed = [sem(f"ada_landed{i}") for i in range(2)]
        ada_used = [sem(f"ada_used{i}") for i in range(2)]

        class Tally:

            def __init__(self, eng):
                self.eng, self.n = eng, {}

            def __call__(self, name, k=1):
                self.n[name] = self.n.get(name, 0) + k
                self.eng.wait_ge(sem(name), self.n[name])

        block = ctx.enter_context(nc.Block())

        def kxn(w, c0, n):
            return w[:, c0:c0 + n].rearrange("(k p) n -> p k n", p=P)

        def dyn(w, c, n=CH):
            return w[:, bass.ds(c * n, n)].rearrange("(k p) n -> p k n", p=P)

        def unit_source(stage, u):
            if stage == "mix0":
                if u < 8:
                    return kxn(a["w_in_ab"][0], (0, 256, 512, 768, 1536, 1792, 1024, 1280)[u], 256)
                return kxn(a["w_out_ab"][0], (u - 8) * 256, 256)
            if stage == "mix1":
                if u < 12:
                    return kxn(a["w_in_c"][0], (D, 2 * D, 0)[u % 3] + (u // 3) * 256, 256)
                return kxn(a["w_out_c"][0], (u - 12) * 256, 256)
            w = a["w_in_2"][0]
            if u < 4:
                return kxn(w, u * 256, 256)
            if u == KR_UNIT:
                return kxn(w, C_KR - MLA_NOPE, MLA_Q)
            if u < 11:
                return kxn(w, C_QB + (u - 5) * 256, 256)
            if u == 11:
                return kxn(a["w_ukv_2"][0], 0, D)
            if u < 16:
                return kxn(a["w_uq_2"][0], (u - 12) * 2 * MLA_Q, 2 * MLA_Q)
            if u < 24:
                return kxn(w, C_GA + (u - 16) * 256, 256)
            if u < 28:
                return kxn(a[("w_o_mla_2", "w_o_moba_2")[u % 2]][0], ((u - 24) // 2) * 512, 512)
            return kxn(a["w_out_2"][0], (u - 28) * 256, 256)

        @block.sync
        def _(sp):
            nsmall = [0]

            def small(dst, src, name="small_landed"):
                sp.dma_start(dst, src).then_inc(sem(name), 16)

            small(xin, a["x"][0].rearrange("(t p) d -> p t d", p=P), "x_landed")
            small(cst[:, :], const_dram, "const_landed")
            sp.wait_ge(sem("rows_cleared"), 1)

            def rows(name, src, cols=slice(0, P)):
                o, n = ROWS[name]
                small(vrows[o:o + n, cols], src, "rows_landed")

            rows("c", a["c"].rearrange("a (k p) -> (a k) p", p=P))
            rows("norm_g", a["norm_g"].rearrange("l n (k p) -> (l n k) p", p=P))
            rows("conv_w", a["conv_w"].rearrange("l n (k p) -> (l n k) p", p=P))
            rows("pool_scale", a["pool_scale"].rearrange("l (k p) -> (l k) p", p=P))
            rows("attn_norm", a["attn_norm_2"].rearrange("l (k p) -> (l k) p", p=P))
            rows("q_norm", a["q_norm_2"].rearrange("l (k p) -> (l k) p", p=P))
            rows("kv_norm", a["kv_norm_2"].rearrange("l (k p) -> (l k) p", p=P))
            rows("ffn_norm", a["ffn_norm_2"].rearrange("l (k p) -> (l k) p", p=P))
            rows("final_norm", a["final_norm_2"].rearrange("(k p) -> k p", p=P))
            rows("subln", a["subln_g"])
            for half in range(2):
                rows("qk_g", a["qk_norm_g"][0], slice(64 * half, 64 * half + 64))
            o, _ = ROWS["lam"]
            for i, name in enumerate(("lambda_q1", "lambda_k1", "lambda_q2", "lambda_k2")):
                small(vrows[o + i:o + i + 1, 0:64], a[name], "rows_landed")
            small(brows[:, :, :], a["b_ada"].rearrange("l (r p) -> r l p", p=P), "rows_landed")

            def ada_load(layer, v, r, n):
                i = r % 2
                if not isinstance(n, int) or n > 0:
                    sp.wait_ge(ada_used[i], n)
                rows_ = a["w_ada"][layer][r * 256:(r + 1) * 256, :]
                src = rows_[:, bass.ds(v * D, D)] if not isinstance(v, int) else rows_[:, v * D:(v + 1) * D]
                sp.dma_start(ada_raw[:, i, :].rearrange("p (k n) -> p k n", k=2),
                             src.rearrange("(k p) n -> p k n", p=P)).then_inc(ada_landed[i], 16)

            def load(s, n, src, width=UW):
                if not isinstance(n, int) or n > 0:
                    sp.wait_ge(split[s], n)
                k = src.shape[1]
                sp.dma_start(raw[s][:, 0:width].rearrange("p (k n) -> p k n", k=k), src).then_inc(landed[s], 16)

            def load_unit(stage, u):
                s = u % 3
                load(s, first[stage][s] + u // 3, unit_source(stage, u), unit_width(stage, u))

            def chunk_loads(stage, wg, wu, wd, ada=None):
                b = first[stage]

                def one(c, quarters=()):
                    load(0, c + b[0], wg(c))
                    load(1, c + b[1], wu(c))
                    for q in quarters:
                        ada_load(*q)
                    load(2, c + b[2], wd(c))

                one(0)
                layer, v0_ = ada if ada else (0, 0)
                with sp.Fori(0, (NCH - 1) // 2) as i:
                    for half in range(2):
                        q = [(layer, i + v0_, r, i * 2 + 2 * (layer * NMOD + v0_) + r // 2)
                             for r in (2 * half, 2 * half + 1)]
                        one(i * 2 + 1 + half, q if ada else ())

            def vector_loads(v):
                for r in range(4):
                    ada_load(v // NMOD, v % NMOD, r, 2 * v + r // 2)

            vector_loads(0)
            vector_loads(1)
            small(poolw[:, :, :], a["pool_w"][0].rearrange("g c d -> c g d"))
            small(wrout[:, :, 0:NG], a["w_router_group_2"][0].rearrange("(k p) g -> p k g", p=P))
            for g in range(NG):
                small(wrout[:, :, NG + EG * g:NG + EG * g + EG],
                      a["w_router_expert_2"][0, g].rearrange("(k p) e -> p k e", p=P))
            small(brout[:, 0:NG], a["b_router_group_2"])
            small(brout[:, NG:NG + NE], a["b_router_expert_2"].rearrange("l g e -> l (g e)"))

            def dense(stage, layer, j, ada):
                wg, wu, wd = a["ffn_wg"][layer, j], a["ffn_wu"][layer, j], a["ffn_wd"][layer, j]

                def down(c):
                    w = wd[bass.ds(c * CH, CH), :] if not isinstance(c, int) else wd[c * CH:(c + 1) * CH, :]
                    return w.rearrange("(k p) n -> p k n", p=P)

                chunk_loads(stage, lambda c: dyn(wg, c) if not isinstance(c, int) else kxn(wg, c * CH, CH),
                            lambda c: dyn(wu, c) if not isinstance(c, int) else kxn(wu, c * CH, CH), down, ada)

            dense("ffn0", 0, 0, (0, 2))
            for u in range(12):
                load_unit("mix0", u)
                if u in (4, 6, 8):
                    vector_loads(7 + (u - 3) // 2)
            dense("ffn1", 0, 1, (1, 1))
            dense("ffn2", 1, 0, None)
            for u in range(16):
                load_unit("mix1", u)
                if u in (5, 8, 11):
                    vector_loads(15 + (u - 3) // 3)
            dense("ffn3", 1, 1, None)
            for u in range(32):
                load_unit("blk2", u)

            b = first["moe"]

            def expert(e, three=(0, 1, 2)):
                srcs = [a["w_exp_gate_2"], a["w_exp_up_2"], a["w_exp_down_2"]]
                for s in three:
                    w = srcs[s][0, e] if isinstance(e, int) else srcs[s][0, bass.ds(e, 1)].rearrange("e k n -> (e k) n")
                    load(s, e + b[s], w.rearrange("(k p) n -> p k n", p=P))

            def weights_row(e, i):
                if not isinstance(e, int) or e >= 2:
                    sp.wait_ge(sem("scaled"), e - 1)
                row = scratch[bass.ds(e, 1), :] if not isinstance(e, int) else scratch[e:e + 1, :]
                sp.dma_start(cbuf[:, i, :], row.to_broadcast([P, T])).then_inc(sem(f"comb_landed{i}"), 16)

            expert(0)
            expert(1)
            sp.wait_ge(sem("combT_ready"), 1)
            sp.dma_start(scratch, combT[:, :]).then_inc(sem("comb_stored"), 16)
            sp.wait_ge(sem("comb_stored"), 16)
            weights_row(0, 0)
            weights_row(1, 1)
            with sp.Fori(0, (NE - 2) // 2) as i:
                for half in range(2):
                    expert(i * 2 + 2 + half)
                    weights_row(i * 2 + 2 + half, half)

            for t in range(2):
                sp.wait_ge(sem("out_ready"), t + 1)
                sp.dma_start(out[0, t * P:(t + 1) * P, :], xout[:, t, :]).then_inc(sem("out_stored"), 16)
            sp.wait_ge(sem("out_stored"), 32)
            sp.wait_ge(sem("comb_stored"), 16)

        @block.gpsimd
        def _(pool):
            wait = Tally(pool)
            n = [0]

            def link(ins):
                n[0] += 1
                ins.then_inc(sem("pool_self"), 1)
                pool.wait_ge(sem("pool_self"), n[0])

            pool.memset(zeros[:, :].bitcast(F32), 0.0).then_inc(sem("zeros_ready"), 1)
            wait("const_landed", 16)
            link(pool.memset(pool_in[:, :, 0:16], 0.0))
            link(pool.memset(pool_a[:, :, 0:16], 0.0))
            link(pool.memset(pool_b[:, :, 0:16], 0.0))
            wait("pool_in_ready", 2)
            src, dst = pool_in, pool_a
            for g, w in enumerate((2, 4, 8, 16)):
                h = w // 2
                link(pool.tensor_tensor(dst[:, g:4, 16:PADT], src[:, g:4, 16:PADT], src[:, g:4, 16 - h:PADT - h], ALU.add))
                o, _ = const_at["inv_count"]
                link(pool.tensor_tensor(pool_d[:, g, 0:16], dst[:, g, 16:32], cst[:, o + g * 16:o + g * 16 + 16], ALU.mult))
                link(pool.tensor_scalar(pool_d[:, g, 16:T], dst[:, g, 32:PADT], 1.0 / w, None, ALU.mult))
                ins = pool.tensor_tensor(pool_d[:, g, :], pool_d[:, g, :], pool_in[:, g, 16:PADT], ALU.subtract)
                if g < 3:
                    link(ins)
                else:
                    ins.then_inc(sem("pooled"), 1)
                if g == 0:
                    src, dst = pool_a, pool_b
                else:
                    src, dst = dst, src

        @block.tensor
        def _(pe):
            wait = Tally(pe)
            freed = {}

            def own(bank):
                if bank in freed:
                    pe.wait_ge(*freed.pop(bank))

            counts = {}

            def frees(bank, name):
                counts[name] = counts.get(name, 0) + 1
                freed[bank] = (sem(name), counts[name])

            def three(o, wh, wl, xh, xl, start, stop, shared=False):
                pe.matmul(o, wh, xh, start=start, stop=False, skip_group_check=shared)
                pe.matmul(o, wh, xl, start=False, stop=False, skip_group_check=shared)
                return pe.matmul(o, wl, xh, start=False, stop=stop, skip_group_check=shared)

            turn = [0, 0, 0]

            def slot_ready(s):
                turn[s] += 1
                pe.wait_ge(split[s], turn[s])

            def feature_major(s, outs, nk, m, xh, xl, k0_=0, step=None, ready=None):
                cols = widths[s][turn[s] - 1] // nk
                wh = whi[s][:, 0:nk * cols].rearrange("p (k n) -> p k n", k=nk)
                wl = wlo[s][:, 0:nk * cols].rearrange("p (k n) -> p k n", k=nk)
                for n, o in enumerate(outs):
                    c = slice(n * (step or m), n * (step or m) + m)
                    for j in range(nk):
                        k = j
                        if ready and n == 0:
                            ready(j)
                        mm = three(o, wh[:, k, c], wl[:, k, c], xh[:, k0_ + k, :], xl[:, k0_ + k, :], j == 0, j == nk - 1)
                mm.then_inc(used[s], 1)

            def bank_pair(b, m=P):
                return [ps[0:m, b, 0:T], ps[0:m, b, T:2 * T]]

            def linear(stage, u, freed_by=None, xh=hhi, xl=hlo, ready=None):
                s, b = u % 3, u % 2
                slot_ready(s)
                own(b)
                feature_major(s, bank_pair(b), KT, P, xh, xl, ready=ready)
                if freed_by:
                    frees(b, freed_by)

            def token_major(stage, u, freed_by):
                s, b = u % 3, u % 2
                slot_ready(s)
                own(b)
                wh = whi[s][:, :].rearrange("p (k n) -> p k n", k=KT)
                wl = wlo[s][:, :].rearrange("p (k n) -> p k n", k=KT)
                for t in range(2):
                    tt = slice(t * P, t * P + P)
                    for k in range(KT):
                        o = ps[:, b, t * T:(t + 1) * T]
                        pe.matmul(o, hhi[:, k, tt], wh[:, k, :], start=(k == 0), stop=False)
                        pe.matmul(o, hhi[:, k, tt], wl[:, k, :], start=False, stop=False)
                        mm = pe.matmul(o, hlo[:, k, tt], wh[:, k, :], start=False, stop=(k == KT - 1))
                mm.then_inc(used[s], 1)
                frees(b, freed_by)

            wait("x_landed", 16)
            wait("const_landed", 16)
            for k in range(KT):
                for t in range(2):
                    mm = pe.transpose(ps[:, 2 + k // 2, (k % 2) * T + t * P:(k % 2) * T + (t + 1) * P],
                                      xin[:, t, k * P:(k + 1) * P], ident)
                if k % 2:
                    mm.then_inc(sem("xT_ready"), 1)
            wait("rows_landed", 16 * 17)
            pe.transpose(ps[:, 7, 0:NROWS], vrows[0:NROWS, :], ident[0:NROWS, 0:NROWS])
            for l in range(2):
                mm = pe.transpose(ps[:, 7, P + 72 * l:P + 72 * l + 72], brows[:, l, :], ident[0:72, 0:72])
            mm.then_inc(sem("vcols_ready"), 1)
            wait("lam_prod")
            pe.matmul(ps[:, 7, 400:402], ones, lam[:, 0:2], start=True, stop=True).then_inc(sem("lam_sum"), 1)

            def ada_quarter(r, n, v_before=None):
                i = r % 2
                pe.wait_ge(ada_landed[i], (n + 1) * 16)
                if r == 0:
                    if not isinstance(v_before, int) or v_before > 0:
                        pe.wait_ge(sem("mod_ready"), v_before)
                for kk in range(2):
                    k = 2 * r + kk
                    for j in range(4):
                        mm = pe.matmul(ps[32 * j:32 * j + 32, 6, 0:T], cact[:, k:k + 1].to_broadcast([P, 32]),
                                       ada_raw[:, i, kk * D + j * T:kk * D + (j + 1) * T],
                                       start=(k == 0), stop=(k == KT - 1))
                mm.then_inc(ada_used[i], 1)

            def ada_turn(v):
                pe.wait_ge(sem("adarow_ready"), v + 1)
                for b in range(2):
                    mm = pe.transpose(ps[:, 6, T + b * P:T + (b + 1) * P], adarow[:, b * P:(b + 1) * P], ident)
                mm.then_inc(sem("adacol_ready"), 1)
                if isinstance(v, int):
                    freed[6] = (sem("mod_ready"), v + 1)

            def ada_vector(v):
                for r in range(4):
                    ada_quarter(r, 2 * v + r // 2, v)

            wait("cact_ready")
            ada_vector(0)
            ada_turn(0)
            ada_vector(1)
            ada_turn(1)

            norms = [0]

            def norm_sums():
                norms[0] += 1
                counts["x_ready"] = 4 * norms[0]
                own(7)
                for k in range(KT):
                    if k % 2 == 0:
                        wait("sq_ready")
                    mm = pe.matmul(ps[:, 7, 0:T], ones, hf[:, k, :], start=(k == 0), stop=(k == KT - 1))
                mm.then_inc(sem("stat_ready"), 1)
                frees(7, "stat_read")

            def chunked(stage, n, layer_v=None, count=NCH):
                b0, ch = first[stage], chunk0[stage]

                def gate(c, e=0):
                    pe.wait_ge(split[0], c + b0[0] + 1)
                    if not (isinstance(c, int) and c + ch == 0):
                        pe.wait_ge(sem("silu_done"), c + ch)
                    halves(0, ps[:, 0, :])

                def up(c):
                    pe.wait_ge(split[1], c + b0[1] + 1)
                    if not (isinstance(c, int) and c + ch == 0):
                        pe.wait_ge(sem("hid_done"), c + ch)
                    halves(1, ps[:, 1, :])

                def halves(s, o):
                    wh = whi[s][:, :].rearrange("p (k n) -> p k n", k=KT)
                    wl = wlo[s][:, :].rearrange("p (k n) -> p k n", k=KT)
                    for m in range(2):
                        for k in range(KT):
                            mm = three(o[:, m * T:(m + 1) * T], wh[:, k, m * P:(m + 1) * P], wl[:, k, m * P:(m + 1) * P],
                                       hhi[:, k, :], hlo[:, k, :], k == 0, k == KT - 1)
                    mm.then_inc(used[s], 1)

                def down(c, parity, last=False):
                    pe.wait_ge(split[2], c + b0[2] + 1)
                    pe.wait_ge(sem("hid_split"), c + ch + 1)
                    wh = whi[2][:, :].rearrange("p (k n) -> p k n", k=2)
                    wl = wlo[2][:, :].rearrange("p (k n) -> p k n", k=2)
                    for m in range(KT):
                        o = ps[:, 2 + m // 2, (m % 2) * T:(m % 2 + 1) * T]
                        for k in range(2):
                            mm = three(o, wh[:, k, m * P:(m + 1) * P], wl[:, k, m * P:(m + 1) * P],
                                       hidhi[parity][:, k, :], hidlo[parity][:, k, :], False, last and k == 1, shared=True)
                    mm.then_inc(used[2], 1)

                for b in range(4):
                    pe.matmul(ps[:, 2 + b, :], zeros[:, :], hhi[:, 0:2, :], start=True, stop=True)
                gate(0)
                up(0)
                with pe.Fori(0, (count - 1) // 2) as i:
                    for half in range(2):
                        c = i * 2 + half
                        gate(c + 1)
                        up(c + 1)
                        if layer_v is not None:
                            for r in (2 * half, 2 * half + 1):
                                ada_quarter(r, i * 2 + 2 * layer_v + r // 2, i + layer_v)
                        down(c, half)
                    if layer_v is not None:
                        ada_turn(i + layer_v)
                c = (count - 1) // 2 * 2
                if c < count - 1:
                    gate(c + 1)
                    up(c + 1)
                    down(c, c % 2)
                    c += 1
                down(c, c % 2, last=True)
                for s in range(3):
                    turn[s] = b0[s] + count

            norm_sums()
            wait("zeros_ready")
            wait("h_ready", KT)
            chunked("ffn0", 0, 2)

            def square_sums(weights, i, b, n=2 * T, start=True, stop=True, o=0):
                own(b)
                return pe.matmul(ps[:, b, o:o + n], weights, sq[:, i, 0:n], start=start, stop=stop)

            def qk_sums(i):
                wait("sq_done")
                square_sums(c_("halves"), i % 2, 7).then_inc(sem("stat_ready"), 1)
                frees(7, "stat_read")

            norm_sums()
            wait("h_ready", KT)
            for u in range(8):
                if u < 6:
                    linear("mix0", u, "sq_done" if u < 4 else "pool_in_ready")
                else:
                    token_major("mix0", u, "v_ready")
                if u in (1, 3, 5):
                    ada_vector(7 + u // 2)
                if u in (2, 4, 6):
                    ada_turn(7 + u // 2 - 1)
                if 1 <= u <= 4:
                    qk_sums(u - 1)

            def scores(i, q, k):
                b = 2 + i % 4
                own(b)
                pe.matmul(ps[:, b, 0:P], q[:, 0:P], k[:, 0:P], start=True, stop=True)
                pe.matmul(ps[:, b, P:3 * P], q[:, P:2 * P], k[:, 0:2 * P], start=True, stop=True).then_inc(sem("scores_ready"), 1)
                frees(b, "exp_done")

            def probs_turn(e):
                own(7)
                wait("probs_ready")
                for j in range(3):
                    mm = pe.transpose(ps[:, 7, j * P:(j + 1) * P], exps[:, e, j * P:(j + 1) * P], ident)
                mm.then_inc(sem("turned"), 1)
                frees(7, "probsT_ready")

            def values(i, o, v):
                wait("probsT_ready")
                p = probsT[:, i % 2, :]
                pe.matmul(o, v[0], p[:, 0:T], start=True, stop=False)
                return pe.matmul(o[:, P:T], v[1], p[:, T:3 * P], start=False, stop=True)

            wait("qk_ready", 4)
            wait("v_ready", 2)

            def diff_scores(h):
                for half in range(2):
                    rows = slice(64 * half, 64 * half + 64)
                    scores(2 * h + half, q0[rows, h, :], k0[rows, h, :])

            diff_scores(0)
            for h in range(4):
                if h < 3:
                    diff_scores(h + 1)
                probs_turn((2 * h) % 4)
                if h % 2 == 0:
                    own(6)
                mm = values(h, ps[:, 6, (h % 2) * T:(h % 2 + 1) * T], [v0[:, t, h * P:(h + 1) * P] for t in range(2)])
                if h % 2:
                    mm.then_inc(sem("o_ready"), 1)
                    frees(6, "o_read")
            wait("pooled")
            wait("small_landed", 16 * 8)
            for j in range(2):
                own(j)
                for g in range(2):
                    mm = pe.matmul(ps[:, j, g * T:(g + 1) * T], poolw[:, 2 * j + g, :], pool_d[:, 2 * j + g, :], start=True, stop=True)
                mm.then_inc(sem("pool_out"), 1)
                frees(j, "pool_read")
            wait("o_read", 2)
            for j in range(2):
                square_sums(ones, j, j).then_inc(sem("stat_ready"), 1)
                frees(j, "stat_read")

            def outputs(stage, u0, ready=None):
                for j in range(4):
                    linear(stage, u0 + j, "x_ready", mhi, mlo, ready if j == 0 else None)

            def mix_ready(j):
                if j == 0:
                    wait("mix_split", 4)

            outputs("mix0", 8, mix_ready)

            norm_sums()
            wait("h_ready", KT)
            chunked("ffn1", 1, 10)
            norm_sums()
            wait("h_ready", KT)
            chunked("ffn2", 2)

            norm_sums()
            wait("h_ready", KT)
            for u in range(12):
                linear("mix1", u, ("evacuated", "v_done", "y_done")[u % 3])
                if u in (2, 5, 8):
                    ada_vector(15 + u // 3)
                if u in (3, 6, 9):
                    ada_turn(15 + u // 3 - 1)
            outputs("mix1", 12, lambda k: wait("mix_split") if k % 2 == 0 else None)
            norm_sums()
            wait("h_ready", KT)
            chunked("ffn3", 3)

            norm_sums()
            wait("h_ready", KT)

            def rope(r):
                b = (7, 6)[r % 2]
                own(b)
                wait("rope_in")
                if r == 0:
                    mm = pe.matmul(ps[64:96, b, 0:T], c_("swap_mla", slice(64, 96)), krope[64:96, :], start=True, stop=True)
                elif r < 5:
                    src = q0[:, 2 * (r - 1):2 * r, :] if r < 3 else k0[:, 2 * (r - 3):2 * (r - 2), :]
                    mm = pe.matmul(ps[:, b, :], c_("swap_moba"), src, start=True, stop=True)
                else:
                    mm = pe.matmul(ps[64:96, b, :], c_("swap_mla", slice(64, 96)), qA[64:96, 2 * (r - 5):2 * (r - 4), :],
                                   start=True, stop=True)
                mm.then_inc(sem("rope_swapped"), 1)
                frees(b, "rope_read")

            def latent_sums(j):
                wait("sq_done")
                b = 7 if j < 3 else 6
                if j in (0, 3):
                    own(b)
                for n in range(2):
                    mm = pe.matmul(ps[:, b, 0:T], ones, sq[:, j % 2, n * T:(n + 1) * T],
                                   start=(j in (0, 3) and n == 0), stop=(j >= 2 and n == 1))
                mm.then_inc(sem("sums_done"), 1)
                if j >= 2:
                    frees(b, "stat_read")

            for u in range(4):
                linear("blk2", u, "sq_done")
                if u:
                    latent_sums(u - 1)
            slot_ready(1)
            own(0)
            feature_major(1, [ps[0:MLA_Q, 0, 0:T]], KT, MLA_Q, hhi, hlo)
            frees(0, "rope_in")
            latent_sums(3)
            linear("blk2", 5, "rope_in")
            rope(0)
            for u in range(6, 9):
                linear("blk2", u, "rope_in")
                rope(u - 5)
            token_major("blk2", 9, "v_ready")
            rope(4)
            token_major("blk2", 10, "v_ready")
            slot_ready(2)
            wait("latent_split", 2)
            wh = whi[2][:, :].rearrange("p (k h n) -> p k h n", k=2, h=MLA_H)
            wl = wlo[2][:, :].rearrange("p (k h n) -> p k h n", k=2, h=MLA_H)
            for h in range(MLA_H):
                for k in range(2):
                    three(ps[:, 2 + h // 2, (h % 2) * T:(h % 2 + 1) * T], wh[:, k, h, :], wl[:, k, h, :],
                          mhi[:, 6 + k, :], mlo[:, 6 + k, :], k == 0, k == 1)
            for t in range(2):
                own(t)
                tt = slice(t * P, t * P + P)
                for k in range(2):
                    pe.matmul(ps[:, t, :], mhi[:, 6 + k, tt], wh[:, k, :, 64:], start=(k == 0), stop=False)
                    pe.matmul(ps[:, t, :], mhi[:, 6 + k, tt], wl[:, k, :, 64:], start=False, stop=False)
                    mm = pe.matmul(ps[:, t, :], mlo[:, 6 + k, tt], wh[:, k, :, 64:], start=False, stop=(k == 1))
                frees(t, "ukv_v_read")
            mm.then_inc(used[2], 1)
            for u in UQ_UNITS:
                s, b = u % 3, u % 2
                slot_ready(s)
                own(b)
                feature_major(s, bank_pair(b, MLA_Q), QL // P, MLA_Q, mhi, mlo)
                frees(b, "rope_in")
                if u > UQ_UNITS[0]:
                    rope(5 + u - UQ_UNITS[0] - 1)
            rope(8)
            wait("ukv_k_read", 1)
            wait("v_ready", 2)
            wait("roped", 5)

            def head(i):
                if i < MOBA_H:
                    r = slice(64 * (i % 2), 64 * (i % 2) + 64)
                    scores(i, q0[r, i // 2, :], k0[r, i // 2, :])
                else:
                    if i == MOBA_H:
                        wait("roped", 4)
                    scores(i, qA[0:MLA_Q, i - 8, :], kA[0:MLA_Q, i - 8, :])

            head(0)
            for i in range(16):
                if i < 15:
                    head(i + 1)
                if i % 2 == 0:
                    linear("blk2", 16 + i // 2, "evacuated")
                probs_turn(i % 4)
                if i % 2 == 0:
                    own(6)
                r = slice(64 * (i % 2), 64 * (i % 2) + 64)
                v, c = (v0, i) if i < MOBA_H else (vA, i - 8)
                mm = values(i, ps[r, 6, 0:T], [v[:, t, c * 64:(c + 1) * 64] for t in range(2)])
                mm.then_inc(sem("o_ready"), 1)
                if i % 2:
                    frees(6, "o_split")
            wait("o_split", 8)
            for j in range(2):
                for which in range(2):
                    u = 24 + 2 * j + which
                    s = u % 3
                    b = (2, 4, 0, 6)[2 * j + which]
                    slot_ready(s)
                    own(b)
                    own(b + 1)
                    feature_major(s, bank_pair(b) + bank_pair(b + 1), 4, P, mhi, mlo, k0_=4 * which)
            wait("mixed_split", 2)
            for j in range(4):
                linear("blk2", 28 + j, "x_ready")

            norm_sums()
            wait("h_ready", KT)
            own(7)
            for t in range(2):
                o = ps[:, 7, 64 * t:64 * t + NG + NE]
                pe.matmul(o, ones[0:1, :], brout[:, :], start=True, stop=False)
                for k in range(KT):
                    mm = pe.matmul(o, hf[:, k, t * P:(t + 1) * P], wrout[:, k, :], start=False, stop=(k == KT - 1))
            mm.then_inc(sem("logits_ready"), 1)
            wait("comb_ready")
            for t in range(2):
                mm = pe.transpose(ps[0:NE, 6, t * P:(t + 1) * P], comb[:, t, :], ident)
            mm.then_inc(sem("comb_turned"), 1)
            chunked("moe", 4, None, NE)

            norm_sums()
            for k in range(KT):
                pe.wait_ge(sem("t_ready"), 8 * KT + k + 1)
                for t in range(2):
                    b = 2 * t + k // 4
                    mm = pe.transpose(ps[:, b, (k % 4) * P:(k % 4 + 1) * P], hf[:, k, t * P:(t + 1) * P], ident)
            mm.then_inc(sem("out_turned"), 1)

        @block.scalar
        def _(act):
            wait = Tally(act)
            turn = [0, 0, 0]

            def split_high(s, n, width=UW, after_use=True):
                act.wait_ge(landed[s], (n + 1) * 16)
                if not isinstance(n, int) or n > 0:
                    act.wait_ge(used[s], n)
                act.activation(whi[s][:, 0:width], raw[s][:, 0:width], ACT.Copy).then_inc(high[s], 1)

            def refill(s):
                n = turn[s]
                if n < len(widths[s]):
                    split_high(s, n, widths[s][n])
                    turn[s] += 1

            def copy(o, i, scale=1.0):
                return act.activation(o, i, ACT.Copy, scale=scale)

            def norm(last=False, final=False):
                for pr in range(4):
                    wait("x_ready")
                    act.activation(hf[:, 2 * pr:2 * pr + 2, :], xT[:, 2 * pr:2 * pr + 2, :], ACT.Square).then_inc(sem("sq_ready"), 1)
                roots(D, T)

            def roots(width, n, b=7, o=0):
                wait("stat_ready")
                act.activation(root[:, o:o + n], ps[:, b, 0:n], ACT.Sqrt, bias=eps[:, 0:1], scale=1.0 / width).then_inc(sem("stat_read"), 1)

            def norm_high(shift):
                for k in range(KT):
                    wait("t_ready")
                    if shift is None:
                        copy(hhi[:, k, :], hf[:, k, :]).then_inc(sem("h_high"), 1)
                    else:
                        act.activation(hhi[:, k, :], hf[:, k, :], ACT.Identity, bias=shift[:, k:k + 1]).then_inc(sem("h_high"), 1)

            eps = lam[:, 7:8]
            wait("vcols_done")
            act.activation(cact[:, :], col("c", 0, KT), ACT.Silu).then_inc(sem("cact_ready"), 1)
            wait("lam_sum")
            act.activation(lam[:, 2:4], ps[:, 7, 400:402], ACT.Exp).then_inc(sem("lam_exp"), 1)
            for s in range(3):
                refill(s)
            norm()
            norm_high(mod(0, 0))

            def chunked(stage, count=NCH):
                b0, ch = first[stage], chunk0[stage]

                def gate(c):
                    act.wait_ge(used[0], c + b0[0] + 1)
                    if not (isinstance(c, int) and c + ch == 0):
                        act.wait_ge(sem("hid_done"), c + ch)
                    act.activation(silu[:, :], ps[:, 0, :], ACT.Silu).then_inc(sem("silu_done"), 1)

                def high_hidden(c, parity):
                    if stage == "moe":
                        act.wait_ge(sem("scaled"), c + 1)
                    else:
                        act.wait_ge(sem("hid_done"), c + ch + 1)
                    if not (isinstance(c, int) and c < 2):
                        act.wait_ge(used[2], c + b0[2] - 1)
                    act.activation(hidhi[parity][:, :, :], hid[:, :].rearrange("p (k t) -> p k t", k=2), ACT.Copy).then_inc(sem("hid_high"), 1)

                def chunk(c, parity, down=True, more=True):
                    gate(c)
                    if more:
                        split_high(0, c + b0[0] + 1)
                    high_hidden(c, parity)
                    if more:
                        split_high(1, c + b0[1] + 1)
                    if down:
                        split_high(2, c + b0[2])

                more = stage != "moe"
                chunk(0, 0, down=False)
                with act.Fori(0, (count - 1) // 2) as i:
                    for half in range(2):
                        chunk(i * 2 + 1 + half, (1 + half) % 2)
                c = (count - 1) // 2 * 2
                if c < count - 1:
                    chunk(c + 1, (c + 1) % 2, more=False)
                    c += 1
                if more:
                    split_high(2, b0[2] + count)
                for s in range(3):
                    turn[s] = b0[s] + count + 1

            chunked("ffn0")
            norm()
            norm_high(mod(0, 3))

            def pair(b, rows=P):
                return ps[0:rows, b, :].rearrange("p (n t) -> p n t", n=2)

            for u in range(8):
                s, b = u % 3, u % 2
                act.wait_ge(used[s], first["mix0"][s] + u // 3 + 1)
                if u < 4:
                    dst = (q0 if u < 2 else k0)[:, 2 * (u % 2):2 * (u % 2) + 2, :]
                    copy(dst, pair(b)).then_inc(sem("qk_copied"), 1)
                    act.activation(sq[:, u % 2, :], ps[:, b, :], ACT.Square).then_inc(sem("sq_done"), 1)
                elif u < 6:
                    copy(pool_in[:, 2 * (u - 4):2 * (u - 4) + 2, 16:PADT], pair(b)).then_inc(sem("pool_in_ready"), 1)
                else:
                    copy(v0[:, :, 256 * (u - 6):256 * (u - 5)], pair(b)).then_inc(sem("v_ready"), 1)
                refill(s)
                if 1 <= u <= 4:
                    if u > 1:
                        wait("qk_ready")
                    roots(64, 2 * T)

            def exps_of(i):
                wait("negmax_ready")
                e, b = i % 4, 2 + i % 4
                act.activation(exps[:, e, 0:P], ps[:, b, 0:P], ACT.Exp, bias=negmax[:, e, 0:1], accum_out=zsum[:, e, 0:1])
                act.activation(exps[:, e, P:3 * P], ps[:, b, P:3 * P], ACT.Exp, bias=negmax[:, e, 1:2],
                               accum_out=zsum[:, e, 1:2]).then_inc(sem("exp_done"), 1)

            def probsT_of(i):
                wait("turned")
                copy(probsT[:, i % 2, :], ps[:, 7, 0:3 * P]).then_inc(sem("probsT_ready"), 1)

            exps_of(0)
            exps_of(1)
            for h in range(4):
                if h < 3:
                    exps_of(2 * h + 2)
                    exps_of(2 * h + 3)
                probsT_of(h)
                if h % 2:
                    j = h // 2
                    wait("o_ready")
                    copy(hf[:, 2 * j:2 * j + 2, :], pair(6)).then_inc(sem("o_copied"), 1)
                    act.activation(sq[:, j, :], ps[:, 6, :], ACT.Square).then_inc(sem("o_read"), 1)
            for j in range(2):
                wait("pool_out")
                for g in range(2):
                    k = 2 * j + g
                    act.activation(hf[:, 4 + k, :], ps[:, j, g * T:(g + 1) * T], ACT.Copy,
                                   scale=col("pool_scale", k)).then_inc(sem("pool_read_half" if g == 0 else "pool_read"), 1)
            for j in range(2):
                act.wait_ge(sem("pool_read_half"), j + 1)
                act.wait_ge(sem("pool_read"), j + 1)
                copy(mhi[:, 4 + 2 * j:6 + 2 * j, :], hf[:, 4 + 2 * j:6 + 2 * j, :]).then_inc(sem("mix_high"), 1)
            wait("qk_ready")
            for j in range(2):
                if j:
                    wait("o_normed")
                roots(P, 2 * T, b=j)
            wait("o_normed")
            for j in range(2):
                copy(mhi[:, 2 * j:2 * j + 2, :], hf[:, 2 * j:2 * j + 2, :]).then_inc(sem("mix_high"), 1)
            for u in range(8, 12):
                refill(u % 3)
            norm()
            norm_high(mod(0, 6))
            chunked("ffn1")
            norm()
            norm_high(mod(1, 0))
            chunked("ffn2")

            norm()
            norm_high(mod(1, 3))
            for u in range(12):
                s, b = u % 3, u % 2
                act.wait_ge(used[s], first["mix1"][s] + u // 3 + 1)
                if u % 3 == 0:
                    if u:
                        wait("v_done")
                    copy(cgate, ps[:, b, :]).then_inc(sem("evacuated"), 1)
                refill(s)
                if u % 3 == 2:
                    j = u // 3
                    wait("y_done")
                    copy(mhi[:, 2 * j:2 * j + 2, :], hf[:, 2 * j:2 * j + 2, :]).then_inc(sem("mix_high"), 1)
            for u in range(12, 16):
                refill(u % 3)
            norm()
            norm_high(mod(1, 6))
            chunked("ffn3")

            norm()
            norm_high(None)

            def latent_high(j):
                wait("latent_normed")
                sl = slice(0, 6) if j == 0 else slice(6, 8)
                copy(mhi[:, sl, :], hf[:, sl, :]).then_inc(sem("latent_high"), 1)

            for u in range(11):
                s, b = u % 3, u % 2
                act.wait_ge(used[s], first["blk2"][s] + u // 3 + 1)
                if u < 4:
                    if u >= 2:
                        wait("sums_done")
                    copy(hf[:, 2 * u:2 * u + 2, :], pair(b)).then_inc(sem("latent_copied"), 1)
                    act.activation(sq[:, u % 2, :], ps[:, b, :], ACT.Square).then_inc(sem("sq_done"), 1)
                elif u == KR_UNIT:
                    copy(krope[64:96, :], ps[64:96, b, 0:T]).then_inc(sem("rope_in"), 1)
                elif u < 9:
                    j = u - 5
                    dst = (q0 if j < 2 else k0)[:, 2 * (j % 2):2 * (j % 2) + 2, :]
                    copy(dst, pair(b), MOBA_HD ** -0.5 if j < 2 else 1.0).then_inc(sem("rope_in"), 1)
                else:
                    copy(v0[:, :, 256 * (u - 9):256 * (u - 8)], pair(b)).then_inc(sem("v_ready"), 1)
                refill(s)
                if u == 4:
                    wait("sums_done")
                    act.activation(root[:, 0:T], ps[:, 7, 0:T], ACT.Sqrt, bias=eps, scale=1.0 / QL).then_inc(sem("stat_read"), 1)
                if u == 5:
                    wait("sums_done")
                    act.activation(root[:, T:2 * T], ps[:, 6, 0:T], ACT.Sqrt, bias=eps, scale=1.0 / KVL).then_inc(sem("stat_read"), 1)
                if u == 7:
                    latent_high(0)
                    latent_high(1)
            act.wait_ge(used[2], first["blk2"][2] + 11 // 3 + 1)
            for j in range(4):
                ins = copy(kA[0:64, 2 * j:2 * j + 2, :], pair(2 + j, 64))
            ins.then_inc(sem("ukv_k_read"), 1)
            for t in range(2):
                copy(vA[:, t, :], ps[:, t, :]).then_inc(sem("ukv_v_read"), 1)
            refill(2)
            for u in UQ_UNITS:
                s, b = u % 3, u % 2
                act.wait_ge(used[s], first["blk2"][s] + u // 3 + 1)
                i = u - UQ_UNITS[0]
                copy(qA[0:MLA_Q, 2 * i:2 * i + 2, :], pair(b, MLA_Q), MLA_Q ** -0.5).then_inc(sem("rope_in"), 1)
                refill(s)

            exps_of(0)
            for i in range(16):
                if i < 15:
                    exps_of(i + 1)
                if i % 2 == 0:
                    g = i // 2
                    u = 16 + g
                    act.wait_ge(used[u % 3], first["blk2"][u % 3] + u // 3 + 1)
                    act.activation(gates[:, g // 4, 2 * (g % 4):2 * (g % 4) + 2, :], pair(u % 2), ACT.Sigmoid).then_inc(sem("evacuated"), 1)
                    refill(u % 3)
                probsT_of(i)
                if i % 2:
                    j = i // 2
                    wait("o_ready", 2)
                    tile_ = 4 + j if j < 4 else j - 4
                    copy(mhi[:, tile_, :], ps[:, 6, 0:T]).then_inc(sem("o_high"), 1)
            for j in range(2):
                refill((24 + 2 * j) % 3)
                refill((25 + 2 * j) % 3)
                wait("mixed")
                copy(hhi[:, 4 * j:4 * j + 4, :], hf[:, 4 * j:4 * j + 4, :]).then_inc(sem("mixed_high"), 1)
            for u in range(28, 32):
                refill(u % 3)

            norm()
            norm_high(None)
            wait("router_max")
            act.activation(rt[:, 64:72], rt[:, 56:64], ACT.Exp).then_inc(sem("router_exp"), 1)
            wait("router_two")
            act.activation(rt[:, 130:132], rt[:, 128:130], ACT.Exp).then_inc(sem("router_exp"), 1)
            wait("comb_turned")
            copy(combT[:, :], ps[0:NE, 6, 0:T]).then_inc(sem("combT_ready"), 1)
            chunked("moe", NE)
            norm()
            wait("out_turned")
            for t in range(2):
                ins = copy(xout[:, t, :].rearrange("p (b n) -> p b n", b=2), ps[:, 2 * t:2 * t + 2, :]).then_inc(sem("out_ready"), 1)

        @block.vector
        def _(dve):
            wait = Tally(dve)
            turn = [0, 0, 0]
            n_self = [0]

            def link(ins):
                n_self[0] += 1
                ins.then_inc(sem("dve_self"), 1)
                dve.wait_ge(sem("dve_self"), n_self[0])

            def split_low(s, n, width=UW):
                dve.wait_ge(high[s], n + 1)
                dve.tensor_tensor(wlo[s][:, 0:width], raw[s][:, 0:width], whi[s][:, 0:width].bitcast(F32),
                                  ALU.subtract).then_inc(split[s], 1)

            def refill(s):
                n = turn[s]
                if n < len(widths[s]):
                    split_low(s, n, widths[s][n])
                    turn[s] += 1

            def stt(o, i0, s, i1, op0=ALU.mult, op1=ALU.add):
                return dve.scalar_tensor_tensor(out=o, in0=i0, scalar=s, in1=i1, op0=op0, op1=op1)

            link(dve.memset(lam[:, :], EPS))
            dve.memset(vrows[:, :], 0.0).then_inc(sem("rows_cleared"), 1)
            for pr in range(4):
                wait("xT_ready")
                dve.tensor_copy(xT[:, 2 * pr:2 * pr + 2, :], ps[:, 2 + pr, :].rearrange("p (n t) -> p n t", n=2)).then_inc(sem("x_ready"), 1)
            wait("vcols_ready")
            link(dve.tensor_copy(bada[:, :], ps[:, 7, P:P + 144]))
            link(dve.tensor_copy(vcols[:, :], ps[:, 7, 0:NROWS]))
            link(dve.tensor_scalar(col("subln"), col("subln"), 1.0 - LAM_INIT, None, ALU.mult))
            dve.tensor_scalar(col("lam", 0), col("lam", 0), 1.0, None, ALU.mult).then_inc(sem("vcols_done"), 1)
            dve.wait_ge(sem("vcols_done"), 1)
            link(dve.tensor_tensor(lam[:, 0:1], col("lam", 0), col("lam", 1), ALU.mult))
            dve.tensor_tensor(lam[:, 1:2], col("lam", 2), col("lam", 3), ALU.mult).then_inc(sem("lam_prod"), 1)
            wait("lam_exp")
            link(dve.tensor_tensor(lam[:, 4:5], lam[:, 3:4], lam[:, 2:3], ALU.subtract))
            link(dve.tensor_scalar(lam[:, 4:5], lam[:, 4:5], LAM_INIT, None, ALU.subtract))

            def ada_rows(v):
                dve.wait_ge(ada_used[1], v * 2 + 2)
                dve.tensor_copy(adarow[:, :], ps[:, 6, 0:T]).then_inc(sem("adarow_ready"), 1)

            def ada_mod(v):
                dve.wait_ge(sem("adacol_ready"), v + 1)
                src = ps[:, 6, T:2 * T].rearrange("p (b j r) -> p j b r", b=2, j=4)[:, :, :, 0]
                sl = bass.ds(v * KT, KT) if not isinstance(v, int) else slice(v * KT, (v + 1) * KT)
                dve.tensor_tensor(modv[:, sl].rearrange("p (j b) -> p j b", j=4), src,
                                  bada[:, sl].rearrange("p (j b) -> p j b", j=4), ALU.add).then_inc(sem("mod_ready"), 1)

            ada_rows(0)
            ada_mod(0)
            ada_rows(1)
            ada_mod(1)
            for s in range(3):
                refill(s)

            def norm(gain, shift, scale=None, final=False, vectors=0):
                if scale is not None:
                    dve.wait_ge(sem("mod_ready"), vectors)
                    link(stt(gmod[:, :], scale, 1.0, gain, ALU.add, ALU.mult))
                    gain = gmod
                wait("stat_read")
                link(dve.reciprocal(rstd[:, 0:T], root[:, 0:T]))

                def scaled(k):
                    stt(hf[:, k, :], xT[:, k, :], gain[:, k:k + 1], rstd[:, 0:T], ALU.mult, ALU.mult).then_inc(sem("t_ready"), 1)

                def low(k):
                    wait("h_high")
                    if shift is None:
                        ins = dve.tensor_tensor(hlo[:, k, :], hf[:, k, :], hhi[:, k, :].bitcast(F32), ALU.subtract)
                    else:
                        ins = stt(hlo[:, k, :], hf[:, k, :], shift[:, k:k + 1], hhi[:, k, :].bitcast(F32), ALU.add, ALU.subtract)
                    ins.then_inc(sem("h_ready"), 1)

                for k in range(KT):
                    scaled(k)
                    if k and not final:
                        low(k - 1)
                if not final:
                    low(KT - 1)

            def ng(l, i):
                return col("norm_g", (l * 3 + i) * KT, KT)

            norm(ng(0, 0), mod(0, 0), mod(0, 1), vectors=2)

            def chunked(stage, vec=None, count=NCH, moe=False):
                b0, ch = first[stage], chunk0[stage]

                def hidden(c, parity):
                    dve.wait_ge(sem("silu_done"), c + ch + 1)
                    dve.wait_ge(used[1], c + b0[1] + 1)
                    if moe:
                        dve.tensor_tensor(hid[:, :], silu[:, :], ps[:, 1, :], ALU.mult).then_inc(sem("hid_done"), 1)
                        dve.wait_ge(sem("hid_done"), c + ch + 1)
                        dve.wait_ge(sem(f"comb_landed{parity}"), ((c - parity) * 8 + 16))
                        h3 = hid[:, :].rearrange("p (k t) -> p k t", k=2)
                        dve.tensor_tensor(h3, h3, cbuf[:, parity:parity + 1, :].to_broadcast([P, 2, T]), ALU.mult).then_inc(sem("scaled"), 1)
                    else:
                        dve.tensor_tensor(hid[:, :], silu[:, :], ps[:, 1, :], ALU.mult).then_inc(sem("hid_done"), 1)

                def hidden_low(c, parity):
                    dve.wait_ge(sem("hid_high"), c + ch + 1)
                    dve.tensor_tensor(hidlo[parity][:, :, :], hid[:, :].rearrange("p (k t) -> p k t", k=2),
                                      hidhi[parity][:, :, :].bitcast(F32), ALU.subtract).then_inc(sem("hid_split"), 1)

                def chunk(c, parity, down=True, more=True):
                    if more:
                        split_low(0, c + b0[0] + 1)
                    hidden(c, parity)
                    hidden_low(c, parity)
                    if more:
                        split_low(1, c + b0[1] + 1)
                    if down:
                        split_low(2, c + b0[2])

                more = stage != "moe"
                chunk(0, 0, down=False)
                with dve.Fori(0, (count - 1) // 2) as i:
                    for half in range(2):
                        chunk(i * 2 + 1 + half, (1 + half) % 2)
                        if half and vec is not None:
                            ada_rows(i + vec)
                            ada_mod(i + vec)
                c = (count - 1) // 2 * 2
                if c < count - 1:
                    chunk(c + 1, (c + 1) % 2, more=False)
                    c += 1
                if more:
                    split_low(2, b0[2] + count)
                for s in range(3):
                    turn[s] = b0[s] + count + 1
                dve.wait_ge(used[2], b0[2] + count)

            def add_output(scale=None, half=False, vectors=0):
                if half:
                    dve.wait_ge(sem("mod_ready"), vectors)
                    link(dve.tensor_scalar(ghalf[:, :], scale, 0.5, None, ALU.mult))
                    scale = ghalf
                for k in range(KT):
                    src = ps[:, 2 + k // 2, (k % 2) * T:(k % 2 + 1) * T]
                    if scale is None:
                        if k % 2 == 0:
                            continue
                        ins = dve.tensor_tensor(xT[:, k - 1:k + 1, :], ps[:, 2 + k // 2, :].rearrange("p (n t) -> p n t", n=2),
                                                xT[:, k - 1:k + 1, :], ALU.add)
                    else:
                        ins = stt(xT[:, k, :], src, scale[:, k:k + 1], xT[:, k, :])
                    if k % 2:
                        ins.then_inc(sem("x_ready"), 1)

            def add_units(stage, u0, gate):
                for j in range(4):
                    s, b = (u0 + j) % 3, (u0 + j) % 2
                    dve.wait_ge(used[s], first[stage][s] + (u0 + j) // 3 + 1)
                    if gate is None:
                        dve.tensor_tensor(xT[:, 2 * j:2 * j + 2, :], ps[:, b, :].rearrange("p (n t) -> p n t", n=2),
                                          xT[:, 2 * j:2 * j + 2, :], ALU.add).then_inc(sem("x_ready"), 1)
                    else:
                        stt(xT[:, 2 * j, :], ps[:, b, 0:T], gate[:, 2 * j:2 * j + 1], xT[:, 2 * j, :])
                        stt(xT[:, 2 * j + 1, :], ps[:, b, T:2 * T], gate[:, 2 * j + 1:2 * j + 2], xT[:, 2 * j + 1, :]).then_inc(sem("x_ready"), 1)
                    refill(s)

            chunked("ffn0", 2)
            add_output(mod(0, 2), half=True, vectors=3)
            norm(ng(0, 1), mod(0, 3), mod(0, 4), vectors=5)

            def mix_low(sl):
                wait("mix_high")
                dve.tensor_tensor(mlo[:, sl, :], hf[:, sl, :], mhi[:, sl, :].bitcast(F32), ALU.subtract).then_inc(sem("mix_split"), 1)

            def qk_norm(i):
                wait("stat_read")
                link(dve.reciprocal(rstd[:, :], root[:, :]))
                dst = (q0 if i < 2 else k0)[:, 2 * (i % 2):2 * (i % 2) + 2, :]
                stt(dst, dst, qk_gain[:, i // 2:i // 2 + 1], rstd[:, :].rearrange("p (n t) -> p n t", n=2), ALU.mult, ALU.mult).then_inc(sem("qk_ready"), 1)

            qk_gain = col("qk_g", 0, 2)
            link(dve.tensor_scalar(qk_gain[:, 0:1], qk_gain[:, 0:1], 64 ** -0.5, None, ALU.mult))
            for u in range(8):
                refill(u % 3)
                if u in (1, 3, 5):
                    ada_rows(7 + u // 2)
                if u in (2, 4, 6):
                    ada_mod(7 + u // 2 - 1)
                if 1 <= u <= 4:
                    qk_norm(u - 1)

            causal = c_("causal")

            def negative_max(i):
                wait("scores_ready")
                e, b = i % 4, 2 + i % 4
                diag = ps[:, b, :].rearrange("p (j n) -> p j n", j=2)[:, :, 0:P]
                link(dve.tensor_tensor(diag, diag, causal.rearrange("p (o n) -> p o n", o=1).to_broadcast([P, 2, P]), ALU.add))
                dve.tensor_reduce(negmax[:, e, 0:1], ps[:, b, 0:P], AX_X, ALU.max, negate=True)
                dve.tensor_reduce(negmax[:, e, 1:2], ps[:, b, P:3 * P], AX_X, ALU.max, negate=True).then_inc(sem("negmax_ready"), 1)

            negative_max(0)
            negative_max(1)
            for h in range(4):
                if h < 3:
                    negative_max(2 * h + 2)
                    negative_max(2 * h + 3)
                e = (2 * h) % 4
                wait("exp_done", 2)
                link(dve.reciprocal(zinv[:, e:e + 2, :], zsum[:, e:e + 2, :]))
                link(dve.tensor_scalar(zinv[:, e + 1, :], zinv[:, e + 1, :], lam[:, 4:5], None, ALU.mult))
                pa = [exps[:, e, 0:P], exps[:, e, P:3 * P]]
                pb = [exps[:, e + 1, 0:P], exps[:, e + 1, P:3 * P]]
                dve.tensor_scalar(pa[0], pa[0], zinv[:, e, 0:1], None, ALU.mult)
                link(dve.tensor_scalar(pa[1], pa[1], zinv[:, e, 1:2], None, ALU.mult))
                stt(pa[0], pb[0], zinv[:, e + 1, 0:1], pa[0])
                stt(pa[1], pb[1], zinv[:, e + 1, 1:2], pa[1]).then_inc(sem("probs_ready"), 1)
            mix_low(slice(4, 6))
            mix_low(slice(6, 8))
            for j in range(2):
                wait("stat_read")
                link(dve.reciprocal(rstd[:, :], root[:, :]))
                stt(hf[:, 2 * j:2 * j + 2, :], hf[:, 2 * j:2 * j + 2, :], col("subln"), rstd[:, :].rearrange("p (n t) -> p n t", n=2),
                    ALU.mult, ALU.mult).then_inc(sem("o_normed"), 1)
            mix_low(slice(0, 2))
            mix_low(slice(2, 4))
            add_units("mix0", 8, mod(0, 5))
            norm(ng(0, 2), mod(0, 6), mod(0, 7), vectors=8)
            chunked("ffn1", 10)
            add_output(mod(0, 8), half=True, vectors=9)
            norm(ng(1, 0), mod(1, 0), mod(1, 1), vectors=11)
            chunked("ffn2")
            add_output(mod(1, 2), half=True, vectors=12)

            norm(ng(1, 1), mod(1, 3), mod(1, 4), vectors=14)
            link(dve.memset(vconv[:, :, 0:2], 0.0))
            for j in range(4):
                refill(0)
                if j:
                    ada_mod(15 + j - 1)
                u = 3 * j + 1
                wait("evacuated")
                dve.wait_ge(used[1], first["mix1"][1] + j + 1)
                dve.tensor_tensor(vconv[:, :, 2:T + 2], cgate.rearrange("p (n t) -> p n t", n=2),
                                  ps[:, u % 2, :].rearrange("p (n t) -> p n t", n=2), ALU.mult).then_inc(sem("v_done"), 1)
                refill(1)
                dve.wait_ge(sem("v_done"), j + 1)
                for tap in range(3):
                    for m in range(2):
                        w = col("conv_w", tap * KT + 2 * j + m)
                        if tap == 0:
                            ins = dve.tensor_scalar(yconv[:, m, :], vconv[:, m, 0:T], w, None, ALU.mult)
                        else:
                            ins = stt(yconv[:, m, :], vconv[:, m, tap:tap + T], w, yconv[:, m, :])
                        if m:
                            link(ins)
                dve.wait_ge(used[2], first["mix1"][2] + j + 1)
                dve.tensor_tensor(hf[:, 2 * j:2 * j + 2, :], yconv, ps[:, (u + 1) % 2, :].rearrange("p (n t) -> p n t", n=2),
                                  ALU.mult).then_inc(sem("y_done"), 1)
                refill(2)
                if j < 3:
                    ada_rows(15 + j)
                mix_low(slice(2 * j, 2 * j + 2))
            add_units("mix1", 12, mod(1, 5))
            norm(ng(1, 2), mod(1, 6), mod(1, 7), vectors=17)
            chunked("ffn3")
            add_output(mod(1, 8), half=True, vectors=18)

            norm(col("attn_norm", 0, KT), None)
            cos_b, sin_b, cos_a, sin_a = (c_(x) for x in ("cos_moba", "sin_moba", "cos_mla", "sin_mla"))

            def both(t, rows):
                return t[rows, :].rearrange("p (o t) -> p o t", o=1).to_broadcast([rows.stop - rows.start, 2, T])

            def rope(r):
                wait("rope_swapped")
                if r:
                    dve.wait_ge(sem("roped"), r)
                b = (7, 6)[r % 2]
                if r == 0:
                    rows = slice(64, 96)
                    dve.tensor_tensor(swapped[rows, 0, :], ps[rows, b, 0:T], sin_a[rows, :], ALU.mult).then_inc(sem("rope_read"), 1)
                    link(dve.tensor_tensor(krope[rows, :], krope[rows, :], cos_a[rows, :], ALU.mult))
                    dve.wait_ge(sem("rope_read"), r + 1)
                    link(dve.tensor_tensor(krope[rows, :], krope[rows, :], swapped[rows, 0, :], ALU.add))
                    dve.tensor_copy(kA[rows, :, :], krope[rows, :].rearrange("p (o t) -> p o t", o=1).to_broadcast([32, MLA_H, T])).then_inc(sem("roped"), 1)
                    return
                if r < 5:
                    rows, c, s = slice(0, P), cos_b, sin_b
                    x = q0[:, 2 * (r - 1):2 * r, :] if r < 3 else k0[:, 2 * (r - 3):2 * (r - 2), :]
                else:
                    rows, c, s = slice(64, 96), cos_a, sin_a
                    x = qA[rows, 2 * (r - 5):2 * (r - 4), :]
                sw = swapped[rows, :, :]
                dve.tensor_tensor(sw, ps[rows, b, :].rearrange("p (n t) -> p n t", n=2), both(s, rows), ALU.mult).then_inc(sem("rope_read"), 1)
                link(dve.tensor_tensor(x, x, both(c, rows), ALU.mult))
                dve.wait_ge(sem("rope_read"), r + 1)
                dve.tensor_tensor(x, x, sw, ALU.add).then_inc(sem("roped"), 1)

            def latent(j):
                wait("stat_read")
                sl = slice(j * T, (j + 1) * T)
                link(dve.reciprocal(rstd[:, sl], root[:, sl]))
                for k in range(*((0, 6) if j == 0 else (6, 8))):
                    g = col("q_norm", k) if j == 0 else col("kv_norm", k - 6)
                    ins = stt(hf[:, k, :], hf[:, k, :], g, rstd[:, sl], ALU.mult, ALU.mult)
                ins.then_inc(sem("latent_normed"), 1)

            def latent_low(j):
                wait("latent_high")
                sl = slice(0, 6) if j == 0 else slice(6, 8)
                dve.tensor_tensor(mlo[:, sl, :], hf[:, sl, :], mhi[:, sl, :].bitcast(F32), ALU.subtract).then_inc(sem("latent_split"), 1)

            for u in range(11):
                refill(u % 3)
                if u == 4:
                    latent(0)
                if u == 5:
                    latent(1)
                    rope(0)
                if 6 <= u < 10:
                    rope(u - 5)
                if u == 8:
                    latent_low(0)
                    latent_low(1)
            refill(2)
            for u in UQ_UNITS:
                refill(u % 3)
                if u > UQ_UNITS[0]:
                    rope(5 + u - UQ_UNITS[0] - 1)
            rope(8)

            negative_max(0)
            for i in range(16):
                if i < 15:
                    negative_max(i + 1)
                if i % 2 == 0:
                    refill((16 + i // 2) % 3)
                e = i % 4
                wait("exp_done")
                link(dve.reciprocal(zinv[:, e, :], zsum[:, e, :]))
                dve.tensor_scalar(exps[:, e, 0:P], exps[:, e, 0:P], zinv[:, e, 0:1], None, ALU.mult)
                dve.tensor_scalar(exps[:, e, P:3 * P], exps[:, e, P:3 * P], zinv[:, e, 1:2], None, ALU.mult).then_inc(sem("probs_ready"), 1)
                if i % 2:
                    j = i // 2
                    tile_ = 4 + j if j < 4 else j - 4
                    wait("o_high")
                    dve.tensor_tensor(mlo[:, tile_, :], ps[:, 6, 0:T], mhi[:, tile_, :].bitcast(F32), ALU.subtract).then_inc(sem("o_split"), 1)
            for j in range(2):
                banks = ((2, 4), (0, 6))[j]
                for which in range(2):
                    u = 24 + 2 * j + which
                    refill(u % 3)
                for which in range(2):
                    u = 24 + 2 * j + which
                    dve.wait_ge(used[u % 3], first["blk2"][u % 3] + u // 3 + 1)
                    g = gates[:, which, 4 * j:4 * j + 4, :]
                    src = ps[:, banks[which]:banks[which] + 2, :].rearrange("p b (n t) -> p (b n) t", n=2)
                    link(dve.tensor_tensor(hf[:, 4 * j:4 * j + 4, :] if which == 0 else g, g, src, ALU.mult))
                dve.tensor_tensor(hf[:, 4 * j:4 * j + 4, :], hf[:, 4 * j:4 * j + 4, :], gates[:, 1, 4 * j:4 * j + 4, :], ALU.add).then_inc(sem("mixed"), 1)
                wait("mixed_high")
                dve.tensor_tensor(hlo[:, 4 * j:4 * j + 4, :], hf[:, 4 * j:4 * j + 4, :], hhi[:, 4 * j:4 * j + 4, :].bitcast(F32),
                                  ALU.subtract).then_inc(sem("mixed_split"), 1)
            add_units("blk2", 28, None)

            norm(col("ffn_norm", 0, KT), None)
            wait("logits_ready")
            link(dve.tensor_copy(logit[:, :, :], ps[:, 7, 0:P].rearrange("p (t n) -> p t n", t=2)[:, :, 0:NG + NE]))
            rank = c_("rank")

            def r_(o, n):
                return rt[:, o:o + 2 * n].rearrange("p (t n) -> p t n", t=2)

            def spread(x, n):
                return x.to_broadcast([P, 2, n])

            def first_best(x, best, cand, hot, n):
                link(dve.tensor_reduce(best, x, AX_X, ALU.max))
                link(dve.tensor_tensor(cand, x, spread(best, n), ALU.is_equal))
                link(dve.tensor_tensor(cand, cand, rank[:, 8 - n:8].rearrange("p (o n) -> p o n", o=1).to_broadcast([P, 2, n]), ALU.mult))
                link(dve.tensor_reduce(r_(252, 1), cand, AX_X, ALU.max))
                link(dve.tensor_tensor(hot, cand, spread(r_(252, 1), n), ALU.is_equal))

            gl = logit[:, :, 0:NG]
            el = logit[:, :, NG:NG + NE].rearrange("p t (g e) -> p t g e", g=NG)
            gbest, ghot, gcand = r_(0, 1), r_(2, NG), r_(10, NG)
            first_best(gl, gbest, gcand, ghot, NG)
            dve.tensor_tensor(r_(56, NG), gl, spread(gbest, NG), ALU.subtract).then_inc(sem("router_max"), 1)
            wait("router_exp")
            pg = r_(18, 1)
            link(dve.tensor_reduce(pg, r_(64, NG), AX_X, ALU.add))
            link(dve.reciprocal(pg, pg))
            picked = r_(72, EG)
            link(dve.tensor_tensor(picked, el[:, :, 0, :], spread(ghot[:, :, 0:1], EG), ALU.mult))
            tmp = r_(88, EG)
            for g in range(1, NG):
                link(dve.tensor_tensor(tmp, el[:, :, g, :], spread(ghot[:, :, g:g + 1], EG), ALU.mult))
                link(dve.tensor_tensor(picked, picked, tmp, ALU.add))
            best1, hot1 = r_(20, 1), r_(104, EG)
            first_best(picked, best1, tmp, hot1, EG)
            rest = r_(136, EG)
            link(dve.tensor_scalar(rest, hot1, BIG, None, ALU.mult))
            link(dve.tensor_tensor(rest, rest, picked, ALU.add))
            best2, hot2 = r_(22, 1), r_(152, EG)
            first_best(rest, best2, tmp, hot2, EG)
            dve.tensor_tensor(r_(128, 1), best2, best1, ALU.subtract).then_inc(sem("router_two"), 1)
            wait("router_exp")
            w1, w2 = r_(24, 1), r_(26, 1)
            link(dve.tensor_scalar(w1, r_(130, 1), 1.0, None, ALU.add))
            link(dve.reciprocal(w1, w1))
            link(dve.tensor_tensor(w1, w1, pg, ALU.mult))
            link(dve.tensor_tensor(w2, w1, r_(130, 1), ALU.mult))
            link(dve.tensor_tensor(hot1, hot1, spread(w1, EG), ALU.mult))
            link(dve.tensor_tensor(hot2, hot2, spread(w2, EG), ALU.mult))
            link(dve.tensor_tensor(hot1, hot1, hot2, ALU.add))
            for g in range(NG):
                ins = dve.tensor_tensor(comb[:, :, EG * g:EG * g + EG], hot1, spread(ghot[:, :, g:g + 1], EG), ALU.mult)
            ins.then_inc(sem("comb_ready"), 1)

            chunked("moe", None, NE, moe=True)
            add_output(None)
            norm(col("final_norm", 0, KT), None, final=True)


_INS = ["x", "c", "norm_g", "w_ada", "b_ada", "ffn_wg", "ffn_wu", "ffn_wd", "w_in_ab", "qk_norm_g", "lambda_q1",
        "lambda_k1", "lambda_q2", "lambda_k2", "subln_g", "pool_w", "pool_scale", "w_out_ab", "w_in_c", "conv_w",
        "w_out_c", "attn_norm_2", "w_in_2", "q_norm_2", "w_uq_2", "kv_norm_2", "w_ukv_2", "w_o_mla_2", "w_o_moba_2",
        "w_out_2", "ffn_norm_2", "w_router_group_2", "b_router_group_2", "w_router_expert_2", "b_router_expert_2",
        "w_exp_gate_2", "w_exp_up_2", "w_exp_down_2", "final_norm_2"]


def kernel(**inputs):
    import concourse.bacc as _bacc
    from concourse.bass_utils import run_bass_kernel_spmd as _run

    nc = _bacc.Bacc("TRN2", target_bir_lowering=False, num_devices=1)
    arrays, aps = {}, {}
    for name in _INS:
        a = np.ascontiguousarray(inputs[name])
        arrays[f"in_{name}_dram"] = a
        aps[name] = nc.dram_tensor(f"in_{name}_dram", a.shape, mybir.dt.from_np(a.dtype), kind="ExternalInput").ap()
    table, _ = constants()
    arrays["const_dram"] = table
    const_dram = nc.dram_tensor("const_dram", table.shape, F32, kind="ExternalInput").ap()
    out = nc.dram_tensor("out_0_dram", (1, T, D), F32, kind="ExternalOutput").ap()
    build(nc, aps, const_dram, out)
    r = _run(nc, [arrays], core_ids=[0])
    return r.results[0]["out_0_dram"]
```

```python
from contextlib import ExitStack

import numpy as np

import concourse.bass as bass
from concourse import mybir

F32 = mybir.dt.float32
F32R = mybir.dt.float32r
ALU = mybir.AluOpType
ACT = mybir.ActivationFunctionType
AX_X = mybir.AxisListType.X

P = 128
T = 256
D = 1024
KT = D // P
F = 2816
CH = 256
NCH = F // CH
NE = 32
NG = 4
EG = NE // NG
NMOD = 9
EPS = 1e-6
BIG = -3.0e38
LAM_INIT = 0.8 - 0.6 * 1.0
UW = 2048

MLA_H, MLA_NOPE, MLA_ROPE, MLA_V = 8, 64, 32, 64
MLA_Q = MLA_NOPE + MLA_ROPE
MOBA_H, MOBA_HD, MOBA_ROT = 8, 64, 16
QL, KVL = 768, 256
C_Q, C_KV, C_KR = 0, QL, QL + KVL
C_QB = C_KR + MLA_ROPE
C_KB, C_VB = C_QB + 512, C_QB + 1024
C_GA, C_GB = C_QB + 1536, C_QB + 1536 + D

STAGES = [
    ("ffn0", NCH), ("mix0", 12), ("ffn1", NCH), ("ffn2", NCH), ("mix1", 16), ("ffn3", NCH),
    ("blk2", 32), ("moe", NE),
]
CHUNKED = ("ffn0", "ffn1", "ffn2", "ffn3", "moe")
KR_UNIT, UQ_UNITS = 4, (12, 13, 14, 15)


def unit_width(stage, u):
    if stage == "blk2" and u == KR_UNIT:
        return KT * MLA_Q
    if stage == "blk2" and u in UQ_UNITS:
        return (QL // P) * 2 * MLA_Q
    return UW


def slot_plan():
    first, widths, chunks, n = {}, [[], [], []], {}, 0
    for stage, units in STAGES:
        first[stage] = [len(w) for w in widths]
        chunks[stage] = n
        if stage in CHUNKED:
            n += units
            for s in range(3):
                widths[s] += [UW] * units
        else:
            for u in range(units):
                widths[u % 3].append(unit_width(stage, u))
    return first, widths, chunks


def constants():
    parts, at = [], {}

    def put(name, a):
        a = np.asarray(a, np.float32)
        full = np.zeros((P, a.shape[1]), np.float32)
        full[: a.shape[0]] = a
        at[name] = (sum(x.shape[1] for x in parts), a.shape[1])
        parts.append(full)

    i = np.arange(P)
    put("ident", np.eye(P))
    put("ones", np.ones((P, P)))
    put("halves", (i[:, None] // 64 == i[None, :] // 64))
    moba = np.zeros((P, P))
    for o in (0, MOBA_HD):
        for r in range(MOBA_ROT // 2):
            moba[o + r + MOBA_ROT // 2, o + r] = -1
            moba[o + r, o + r + MOBA_ROT // 2] = 1
    put("swap_moba", moba)
    mla = np.zeros((P, MLA_ROPE))
    for r in range(MLA_ROPE // 2):
        mla[MLA_NOPE + r + MLA_ROPE // 2, r] = -1
        mla[MLA_NOPE + r, r + MLA_ROPE // 2] = 1
    put("swap_mla", mla)
    put("causal", np.where(i[None, :] <= i[:, None], 0.0, BIG))

    def rope(rot):
        half = rot // 2
        freq = np.power(np.float32(500000.0), -np.arange(half, dtype=np.float32) / np.float32(half)).astype(np.float32)
        ang = (np.arange(T, dtype=np.float32)[:, None] * freq[None, :]).astype(np.float32)
        return np.cos(ang).T, np.sin(ang).T

    cos, sin = rope(MOBA_ROT)
    c, s = np.ones((P, T)), np.zeros((P, T))
    for o in (0, MOBA_HD):
        c[o:o + MOBA_ROT] = np.concatenate([cos, cos])
        s[o:o + MOBA_ROT] = np.concatenate([sin, sin])
    put("cos_moba", c)
    put("sin_moba", s)
    cos, sin = rope(MLA_ROPE)
    c, s = np.ones((P, T)), np.zeros((P, T))
    c[MLA_NOPE:MLA_Q] = np.concatenate([cos, cos])
    s[MLA_NOPE:MLA_Q] = np.concatenate([sin, sin])
    put("cos_mla", c)
    put("sin_mla", s)
    t = np.arange(16)
    put("inv_count", np.tile(np.concatenate([1.0 / np.minimum(t + 1, w) for w in (2, 4, 8, 16)]).astype(np.float32), (P, 1)))
    put("rank", np.tile(np.arange(8, 0, -1), (P, 1)))
    return np.concatenate(parts, axis=1), at


ROWS = {}
_n = 0
for _name, _k in (("c", 8), ("norm_g", 48), ("conv_w", 24), ("pool_scale", 4), ("attn_norm", 8), ("q_norm", 6),
                  ("kv_norm", 2), ("ffn_norm", 8), ("final_norm", 8), ("subln", 1), ("qk_g", 2), ("lam", 4)):
    ROWS[_name] = (_n, _k)
    _n += _k
NROWS = _n


def build(nc, a, const_dram, out):
    first, widths, chunk0 = slot_plan()
    const_np, const_at = constants()

    ctx = ExitStack()
    with ctx:
        def sb(name, shape, dt=F32):
            return ctx.enter_context(nc.sbuf_tensor(name, shape, dt))

        sem_of = {}

        def sem(name):
            if name not in sem_of:
                sem_of[name] = ctx.enter_context(nc.semaphore(name))
            return sem_of[name]

        raw = [sb(f"raw{s}", [P, UW]) for s in range(3)]
        whi = [sb(f"whi{s}", [P, UW], F32R) for s in range(3)]
        wlo = [sb(f"wlo{s}", [P, UW], F32R) for s in range(3)]
        ada_raw = sb("ada_raw", [P, 2, UW])
        xT = sb("xT", [P, KT, T])
        hf = sb("hf", [P, KT, T])
        hhi = sb("hhi", [P, KT, T], F32R)
        hlo = sb("hlo", [P, KT, T], F32R)
        mhi = sb("mhi", [P, KT, T], F32R)
        mlo = sb("mlo", [P, KT, T], F32R)
        act_tile = sb("act_tile", [P, 4 * T])
        silu, hid = act_tile[:, 0:2 * T], act_tile[:, 2 * T:4 * T]
        sq = act_tile[:, :].rearrange("p (i n) -> p i n", i=2)
        hidhi = [sb(f"hidhi{i}", [P, 2, T], F32R) for i in range(2)]
        hidlo = [sb(f"hidlo{i}", [P, 2, T], F32R) for i in range(2)]
        arena = sb("arena", [P, 8192])
        exps = sb("exps", [P, 4, 384])
        probsT = sb("probsT", [P, 2, 384])
        root = sb("root", [P, 2 * T])
        rstd = sb("rstd", [P, 2 * T])
        swapped = exps[:, 0:2, 0:T]
        cst = sb("cst", [P, const_np.shape[1]])
        zeros = sb("zeros", [P, P], F32R)
        vcols = sb("vcols", [P, NROWS])
        bada = sb("bada", [P, 2 * NMOD * KT])
        modv = sb("modv", [P, 2 * NMOD * KT])
        adarow = sb("adarow", [P, T])
        cact = sb("cact", [P, KT])
        gmod = sb("gmod", [P, KT])
        ghalf = sb("ghalf", [P, KT])
        lam = sb("lam", [P, 8])
        negmax = sb("negmax", [P, 4, 2])
        zsum = sb("zsum", [P, 4, 2])
        zinv = sb("zinv", [P, 4, 2])
        wrout = sb("wrout", [P, KT, NG + NE])
        brout = sb("brout", [1, NG + NE])

        def c_(name, rows=slice(0, P)):
            o, n = const_at[name]
            return cst[rows, o:o + n]

        def col(name, k=0, n=1):
            o, _ = ROWS[name]
            return vcols[:, o + k:o + k + n]

        def mod(layer, v, k=None):
            o = (layer * NMOD + v) * KT
            return modv[:, o:o + KT] if k is None else modv[:, o + k:o + k + 1]

        ident, ones = c_("ident"), c_("ones")
        ar = lambda o, n: arena[:, o:o + n]
        xin = ar(0, 2048).rearrange("p (t d) -> p t d", t=2)
        q0 = ar(0, 1024).rearrange("p (h t) -> p h t", h=4)
        k0 = ar(1024, 1024).rearrange("p (h t) -> p h t", h=4)
        v0 = ar(2048, 1024).rearrange("p (t n) -> p t n", t=2)
        PADT = T + 16
        pool_in = ar(3072, 4 * PADT).rearrange("p (g t) -> p g t", g=4)
        pool_a = ar(3072 + 4 * PADT, 4 * PADT).rearrange("p (g t) -> p g t", g=4)
        pool_b = ar(3072 + 8 * PADT, 4 * PADT).rearrange("p (g t) -> p g t", g=4)
        pool_d = ar(3072 + 12 * PADT, 4 * T).rearrange("p (g t) -> p g t", g=4)
        cgate = ar(0, 2 * T)
        vconv = ar(512, 2 * (T + 2)).rearrange("p (g t) -> p g t", g=2)
        yconv = ar(1040, 2 * T).rearrange("p (g t) -> p g t", g=2)
        vA = ar(3072, 1024).rearrange("p (t n) -> p t n", t=2)
        qA = ar(4096, 2048).rearrange("p (h t) -> p h t", h=8)
        kA = ar(6144, 2048).rearrange("p (h t) -> p h t", h=8)
        krope = adarow[:, :]
        poolw = ar(7424, 4 * P).rearrange("p (g n) -> p g n", g=4)
        vrows = ar(2048, P)
        brows = arena[0:72, 2048 + P:2048 + 3 * P].rearrange("p (l n) -> p l n", l=2)
        cbuf = ar(2048, 2 * T).rearrange("p (i t) -> p i t", i=2)
        rt = ar(2560, 256)
        logit = ar(2816, 2 * (NG + NE)).rearrange("p (t n) -> p t n", t=2)
        comb = ar(2888, 2 * NE).rearrange("p (t n) -> p t n", t=2)
        combT = arena[0:NE, 2952:2952 + T]
        gates = ada_raw[:, :, :].rearrange("p g (k t) -> p g k t", k=KT)
        xout = xin

        ps = ctx.enter_context(nc.psum_tensor("ps", [P, 8, 512], F32))
        scratch = nc.dram_tensor("comb_rows", [NE, T], F32, kind="Internal").ap()

        landed = [sem(f"landed{s}") for s in range(3)]
        high = [sem(f"high{s}") for s in range(3)]
        split = [sem(f"split{s}") for s in range(3)]
        used = [sem(f"used{s}") for s in range(3)]
        ada_landed = [sem(f"ada_landed{i}") for i in range(2)]
        ada_used = [sem(f"ada_used{i}") for i in range(2)]

        class Tally:

            def __init__(self, eng):
                self.eng, self.n = eng, {}

            def __call__(self, name, k=1):
                self.n[name] = self.n.get(name, 0) + k
                self.eng.wait_ge(sem(name), self.n[name])

        block = ctx.enter_context(nc.Block())

        def columns(t, half):
            return t[:, :].rearrange("p (k n) -> p k n", k=2)[:, :, half * UW // 4:(half + 1) * UW // 4]

        def kxn(w, c0, n):
            return w[:, c0:c0 + n].rearrange("(k p) n -> p k n", p=P)

        def dyn(w, c, n=CH):
            return w[:, bass.ds(c * n, n)].rearrange("(k p) n -> p k n", p=P)

        def unit_source(stage, u):
            if stage == "mix0":
                if u < 8:
                    return kxn(a["w_in_ab"][0], (0, 256, 512, 768, 1536, 1792, 1024, 1280)[u], 256)
                return kxn(a["w_out_ab"][0], (u - 8) * 256, 256)
            if stage == "mix1":
                if u < 12:
                    return kxn(a["w_in_c"][0], (D, 2 * D, 0)[u % 3] + (u // 3) * 256, 256)
                return kxn(a["w_out_c"][0], (u - 12) * 256, 256)
            w = a["w_in_2"][0]
            if u < 4:
                return kxn(w, u * 256, 256)
            if u == KR_UNIT:
                return kxn(w, C_KR - MLA_NOPE, MLA_Q)
            if u < 11:
                return kxn(w, C_QB + (u - 5) * 256, 256)
            if u == 11:
                return kxn(a["w_ukv_2"][0], 0, D)
            if u < 16:
                return kxn(a["w_uq_2"][0], (u - 12) * 2 * MLA_Q, 2 * MLA_Q)
            if u < 24:
                return kxn(w, C_GA + (u - 16) * 256, 256)
            if u < 28:
                return kxn(a[("w_o_mla_2", "w_o_moba_2")[u % 2]][0], ((u - 24) // 2) * 512, 512)
            return kxn(a["w_out_2"][0], (u - 28) * 256, 256)

        @block.sync
        def _(sp):
            nsmall = [0]

            def small(dst, src, name="small_landed"):
                sp.dma_start(dst, src).then_inc(sem(name), 16)

            small(xin, a["x"][0].rearrange("(t p) d -> p t d", p=P), "x_landed")
            small(cst[:, :], const_dram, "const_landed")
            sp.wait_ge(sem("rows_cleared"), 1)

            def rows(name, src, cols=slice(0, P)):
                o, n = ROWS[name]
                small(vrows[o:o + n, cols], src, "rows_landed")

            rows("c", a["c"].rearrange("a (k p) -> (a k) p", p=P))
            rows("norm_g", a["norm_g"].rearrange("l n (k p) -> (l n k) p", p=P))
            rows("conv_w", a["conv_w"].rearrange("l n (k p) -> (l n k) p", p=P))
            rows("pool_scale", a["pool_scale"].rearrange("l (k p) -> (l k) p", p=P))
            rows("attn_norm", a["attn_norm_2"].rearrange("l (k p) -> (l k) p", p=P))
            rows("q_norm", a["q_norm_2"].rearrange("l (k p) -> (l k) p", p=P))
            rows("kv_norm", a["kv_norm_2"].rearrange("l (k p) -> (l k) p", p=P))
            rows("ffn_norm", a["ffn_norm_2"].rearrange("l (k p) -> (l k) p", p=P))
            rows("final_norm", a["final_norm_2"].rearrange("(k p) -> k p", p=P))
            rows("subln", a["subln_g"])
            for half in range(2):
                rows("qk_g", a["qk_norm_g"][0], slice(64 * half, 64 * half + 64))
            o, _ = ROWS["lam"]
            for i, name in enumerate(("lambda_q1", "lambda_k1", "lambda_q2", "lambda_k2")):
                small(vrows[o + i:o + i + 1, 0:64], a[name], "rows_landed")
            small(brows[:, :, :], a["b_ada"].rearrange("l (r p) -> r l p", p=P), "rows_landed")

            def ada_load(layer, v, r, n):
                i = r % 2
                if not isinstance(n, int) or n > 0:
                    sp.wait_ge(ada_used[i], n)
                rows_ = a["w_ada"][layer][r * 256:(r + 1) * 256, :]
                src = rows_[:, bass.ds(v * D, D)] if not isinstance(v, int) else rows_[:, v * D:(v + 1) * D]
                sp.dma_start(ada_raw[:, i, :].rearrange("p (k n) -> p k n", k=2),
                             src.rearrange("(k p) n -> p k n", p=P)).then_inc(ada_landed[i], 16)

            last_down = []

            def load(s, n, src, width=UW):
                if s == 2 and last_down:
                    load_last = last_down.pop()
                    load_last()
                if not isinstance(n, int) or n > 0:
                    sp.wait_ge(split[s], n)
                k = src.shape[1]
                sp.dma_start(raw[s][:, 0:width].rearrange("p (k n) -> p k n", k=k), src).then_inc(landed[s], 16)

            def load_unit(stage, u):
                s = u % 3
                load(s, first[stage][s] + u // 3, unit_source(stage, u), unit_width(stage, u))

            def chunk_loads(stage, wg, wu, wd, ada=None):
                b = first[stage]

                def pair(c):
                    load(0, c + b[0], wg(c))
                    load(1, c + b[1], wu(c))

                def down(c):
                    load(2, c + b[2], wd(c))

                layer, v0_, nv = ada if ada else (0, 0, 0)

                def quarters(half, i):
                    if ada:
                        for r in (2 * half, 2 * half + 1):
                            ada_load(layer, i + v0_, r, i * 2 + 2 * (layer * NMOD + v0_) + r // 2)

                pair(0)
                down(0)
                pair(1)
                quarters(0, 0)
                full = (NCH - 1) // 2 - 1
                looped = min(full, nv - 1) if nv else full
                with sp.Fori(0, looped) as i:
                    for half in range(2):
                        pair(i * 2 + 2 + half)
                        quarters(1 - half, i + half)
                        down(i * 2 + 1 + half)
                for c in range(2 * looped + 1, NCH - 1):
                    pair(c + 1)
                    if c == 2 * nv - 1:
                        quarters(1, nv - 1)
                    down(c)
                last_down.append(lambda: down(NCH - 1))

            ADA_BEHIND = {4: (7, (0, 1)), 6: (7, (2, 3)), 8: (8, (0, 1)), 10: (8, (2, 3))}

            def vector_loads(v, quarters=(0, 1, 2, 3)):
                for r in quarters:
                    ada_load(v // NMOD, v % NMOD, r, 2 * v + r // 2)

            vector_loads(0)
            vector_loads(1)
            small(poolw[:, :, :], a["pool_w"][0].rearrange("g c d -> c g d"))
            small(wrout[:, :, 0:NG], a["w_router_group_2"][0].rearrange("(k p) g -> p k g", p=P))
            for g in range(NG):
                small(wrout[:, :, NG + EG * g:NG + EG * g + EG],
                      a["w_router_expert_2"][0, g].rearrange("(k p) e -> p k e", p=P))
            small(brout[:, 0:NG], a["b_router_group_2"])
            small(brout[:, NG:NG + NE], a["b_router_expert_2"].rearrange("l g e -> l (g e)"))

            def dense(stage, layer, j, ada):
                wg, wu, wd = a["ffn_wg"][layer, j], a["ffn_wu"][layer, j], a["ffn_wd"][layer, j]

                def down(c):
                    w = wd[bass.ds(c * CH, CH), :] if not isinstance(c, int) else wd[c * CH:(c + 1) * CH, :]
                    return w.rearrange("(k p) n -> p k n", p=P)

                chunk_loads(stage, lambda c: dyn(wg, c) if not isinstance(c, int) else kxn(wg, c * CH, CH),
                            lambda c: dyn(wu, c) if not isinstance(c, int) else kxn(wu, c * CH, CH), down, ada)

            dense("ffn0", 0, 0, (0, 2, 5))
            for u in range(12):
                load_unit("mix0", u)
                if u in ADA_BEHIND:
                    vector_loads(*ADA_BEHIND[u])
            dense("ffn1", 0, 1, (1, 0, 5))
            dense("ffn2", 1, 0, (1, 5, 4))
            for u in range(16):
                load_unit("mix1", u)
            dense("ffn3", 1, 1, None)
            for u in range(32):
                load_unit("blk2", u)

            b = first["moe"]

            def expert(e, three=(0, 1, 2)):
                srcs = [a["w_exp_gate_2"], a["w_exp_up_2"], a["w_exp_down_2"]]
                for s in three:
                    w = srcs[s][0, e] if isinstance(e, int) else srcs[s][0, bass.ds(e, 1)].rearrange("e k n -> (e k) n")
                    load(s, e + b[s], w.rearrange("(k p) n -> p k n", p=P))

            def weights_row(e, i):
                if not isinstance(e, int) or e >= 2:
                    sp.wait_ge(sem("scaled"), e - 1)
                row = scratch[bass.ds(e, 1), :] if not isinstance(e, int) else scratch[e:e + 1, :]
                sp.dma_start(cbuf[:, i, :], row.to_broadcast([P, T])).then_inc(sem(f"comb_landed{i}"), 16)

            expert(0)
            expert(1, (0, 1))
            sp.wait_ge(sem("combT_ready"), 1)
            sp.dma_start(scratch, combT[:, :]).then_inc(sem("comb_stored"), 16)
            sp.wait_ge(sem("comb_stored"), 16)
            weights_row(0, 0)
            weights_row(1, 1)
            with sp.Fori(0, (NE - 2) // 2) as i:
                for half in range(2):
                    expert(i * 2 + 2 + half, (0, 1))
                    weights_row(i * 2 + 2 + half, half)
                    expert(i * 2 + 1 + half, (2,))
            expert(NE - 1, (2,))

            for t in range(2):
                sp.wait_ge(sem("out_ready"), t + 1)
                sp.dma_start(out[0, t * P:(t + 1) * P, :], xout[:, t, :]).then_inc(sem("out_stored"), 16)
            sp.wait_ge(sem("out_stored"), 32)
            sp.wait_ge(sem("comb_stored"), 16)

        @block.gpsimd
        def _(pool):
            wait = Tally(pool)
            n = [0]

            def link(ins):
                n[0] += 1
                ins.then_inc(sem("pool_self"), 1)
                pool.wait_ge(sem("pool_self"), n[0])

            pool.memset(zeros[:, :].bitcast(F32), 0.0).then_inc(sem("zeros_ready"), 1)
            wait("const_landed", 16)
            link(pool.memset(pool_in[:, :, 0:16], 0.0))
            link(pool.memset(pool_a[:, :, 0:16], 0.0))
            link(pool.memset(pool_b[:, :, 0:16], 0.0))
            wait("pool_in_ready", 2)
            src, dst = pool_in, pool_a
            for g, w in enumerate((2, 4, 8, 16)):
                h = w // 2
                link(pool.tensor_tensor(dst[:, g:4, 16:PADT], src[:, g:4, 16:PADT], src[:, g:4, 16 - h:PADT - h], ALU.add))
                o, _ = const_at["inv_count"]
                link(pool.tensor_tensor(pool_d[:, g, 0:16], dst[:, g, 16:32], cst[:, o + g * 16:o + g * 16 + 16], ALU.mult))
                link(pool.tensor_scalar(pool_d[:, g, 16:T], dst[:, g, 32:PADT], 1.0 / w, None, ALU.mult))
                ins = pool.tensor_tensor(pool_d[:, g, :], pool_d[:, g, :], pool_in[:, g, 16:PADT], ALU.subtract)
                if g < 3:
                    link(ins)
                else:
                    ins.then_inc(sem("pooled"), 1)
                if g == 0:
                    src, dst = pool_a, pool_b
                else:
                    src, dst = dst, src

        @block.tensor
        def _(pe):
            wait = Tally(pe)
            freed = {}

            def own(bank):
                if bank in freed:
                    pe.wait_ge(*freed.pop(bank))

            counts = {}

            def frees(bank, name):
                counts[name] = counts.get(name, 0) + 1
                freed[bank] = (sem(name), counts[name])

            def three(o, wh, wl, xh, xl, start, stop, shared=False):
                pe.matmul(o, wh, xh, start=start, stop=False, skip_group_check=shared)
                pe.matmul(o, wh, xl, start=False, stop=False, skip_group_check=shared)
                return pe.matmul(o, wl, xh, start=False, stop=stop, skip_group_check=shared)

            turn = [0, 0, 0]

            def slot_ready(s):
                turn[s] += 1
                pe.wait_ge(split[s], turn[s])

            def feature_major(s, outs, nk, m, xh, xl, k0_=0, step=None, ready=None):
                cols = widths[s][turn[s] - 1] // nk
                wh = whi[s][:, 0:nk * cols].rearrange("p (k n) -> p k n", k=nk)
                wl = wlo[s][:, 0:nk * cols].rearrange("p (k n) -> p k n", k=nk)
                for n, o in enumerate(outs):
                    c = slice(n * (step or m), n * (step or m) + m)
                    for j in range(nk):
                        k = j
                        if ready and n == 0:
                            ready(j)
                        mm = three(o, wh[:, k, c], wl[:, k, c], xh[:, k0_ + k, :], xl[:, k0_ + k, :], j == 0, j == nk - 1)
                mm.then_inc(used[s], 1)

            def first_two(between=None):
                def product(s, k, m):
                    c = slice(k * 2 * P + m * P, k * 2 * P + (m + 1) * P)
                    return three(ps[:, s, m * T:(m + 1) * T], whi[s][:, c], wlo[s][:, c], hhi[:, k, :], hlo[:, k, :],
                                 k == 0, k == KT - 1)

                for k in range(KT):
                    wait("h_ready")
                    for s in range(2):
                        product(s, k, 0)
                if between:
                    between()
                for s in range(2):
                    for k in range(KT):
                        mm = product(s, k, 1)
                    mm.then_inc(used[s], 1)

            def first_units(freed_by):
                for s in range(2):
                    slot_ready(s)
                    own(s)
                first_two()
                for s in range(2):
                    frees(s, freed_by[s])

            def bank_pair(b, m=P):
                return [ps[0:m, b, 0:T], ps[0:m, b, T:2 * T]]

            def one_tile(s, n, o, xh=hhi, xl=hlo):
                for k in range(KT):
                    c = slice(k * 2 * P + n * P, k * 2 * P + (n + 1) * P)
                    mm = three(o, whi[s][:, c], wlo[s][:, c], xh[:, k, :], xl[:, k, :], k == 0, k == KT - 1)
                return mm

            def linear(stage, u, freed_by=None, xh=hhi, xl=hlo, ready=None, b=None):
                s, b = u % 3, u % 2 if b is None else b
                slot_ready(s)
                own(b)
                feature_major(s, bank_pair(b), KT, P, xh, xl, ready=ready)
                if freed_by:
                    frees(b, freed_by)

            def token_major(stage, u, freed_by):
                s, b = u % 3, u % 2
                slot_ready(s)
                own(b)
                wh = whi[s][:, :].rearrange("p (k n) -> p k n", k=KT)
                wl = wlo[s][:, :].rearrange("p (k n) -> p k n", k=KT)
                for t in range(2):
                    tt = slice(t * P, t * P + P)
                    for k in range(KT):
                        o = ps[:, b, t * T:(t + 1) * T]
                        pe.matmul(o, hhi[:, k, tt], wh[:, k, :], start=(k == 0), stop=False)
                        pe.matmul(o, hhi[:, k, tt], wl[:, k, :], start=False, stop=False)
                        mm = pe.matmul(o, hlo[:, k, tt], wh[:, k, :], start=False, stop=(k == KT - 1))
                mm.then_inc(used[s], 1)
                frees(b, freed_by)

            wait("x_landed", 16)
            wait("const_landed", 16)
            for k in range(KT):
                for t in range(2):
                    mm = pe.transpose(ps[:, 2 + k // 2, (k % 2) * T + t * P:(k % 2) * T + (t + 1) * P],
                                      xin[:, t, k * P:(k + 1) * P], ident)
                if k % 2:
                    mm.then_inc(sem("xT_ready"), 1)
            wait("rows_landed", 16 * 17)
            pe.transpose(ps[:, 7, 0:NROWS], vrows[0:NROWS, :], ident[0:NROWS, 0:NROWS])
            for l in range(2):
                mm = pe.transpose(ps[:, 7, P + 72 * l:P + 72 * l + 72], brows[:, l, :], ident[0:72, 0:72])
            mm.then_inc(sem("vcols_ready"), 1)
            wait("lam_prod")
            pe.matmul(ps[:, 7, 400:402], ones, lam[:, 0:2], start=True, stop=True).then_inc(sem("lam_sum"), 1)

            def ada_quarter(r, n, v_before=None):
                i = r % 2
                pe.wait_ge(ada_landed[i], (n + 1) * 16)
                if r == 0:
                    if not isinstance(v_before, int) or v_before > 0:
                        pe.wait_ge(sem("mod_ready"), v_before)
                for kk in range(2):
                    k = 2 * r + kk
                    for j in range(4):
                        mm = pe.matmul(ps[32 * j:32 * j + 32, 6, 0:T], cact[:, k:k + 1].to_broadcast([P, 32]),
                                       ada_raw[:, i, kk * D + j * T:kk * D + (j + 1) * T],
                                       start=(k == 0), stop=(k == KT - 1))
                mm.then_inc(ada_used[i], 1)

            def ada_turn(v):
                pe.wait_ge(sem("adarow_ready"), v + 1)
                for b in range(2):
                    mm = pe.transpose(ps[:, 6, T + b * P:T + (b + 1) * P], adarow[:, b * P:(b + 1) * P], ident)
                mm.then_inc(sem("adacol_ready"), 1)
                if isinstance(v, int):
                    freed[6] = (sem("mod_ready"), v + 1)

            def ada_half(v, half):
                for r in (2 * half, 2 * half + 1):
                    ada_quarter(r, 2 * v + half, v)

            def ada_vector(v):
                ada_half(v, 0)
                ada_half(v, 1)

            wait("cact_ready")
            ada_vector(0)
            ada_turn(0)
            ada_vector(1)
            ada_turn(1)

            norms = [0]

            def norm_sums():
                norms[0] += 1
                counts["x_ready"] = 4 * norms[0]
                own(7)
                for k in range(KT):
                    if k % 2 == 0:
                        wait("sq_ready")
                    mm = pe.matmul(ps[:, 7, 0:T], ones, hf[:, k, :], start=(k == 0), stop=(k == KT - 1))
                mm.then_inc(sem("stat_ready"), 1)
                frees(7, "stat_read")

            def chunked(stage, layer_v=None, nv=5, count=NCH, between=None, then=None):
                b0, ch = first[stage], chunk0[stage]

                def gate(c, e=0):
                    pe.wait_ge(split[0], c + b0[0] + 1)
                    if not (isinstance(c, int) and c + ch == 0):
                        pe.wait_ge(sem("silu_done"), c + ch)
                    halves(0, ps[:, 0, :])

                def up(c):
                    pe.wait_ge(split[1], c + b0[1] + 1)
                    if not (isinstance(c, int) and c + ch == 0):
                        pe.wait_ge(sem("hid_done"), c + ch)
                    halves(1, ps[:, 1, :])

                def halves(s, o):
                    wh = whi[s][:, :].rearrange("p (k n) -> p k n", k=KT)
                    wl = wlo[s][:, :].rearrange("p (k n) -> p k n", k=KT)
                    for m in range(2):
                        for k in range(KT):
                            mm = three(o[:, m * T:(m + 1) * T], wh[:, k, m * P:(m + 1) * P], wl[:, k, m * P:(m + 1) * P],
                                       hhi[:, k, :], hlo[:, k, :], k == 0, k == KT - 1)
                    mm.then_inc(used[s], 1)

                def down(c, parity, last=False):
                    if last:
                        wait("last_split")
                    else:
                        pe.wait_ge(split[2], c + b0[2] + 1)
                    pe.wait_ge(sem("hid_split"), c + ch + 1)
                    wh = whi[2][:, :].rearrange("p (k n) -> p k n", k=2)
                    wl = wlo[2][:, :].rearrange("p (k n) -> p k n", k=2)
                    for m in range(KT):
                        if last and m == 4:
                            pe.wait_ge(split[2], c + b0[2] + 1)
                        o = ps[:, 2 + m // 2, (m % 2) * T:(m % 2 + 1) * T]
                        for k in range(2):
                            mm = three(o, wh[:, k, m * P:(m + 1) * P], wl[:, k, m * P:(m + 1) * P],
                                       hidhi[parity][:, k, :], hidlo[parity][:, k, :], False, last and k == 1, shared=True)
                        if last and m in (1, 3, 5):
                            mm.then_inc(sem("out_pair"), 1)
                        if m == 3 and not last:
                            mm.then_inc(sem("down_half"), 1)
                    mm.then_inc(used[2], 1)

                for o in range(16):
                    pe.matmul(ps[:, 2 + o // 4, (o % 4) * P:(o % 4 + 1) * P], zeros[:, :], zeros[:, :], start=True, stop=True)
                pe.wait_ge(split[0], b0[0] + 1)
                if ch:
                    pe.wait_ge(sem("silu_done"), ch)
                pe.wait_ge(split[1], b0[1] + 1)
                if ch:
                    pe.wait_ge(sem("hid_done"), ch)
                first_two(between)
                if then:
                    then()

                def pair(i, v=None):
                    for half in range(2):
                        c = i * 2 + half
                        gate(c + 1)
                        up(c + 1)
                        if v is not None:
                            for r in (2 * half, 2 * half + 1):
                                ada_quarter(r, i * 2 + 2 * layer_v + r // 2, v)
                        down(c, half)
                    if v is not None:
                        ada_turn(v)

                pairs = (count - 1) // 2
                if layer_v is None:
                    nv = 0
                else:
                    with pe.Fori(0, nv) as i:
                        pair(i, i + layer_v)
                if nv < pairs:
                    with pe.Fori(nv, pairs) as i:
                        pair(i)
                c = (count - 1) // 2 * 2
                if c < count - 1:
                    gate(c + 1)
                    up(c + 1)
                    down(c, c % 2)
                    c += 1
                down(c, c % 2, last=True)
                for s in range(3):
                    turn[s] = b0[s] + count

            norm_sums()
            wait("zeros_ready")
            chunked("ffn0", 2)

            def square_sums(weights, i, b, n=2 * T, start=True, stop=True, o=0):
                own(b)
                return pe.matmul(ps[:, b, o:o + n], weights, sq[:, i, 0:n], start=start, stop=stop)

            def qk_sums(i):
                wait("sq_done")
                square_sums(c_("halves"), i % 2, 7).then_inc(sem("stat_ready"), 1)
                frees(7, "stat_read")

            def scores(i, q, k):
                b = 2 + i % 4
                own(b)
                pe.matmul(ps[:, b, 0:P], q[:, 0:P], k[:, 0:P], start=True, stop=True)
                pe.matmul(ps[:, b, P:3 * P], q[:, P:2 * P], k[:, 0:2 * P], start=True, stop=True).then_inc(sem("scores_ready"), 1)
                frees(b, "exp_done")

            def probs_turn(e):
                own(7)
                wait("probs_ready")
                for j in range(3):
                    mm = pe.transpose(ps[:, 7, j * P:(j + 1) * P], exps[:, e, j * P:(j + 1) * P], ident)
                mm.then_inc(sem("turned"), 1)
                frees(7, "probsT_ready")

            def values(i, o, v):
                wait("probsT_ready")
                p = probsT[:, i % 2, :]
                pe.matmul(o, v[0], p[:, 0:T], start=True, stop=False)
                return pe.matmul(o[:, P:T], v[1], p[:, T:3 * P], start=False, stop=True)

            def diff_scores(h):
                for half in range(2):
                    rows = slice(64 * half, 64 * half + 64)
                    scores(2 * h + half, q0[rows, h, :], k0[rows, h, :])

            norm_sums()
            first_units(("sq_done", "sq_done"))
            for u in range(8):
                if 1 < u < 6:
                    linear("mix0", u, "sq_done" if u < 4 else "pool_in_ready")
                elif u < 2:
                    pass
                else:
                    token_major("mix0", u, "v_ready")
                if u in (2, 3):
                    ada_half(7, u - 2)
                if u == 4:
                    ada_turn(7)
                if u in (5, 7):
                    ada_half(8, (u - 5) // 2)
                if 1 <= u <= 4:
                    qk_sums(u - 1)
                if u == 6:
                    wait("qk_ready", 4)
                    diff_scores(0)

            wait("v_ready", 2)
            for h in range(5):
                if h < 3:
                    diff_scores(h + 1)
                if h == 0:
                    ada_turn(8)
                if h < 4:
                    probs_turn((2 * h) % 4)
                if h == 4:
                    own(2)
                    wait("o_read")
                    square_sums(ones, 0, 2).then_inc(sem("stat_ready"), 1)
                    frees(2, "stat_read")
                if h:
                    g = h - 1
                    if g % 2 == 0:
                        own(6)
                    mm = values(g, ps[:, 6, (g % 2) * T:(g % 2 + 1) * T], [v0[:, t, g * P:(g + 1) * P] for t in range(2)])
                    if g % 2:
                        mm.then_inc(sem("o_ready"), 1)
                        frees(6, "o_read")
                if h == 3:
                    wait("pooled")
                    wait("small_landed", 16 * 8)
                    for j in range(2):
                        own(j)
                        for g in range(2):
                            mm = pe.matmul(ps[:, j, g * T:(g + 1) * T], poolw[:, 2 * j + g, :], pool_d[:, 2 * j + g, :], start=True, stop=True)
                        mm.then_inc(sem("pool_out"), 1)
                        frees(j, "pool_read")

            def open_bank(b):
                own(b)
                for o in range(4):
                    pe.matmul(ps[:, b, o * P:(o + 1) * P], zeros[:, :], zeros[:, :], start=True, stop=True)

            def output_part(s, b, k, xh, xl, last=False):
                for m in range(2):
                    c = slice(k * 2 * P + m * P, k * 2 * P + (m + 1) * P)
                    mm = three(ps[:, b, m * T:(m + 1) * T], whi[s][:, c], wlo[s][:, c], xh[:, k, :], xl[:, k, :],
                               False, last, shared=True)
                if last:
                    mm.then_inc(used[s], 1)

            for s, b in ((2, 0), (0, 1)):
                open_bank(b)
                slot_ready(s)
                for k in range(4, 8):
                    if b == 0 and k % 2 == 0:
                        wait("mix_split")
                    output_part(s, b, k, mhi, mlo)
                if b == 0:
                    own(3)
                    wait("o_read")
                    square_sums(ones, 1, 3).then_inc(sem("stat_ready"), 1)
                    frees(3, "stat_read")
            for s, b in ((2, 0), (0, 1)):
                for k in range(4):
                    if b == 0 and k % 2 == 0:
                        wait("mix_split")
                    output_part(s, b, k, mhi, mlo, last=(k == 3))
                frees(b, "x_ready")
            for u in (10, 11):
                linear("mix0", u, "x_ready", mhi, mlo)

            def outputs(stage, u0, ready=None):
                for j in range(4):
                    linear(stage, u0 + j, "x_ready", mhi, mlo, ready if j == 0 else None)

            norm_sums()
            chunked("ffn1", 9)
            norm_sums()
            chunked("ffn2", 14, 4)

            norm_sums()
            first_units(("evacuated", "v_done"))
            for u in range(2, 12):
                linear("mix1", u, ("evacuated", "v_done", "y_done")[u % 3])
            outputs("mix1", 12, lambda k: wait("mix_split") if k % 2 == 0 else None)
            norm_sums()
            chunked("ffn3")

            norm_sums()

            def rope(r):
                b = (7, 6)[r % 2]
                own(b)
                wait("rope_in")
                if r == 0:
                    mm = pe.matmul(ps[64:96, b, 0:T], c_("swap_mla", slice(64, 96)), krope[64:96, :], start=True, stop=True)
                elif r < 5:
                    src = q0[:, 2 * (r - 1):2 * r, :] if r < 3 else k0[:, 2 * (r - 3):2 * (r - 2), :]
                    mm = pe.matmul(ps[:, b, :], c_("swap_moba"), src, start=True, stop=True)
                else:
                    mm = pe.matmul(ps[64:96, b, :], c_("swap_mla", slice(64, 96)), qA[64:96, 2 * (r - 5):2 * (r - 4), :],
                                   start=True, stop=True)
                mm.then_inc(sem("rope_swapped"), 1)
                frees(b, "rope_read")

            def latent_sums(j):
                wait("sq_done")
                b = 7 if j < 3 else 6
                if j in (0, 3):
                    own(b)
                for n in range(2):
                    mm = pe.matmul(ps[:, b, 0:T], ones, sq[:, j % 2, n * T:(n + 1) * T],
                                   start=(j in (0, 3) and n == 0), stop=(j >= 2 and n == 1))
                mm.then_inc(sem("sums_done"), 1)
                if j >= 2:
                    frees(b, "stat_read")

            first_units(("sq_done", "sq_done"))
            for u in range(4):
                if u > 1:
                    linear("blk2", u, "sq_done")
                if u:
                    latent_sums(u - 1)
            slot_ready(1)
            own(0)
            feature_major(1, [ps[0:MLA_Q, 0, 0:T]], KT, MLA_Q, hhi, hlo)
            frees(0, "rope_in")
            latent_sums(3)
            linear("blk2", 5, "rope_in")
            rope(0)
            for u in range(6, 9):
                linear("blk2", u, "rope_in")
                rope(u - 5)
            token_major("blk2", 9, "v_ready")
            rope(4)
            token_major("blk2", 10, "v_ready")
            slot_ready(2)
            wait("latent_split", 2)
            wh = whi[2][:, :].rearrange("p (k h n) -> p k h n", k=2, h=MLA_H)
            wl = wlo[2][:, :].rearrange("p (k h n) -> p k h n", k=2, h=MLA_H)
            for h in range(MLA_H):
                for k in range(2):
                    three(ps[:, 2 + h // 2, (h % 2) * T:(h % 2 + 1) * T], wh[:, k, h, :], wl[:, k, h, :],
                          mhi[:, 6 + k, :], mlo[:, 6 + k, :], k == 0, k == 1)
            for t in range(2):
                own(t)
                tt = slice(t * P, t * P + P)
                for k in range(2):
                    pe.matmul(ps[:, t, :], mhi[:, 6 + k, tt], wh[:, k, :, 64:], start=(k == 0), stop=False)
                    pe.matmul(ps[:, t, :], mhi[:, 6 + k, tt], wl[:, k, :, 64:], start=False, stop=False)
                    mm = pe.matmul(ps[:, t, :], mlo[:, 6 + k, tt], wh[:, k, :, 64:], start=False, stop=(k == 1))
                frees(t, "ukv_v_read")
            mm.then_inc(used[2], 1)
            for u in UQ_UNITS:
                s, b = u % 3, u % 2
                slot_ready(s)
                own(b)
                feature_major(s, bank_pair(b, MLA_Q), QL // P, MLA_Q, mhi, mlo)
                frees(b, "rope_in")
                if u > UQ_UNITS[0]:
                    rope(5 + u - UQ_UNITS[0] - 1)
            rope(8)
            wait("ukv_k_read", 1)
            wait("v_ready", 2)
            wait("roped", 5)

            def head(i):
                if i < MOBA_H:
                    r = slice(64 * (i % 2), 64 * (i % 2) + 64)
                    scores(i, q0[r, i // 2, :], k0[r, i // 2, :])
                else:
                    if i == MOBA_H:
                        wait("roped", 4)
                    scores(i, qA[0:MLA_Q, i - 8, :], kA[0:MLA_Q, i - 8, :])

            head(0)
            head(1)
            for i in range(17):
                if i + 2 < 16:
                    head(i + 2)
                if i < 16:
                    u, n = 16 + i // 2, i % 2
                    if n == 0:
                        slot_ready(u % 3)
                        own(u % 2)
                    mm = one_tile(u % 3, n, bank_pair(u % 2)[n])
                    if n == 1:
                        mm.then_inc(used[u % 3], 1)
                        frees(u % 2, "evacuated")
                    probs_turn(i % 4)
                if i:
                    h = i - 1
                    if h % 2 == 0:
                        own(6)
                    r = slice(64 * (h % 2), 64 * (h % 2) + 64)
                    v, c = (v0, h) if h < MOBA_H else (vA, h - 8)
                    mm = values(h, ps[r, 6, 0:T], [v[:, t, c * 64:(c + 1) * 64] for t in range(2)])
                    mm.then_inc(sem("o_ready"), 1)
                    if h % 2:
                        frees(6, "o_split")
            wait("o_split", 8)
            for j in range(2):
                for which in range(2):
                    u = 24 + 2 * j + which
                    s = u % 3
                    b = (2, 4, 0, 6)[2 * j + which]
                    slot_ready(s)
                    own(b)
                    own(b + 1)
                    feature_major(s, bank_pair(b) + bank_pair(b + 1), 4, P, mhi, mlo, k0_=4 * which)
                if j == 0:
                    for b in (2, 3):
                        freed[b] = (sem("mixed"), 1)
            for u in (28, 29):
                open_bank(2 + u % 2)
                slot_ready(u % 3)
            for half in range(2):
                wait("mixed_split")
                for u in (28, 29):
                    for k in range(4 * half, 4 * half + 4):
                        output_part(u % 3, 2 + u % 2, k, hhi, hlo, last=(k == KT - 1))
                    if half:
                        frees(2 + u % 2, "x_ready")
            for u in (30, 31):
                linear("blk2", u, "x_ready", b=2 + u % 2)

            norm_sums()

            def router_logits():
                own(7)
                for t in range(2):
                    o = ps[:, 7, 64 * t:64 * t + NG + NE]
                    pe.matmul(o, ones[0:1, :], brout[:, :], start=True, stop=False)
                    for k in range(KT):
                        mm = pe.matmul(o, hf[:, k, t * P:(t + 1) * P], wrout[:, k, :], start=False, stop=(k == KT - 1))
                mm.then_inc(sem("logits_ready"), 1)

            def weights_turned():
                wait("comb_ready")
                for t in range(2):
                    mm = pe.transpose(ps[0:NE, 6, t * P:(t + 1) * P], comb[:, t, :], ident)
                mm.then_inc(sem("comb_turned"), 1)

            chunked("moe", count=NE, between=router_logits, then=weights_turned)

            norm_sums()
            for k in range(KT):
                pe.wait_ge(sem("t_ready"), 8 * KT + k + 1)
                for t in range(2):
                    b = 2 * t + k // 4
                    mm = pe.transpose(ps[:, b, (k % 4) * P:(k % 4 + 1) * P], hf[:, k, t * P:(t + 1) * P], ident)
            mm.then_inc(sem("out_turned"), 1)

        @block.scalar
        def _(act):
            wait = Tally(act)
            turn = [0, 0, 0]

            def split_high(s, n, width=UW, after_use=True):
                act.wait_ge(landed[s], (n + 1) * 16)
                if not isinstance(n, int) or n > 0:
                    act.wait_ge(used[s], n)
                act.activation(whi[s][:, 0:width], raw[s][:, 0:width], ACT.Copy).then_inc(high[s], 1)

            def refill(s):
                n = turn[s]
                if n < len(widths[s]):
                    split_high(s, n, widths[s][n])
                    turn[s] += 1

            def copy(o, i, scale=1.0):
                return act.activation(o, i, ACT.Copy, scale=scale)

            def norm(slots=()):
                if stats[0]:
                    act.wait_ge(sem("table_in"), stats[0])
                stats[0] += 1
                act.activation(lam[:, 6:7], eps, ACT.Sqrt).then_inc(sem("table_in"), 1)
                for pr in range(4):
                    if pr < len(slots):
                        refill(slots[pr])
                    wait("x_ready")
                    act.activation(hf[:, 2 * pr:2 * pr + 2, :], xT[:, 2 * pr:2 * pr + 2, :], ACT.Square).then_inc(sem("sq_ready"), 1)
                roots(D, T)

            def roots(width, n, b=7, o=0):
                wait("stat_ready")
                act.activation(root[:, o:o + n], ps[:, b, 0:n], ACT.Sqrt, bias=eps[:, 0:1], scale=1.0 / width).then_inc(sem("stat_read"), 1)

            def norm_high(shift):
                for k in range(KT):
                    wait("t_ready")
                    if shift is None:
                        copy(hhi[:, k, :], hf[:, k, :]).then_inc(sem("h_high"), 1)
                    else:
                        act.activation(hhi[:, k, :], hf[:, k, :], ACT.Identity, bias=shift[:, k:k + 1]).then_inc(sem("h_high"), 1)

            eps = lam[:, 7:8]
            stats = [0]
            wait("vcols_done")
            act.activation(cact[:, :], col("c", 0, KT), ACT.Silu).then_inc(sem("cact_ready"), 1)
            wait("lam_sum")
            act.activation(lam[:, 2:4], ps[:, 7, 400:402], ACT.Exp).then_inc(sem("lam_exp"), 1)
            for s in range(3):
                refill(s)
            norm()
            norm_high(mod(0, 0))

            def chunked(stage, count=NCH):
                b0, ch = first[stage], chunk0[stage]

                def gate(c):
                    act.wait_ge(used[0], c + b0[0] + 1)
                    if not (isinstance(c, int) and c + ch == 0):
                        act.wait_ge(sem("hid_done"), c + ch)
                    act.activation(silu[:, :], ps[:, 0, :], ACT.Silu).then_inc(sem("silu_done"), 1)

                def high_hidden(c, parity):
                    if stage == "moe":
                        act.wait_ge(sem("scaled"), c + 1)
                    else:
                        act.wait_ge(sem("hid_done"), c + ch + 1)
                    if not (isinstance(c, int) and c < 2):
                        act.wait_ge(used[2], c + b0[2] - 1)
                    act.activation(hidhi[parity][:, :, :], hid[:, :].rearrange("p (k t) -> p k t", k=2), ACT.Copy).then_inc(sem("hid_high"), 1)

                def last_halves():
                    n = b0[2] + count - 1
                    act.wait_ge(landed[2], (n + 1) * 16)
                    act.wait_ge(sem("down_half"), ch + count - 1 - CHUNKED.index(stage))
                    act.activation(columns(whi[2], 0), columns(raw[2], 0), ACT.Copy).then_inc(sem("last_high"), 1)
                    act.wait_ge(used[2], n)
                    act.activation(columns(whi[2], 1), columns(raw[2], 1), ACT.Copy).then_inc(high[2], 1)

                def chunk(c, parity, down=True, more=True, last=False):
                    if down:
                        gate(c)
                    if more:
                        split_high(0, c + b0[0] + 1)
                    if not down:
                        gate(c)
                    high_hidden(c, parity)
                    if more:
                        split_high(1, c + b0[1] + 1)
                    if last:
                        last_halves()
                    elif down:
                        split_high(2, c + b0[2])

                chunk(0, 0, down=False)
                with act.Fori(0, (count - 2) // 2) as i:
                    for half in range(2):
                        chunk(i * 2 + 1 + half, (1 + half) % 2)
                for c in range((count - 2) // 2 * 2 + 1, count):
                    chunk(c, c % 2, more=stage != "moe" or c < count - 1, last=(c == count - 1))
                for s in range(3):
                    turn[s] = b0[s] + count + (s < 2)

            chunked("ffn0")
            norm()
            norm_high(mod(0, 3))
            refill(2)

            def pair(b, rows=P):
                return ps[0:rows, b, :].rearrange("p (n t) -> p n t", n=2)

            def exps_of(i):
                wait("negmax_ready")
                e, b = i % 4, 2 + i % 4
                act.activation(exps[:, e, 0:P], ps[:, b, 0:P], ACT.Exp, bias=negmax[:, e, 0:1], accum_out=zsum[:, e, 0:1])
                act.activation(exps[:, e, P:3 * P], ps[:, b, P:3 * P], ACT.Exp, bias=negmax[:, e, 1:2],
                               accum_out=zsum[:, e, 1:2]).then_inc(sem("exp_done"), 1)

            def probsT_of(i):
                wait("turned")
                copy(probsT[:, i % 2, :], ps[:, 7, 0:3 * P]).then_inc(sem("probsT_ready"), 1)

            def o_out(j):
                wait("o_ready")
                copy(hf[:, 2 * j:2 * j + 2, :], pair(6)).then_inc(sem("o_copied"), 1)
                act.activation(sq[:, j, :], ps[:, 6, :], ACT.Square).then_inc(sem("o_read"), 1)

            for u in range(8):
                s, b = u % 3, u % 2
                if u == 7:
                    exps_of(0)
                    exps_of(1)
                act.wait_ge(used[s], first["mix0"][s] + u // 3 + 1)
                if u < 4:
                    dst = (q0 if u < 2 else k0)[:, 2 * (u % 2):2 * (u % 2) + 2, :]
                    copy(dst, pair(b)).then_inc(sem("qk_copied"), 1)
                    act.activation(sq[:, u % 2, :], ps[:, b, :], ACT.Square).then_inc(sem("sq_done"), 1)
                elif u < 6:
                    copy(pool_in[:, 2 * (u - 4):2 * (u - 4) + 2, 16:PADT], pair(b)).then_inc(sem("pool_in_ready"), 1)
                else:
                    copy(v0[:, :, 256 * (u - 6):256 * (u - 5)], pair(b)).then_inc(sem("v_ready"), 1)
                refill(s)
                if 1 <= u <= 4:
                    if u > 1:
                        wait("qk_ready")
                    roots(64, 2 * T)

            for h in range(4):
                if h < 3:
                    exps_of(2 * h + 2)
                    exps_of(2 * h + 3)
                probsT_of(h)
                if h == 2:
                    o_out(0)
            for j in range(2):
                wait("pool_out")
                for g in range(2):
                    k = 2 * j + g
                    act.activation(hf[:, 4 + k, :], ps[:, j, g * T:(g + 1) * T], ACT.Copy,
                                   scale=col("pool_scale", k)).then_inc(sem("pool_read_half" if g == 0 else "pool_read"), 1)
            for j in range(2):
                act.wait_ge(sem("pool_read_half"), j + 1)
                act.wait_ge(sem("pool_read"), j + 1)
                copy(mhi[:, 4 + 2 * j:6 + 2 * j, :], hf[:, 4 + 2 * j:6 + 2 * j, :]).then_inc(sem("mix_high"), 1)
            o_out(1)
            roots(P, 2 * T, b=2)
            wait("o_normed")
            copy(mhi[:, 0:2, :], hf[:, 0:2, :]).then_inc(sem("mix_high"), 1)
            roots(P, 2 * T, b=3)
            wait("o_normed")
            copy(mhi[:, 2:4, :], hf[:, 2:4, :]).then_inc(sem("mix_high"), 1)
            norm((2, 0, 1))
            norm_high(mod(0, 6))
            refill(2)
            chunked("ffn1")
            norm()
            norm_high(mod(1, 0))
            refill(2)
            chunked("ffn2")

            norm()
            norm_high(mod(1, 3))
            refill(2)
            for u in range(12):
                s, b = u % 3, u % 2
                act.wait_ge(used[s], first["mix1"][s] + u // 3 + 1)
                if u % 3 == 0:
                    if u:
                        wait("v_done")
                    copy(cgate, ps[:, b, :]).then_inc(sem("evacuated"), 1)
                refill(s)
                if u % 3 == 2:
                    j = u // 3
                    wait("y_done")
                    copy(mhi[:, 2 * j:2 * j + 2, :], hf[:, 2 * j:2 * j + 2, :]).then_inc(sem("mix_high"), 1)
            norm((0, 1, 2))
            refill(0)
            norm_high(mod(1, 6))
            chunked("ffn3")

            norm()
            norm_high(None)
            refill(2)

            def latent_high(j):
                wait("latent_normed")
                sl = slice(0, 6) if j == 0 else slice(6, 8)
                copy(mhi[:, sl, :], hf[:, sl, :]).then_inc(sem("latent_high"), 1)

            for u in range(11):
                s, b = u % 3, u % 2
                act.wait_ge(used[s], first["blk2"][s] + u // 3 + 1)
                if u < 4:
                    if u >= 2:
                        wait("sums_done")
                    copy(hf[:, 2 * u:2 * u + 2, :], pair(b)).then_inc(sem("latent_copied"), 1)
                    act.activation(sq[:, u % 2, :], ps[:, b, :], ACT.Square).then_inc(sem("sq_done"), 1)
                elif u == KR_UNIT:
                    copy(krope[64:96, :], ps[64:96, b, 0:T]).then_inc(sem("rope_in"), 1)
                elif u < 9:
                    j = u - 5
                    dst = (q0 if j < 2 else k0)[:, 2 * (j % 2):2 * (j % 2) + 2, :]
                    copy(dst, pair(b), MOBA_HD ** -0.5 if j < 2 else 1.0).then_inc(sem("rope_in"), 1)
                else:
                    copy(v0[:, :, 256 * (u - 9):256 * (u - 8)], pair(b)).then_inc(sem("v_ready"), 1)
                refill(s)
                if u == 4:
                    wait("sums_done")
                    act.activation(root[:, 0:T], ps[:, 7, 0:T], ACT.Sqrt, bias=eps, scale=1.0 / QL).then_inc(sem("stat_read"), 1)
                if u == 5:
                    wait("sums_done")
                    act.activation(root[:, T:2 * T], ps[:, 6, 0:T], ACT.Sqrt, bias=eps, scale=1.0 / KVL).then_inc(sem("stat_read"), 1)
                if u == 7:
                    latent_high(0)
                    latent_high(1)
            act.wait_ge(used[2], first["blk2"][2] + 11 // 3 + 1)
            for j in range(4):
                ins = copy(kA[0:64, 2 * j:2 * j + 2, :], pair(2 + j, 64))
            ins.then_inc(sem("ukv_k_read"), 1)
            for t in range(2):
                copy(vA[:, t, :], ps[:, t, :]).then_inc(sem("ukv_v_read"), 1)
            refill(2)
            for u in UQ_UNITS:
                s, b = u % 3, u % 2
                act.wait_ge(used[s], first["blk2"][s] + u // 3 + 1)
                i = u - UQ_UNITS[0]
                copy(qA[0:MLA_Q, 2 * i:2 * i + 2, :], pair(b, MLA_Q), MLA_Q ** -0.5).then_inc(sem("rope_in"), 1)
                refill(s)

            exps_of(0)
            exps_of(1)
            for i in range(17):
                if i + 2 < 16:
                    exps_of(i + 2)
                if i % 2:
                    g = i // 2
                    u = 16 + g
                    act.wait_ge(used[u % 3], first["blk2"][u % 3] + u // 3 + 1)
                    copy(gates[:, g // 4, 2 * (g % 4):2 * (g % 4) + 2, :], pair(u % 2)).then_inc(sem("evacuated"), 1)
                    refill(u % 3)
                if i < 16:
                    probsT_of(i)
                if i and i % 2 == 0:
                    j = i // 2 - 1
                    wait("o_ready", 2)
                    tile_ = 4 + j if j < 4 else j - 4
                    copy(mhi[:, tile_, :], ps[:, 6, 0:T]).then_inc(sem("o_high"), 1)
            for j in range(2):
                act.wait_ge(sem("evacuated"), 4 + 8)
                g = gates[:, :, 4 * j:4 * j + 4, :]
                act.activation(g, g, ACT.Sigmoid).then_inc(sem("gates_ready"), 1)
            for j in range(2):
                for which in range(2 - j):
                    refill((24 + 2 * j + which) % 3)
                wait("mixed")
                copy(hhi[:, 4 * j:4 * j + 4, :], hf[:, 4 * j:4 * j + 4, :]).then_inc(sem("mixed_high"), 1)
            refill(27 % 3)
            norm((1, 2, 0))
            refill(1)
            norm_high(None)
            wait("router_max")
            act.activation(rt[:, 64:72], rt[:, 56:64], ACT.Exp).then_inc(sem("router_exp"), 1)
            wait("router_two")
            act.activation(rt[:, 130:132], rt[:, 128:130], ACT.Exp).then_inc(sem("router_exp"), 1)
            wait("comb_turned")
            copy(combT[:, :], ps[0:NE, 6, 0:T]).then_inc(sem("combT_ready"), 1)
            chunked("moe", NE)
            norm()
            wait("out_turned")
            for t in range(2):
                ins = copy(xout[:, t, :].rearrange("p (b n) -> p b n", b=2), ps[:, 2 * t:2 * t + 2, :]).then_inc(sem("out_ready"), 1)

        @block.vector
        def _(dve):
            wait = Tally(dve)
            turn = [0, 0, 0]
            n_self = [0]

            def link(ins):
                n_self[0] += 1
                ins.then_inc(sem("dve_self"), 1)
                dve.wait_ge(sem("dve_self"), n_self[0])

            def split_low(s, n, width=UW):
                dve.wait_ge(high[s], n + 1)
                dve.tensor_tensor(wlo[s][:, 0:width], raw[s][:, 0:width], whi[s][:, 0:width].bitcast(F32),
                                  ALU.subtract).then_inc(split[s], 1)

            def refill(s):
                n = turn[s]
                if n < len(widths[s]):
                    split_low(s, n, widths[s][n])
                    turn[s] += 1

            def stt(o, i0, s, i1, op0=ALU.mult, op1=ALU.add):
                return dve.scalar_tensor_tensor(out=o, in0=i0, scalar=s, in1=i1, op0=op0, op1=op1)

            link(dve.memset(lam[:, :], EPS))
            dve.memset(vrows[:, :], 0.0).then_inc(sem("rows_cleared"), 1)
            for pr in range(4):
                wait("xT_ready")
                dve.tensor_copy(xT[:, 2 * pr:2 * pr + 2, :], ps[:, 2 + pr, :].rearrange("p (n t) -> p n t", n=2)).then_inc(sem("x_ready"), 1)
            wait("vcols_ready")
            link(dve.tensor_copy(bada[:, :], ps[:, 7, P:P + 144]))
            link(dve.tensor_copy(vcols[:, :], ps[:, 7, 0:NROWS]))
            link(dve.tensor_scalar(col("subln"), col("subln"), 1.0 - LAM_INIT, None, ALU.mult))
            dve.tensor_scalar(col("lam", 0), col("lam", 0), 1.0, None, ALU.mult).then_inc(sem("vcols_done"), 1)
            dve.wait_ge(sem("vcols_done"), 1)
            link(dve.tensor_tensor(lam[:, 0:1], col("lam", 0), col("lam", 1), ALU.mult))
            dve.tensor_tensor(lam[:, 1:2], col("lam", 2), col("lam", 3), ALU.mult).then_inc(sem("lam_prod"), 1)
            wait("lam_exp")
            link(dve.tensor_tensor(lam[:, 4:5], lam[:, 3:4], lam[:, 2:3], ALU.subtract))
            link(dve.tensor_scalar(lam[:, 4:5], lam[:, 4:5], LAM_INIT, None, ALU.subtract))

            def ada_rows(v):
                dve.wait_ge(ada_used[1], v * 2 + 2)
                dve.tensor_copy(adarow[:, :], ps[:, 6, 0:T]).then_inc(sem("adarow_ready"), 1)

            def ada_mod(v):
                dve.wait_ge(sem("adacol_ready"), v + 1)
                src = ps[:, 6, T:2 * T].rearrange("p (b j r) -> p j b r", b=2, j=4)[:, :, :, 0]
                sl = bass.ds(v * KT, KT) if not isinstance(v, int) else slice(v * KT, (v + 1) * KT)
                dve.tensor_tensor(modv[:, sl].rearrange("p (j b) -> p j b", j=4), src,
                                  bada[:, sl].rearrange("p (j b) -> p j b", j=4), ALU.add).then_inc(sem("mod_ready"), 1)

            ada_rows(0)
            ada_mod(0)
            ada_rows(1)
            ada_mod(1)
            for s in range(3):
                refill(s)

            def norm(gain, shift, scale=None, final=False, vectors=0):
                if scale is not None:
                    dve.wait_ge(sem("mod_ready"), vectors)
                    link(stt(gmod[:, :], scale, 1.0, gain, ALU.add, ALU.mult))
                    gain = gmod
                wait("stat_read")
                link(dve.reciprocal(rstd[:, 0:T], root[:, 0:T]))

                def scaled(k):
                    stt(hf[:, k, :], xT[:, k, :], gain[:, k:k + 1], rstd[:, 0:T], ALU.mult, ALU.mult).then_inc(sem("t_ready"), 1)

                def low(k):
                    wait("h_high")
                    if shift is None:
                        ins = dve.tensor_tensor(hlo[:, k, :], hf[:, k, :], hhi[:, k, :].bitcast(F32), ALU.subtract)
                    else:
                        ins = stt(hlo[:, k, :], hf[:, k, :], shift[:, k:k + 1], hhi[:, k, :].bitcast(F32), ALU.add, ALU.subtract)
                    ins.then_inc(sem("h_ready"), 1)

                for k in range(KT):
                    scaled(k)
                    if k and not final:
                        low(k - 1)
                if not final:
                    low(KT - 1)

            def ng(l, i):
                return col("norm_g", (l * 3 + i) * KT, KT)

            norm(ng(0, 0), mod(0, 0), mod(0, 1), vectors=2)

            def chunked(stage, vec=None, nv=5, count=NCH, moe=False):
                b0, ch = first[stage], chunk0[stage]

                def hidden(c, parity):
                    dve.wait_ge(sem("silu_done"), c + ch + 1)
                    dve.wait_ge(used[1], c + b0[1] + 1)
                    if moe:
                        dve.tensor_tensor(hid[:, :], silu[:, :], ps[:, 1, :], ALU.mult).then_inc(sem("hid_done"), 1)
                        dve.wait_ge(sem("hid_done"), c + ch + 1)
                        dve.wait_ge(sem(f"comb_landed{parity}"), ((c - parity) * 8 + 16))
                        h3 = hid[:, :].rearrange("p (k t) -> p k t", k=2)
                        dve.tensor_tensor(h3, h3, cbuf[:, parity:parity + 1, :].to_broadcast([P, 2, T]), ALU.mult).then_inc(sem("scaled"), 1)
                    else:
                        dve.tensor_tensor(hid[:, :], silu[:, :], ps[:, 1, :], ALU.mult).then_inc(sem("hid_done"), 1)

                def hidden_low(c, parity):
                    dve.wait_ge(sem("hid_high"), c + ch + 1)
                    dve.tensor_tensor(hidlo[parity][:, :, :], hid[:, :].rearrange("p (k t) -> p k t", k=2),
                                      hidhi[parity][:, :, :].bitcast(F32), ALU.subtract).then_inc(sem("hid_split"), 1)

                def last_halves():
                    wait("last_high")
                    dve.tensor_tensor(columns(wlo[2], 0), columns(raw[2], 0), columns(whi[2], 0).bitcast(F32),
                                      ALU.subtract).then_inc(sem("last_split"), 1)
                    dve.wait_ge(high[2], b0[2] + count)
                    dve.tensor_tensor(columns(wlo[2], 1), columns(raw[2], 1), columns(whi[2], 1).bitcast(F32),
                                      ALU.subtract).then_inc(split[2], 1)

                def chunk(c, parity, down=True, more=True, v=None, last=False):
                    if more:
                        split_low(0, c + b0[0] + 1)
                    hidden(c, parity)
                    hidden_low(c, parity)
                    if more:
                        split_low(1, c + b0[1] + 1)
                    if v is not None:
                        ada_rows(v)
                    if last:
                        last_halves()
                    elif down:
                        split_low(2, c + b0[2])
                    if v is not None:
                        ada_mod(v)

                chunk(0, 0, down=False)
                pairs = (count - 2) // 2
                if vec is None:
                    nv = 0
                else:
                    with dve.Fori(0, min(nv, pairs)) as i:
                        for half in range(2):
                            chunk(i * 2 + 1 + half, (1 + half) % 2, v=i + vec if half else None)
                if nv < pairs:
                    with dve.Fori(nv, pairs) as i:
                        for half in range(2):
                            chunk(i * 2 + 1 + half, (1 + half) % 2)
                for c in range(2 * pairs + 1, count):
                    chunk(c, c % 2, more=not moe or c < count - 1, v=vec + nv - 1 if nv > pairs and c == 2 * nv else None,
                          last=(c == count - 1))
                for s in range(3):
                    turn[s] = b0[s] + count + (s < 2)

            def add_output(stage, scale=None, half=False, vectors=0):
                if half:
                    dve.wait_ge(sem("mod_ready"), vectors)
                    link(dve.tensor_scalar(ghalf[:, :], scale, 0.5, None, ALU.mult))
                    scale = ghalf
                for k in range(KT):
                    src = ps[:, 2 + k // 2, (k % 2) * T:(k % 2 + 1) * T]
                    if k in (0, 2, 4):
                        wait("out_pair")
                    elif k == 6:
                        dve.wait_ge(used[2], first[stage][2] + dict(STAGES)[stage])
                    if scale is None:
                        if k % 2 == 0:
                            continue
                        ins = dve.tensor_tensor(xT[:, k - 1:k + 1, :], ps[:, 2 + k // 2, :].rearrange("p (n t) -> p n t", n=2),
                                                xT[:, k - 1:k + 1, :], ALU.add)
                    else:
                        ins = stt(xT[:, k, :], src, scale[:, k:k + 1], xT[:, k, :])
                    if k % 2:
                        ins.then_inc(sem("x_ready"), 1)

            def add_units(stage, u0, gate):
                for j in range(4):
                    s, b = (u0 + j) % 3, (u0 + j) % 2 + (2 if stage == "blk2" else 0)
                    dve.wait_ge(used[s], first[stage][s] + (u0 + j) // 3 + 1)
                    if gate is None:
                        dve.tensor_tensor(xT[:, 2 * j:2 * j + 2, :], ps[:, b, :].rearrange("p (n t) -> p n t", n=2),
                                          xT[:, 2 * j:2 * j + 2, :], ALU.add).then_inc(sem("x_ready"), 1)
                    else:
                        stt(xT[:, 2 * j, :], ps[:, b, 0:T], gate[:, 2 * j:2 * j + 1], xT[:, 2 * j, :])
                        stt(xT[:, 2 * j + 1, :], ps[:, b, T:2 * T], gate[:, 2 * j + 1:2 * j + 2], xT[:, 2 * j + 1, :]).then_inc(sem("x_ready"), 1)
                    if j < 3:
                        refill(s)

            chunked("ffn0", 2)
            add_output("ffn0", mod(0, 2), half=True, vectors=3)
            norm(ng(0, 1), mod(0, 3), mod(0, 4), vectors=5)
            refill(2)

            def mix_low(sl):
                wait("mix_high")
                dve.tensor_tensor(mlo[:, sl, :], hf[:, sl, :], mhi[:, sl, :].bitcast(F32), ALU.subtract).then_inc(sem("mix_split"), 1)

            def qk_norm(i):
                wait("stat_read")
                link(dve.reciprocal(rstd[:, :], root[:, :]))
                dst = (q0 if i < 2 else k0)[:, 2 * (i % 2):2 * (i % 2) + 2, :]
                stt(dst, dst, qk_gain[:, i // 2:i // 2 + 1], rstd[:, :].rearrange("p (n t) -> p n t", n=2), ALU.mult, ALU.mult).then_inc(sem("qk_ready"), 1)

            qk_gain = col("qk_g", 0, 2)
            link(dve.tensor_scalar(qk_gain[:, 0:1], qk_gain[:, 0:1], 64 ** -0.5, None, ALU.mult))
            causal = c_("causal")

            def negative_max(i):
                wait("scores_ready")
                e, b = i % 4, 2 + i % 4
                diag = ps[:, b, :].rearrange("p (j n) -> p j n", j=2)[:, :, 0:P]
                link(dve.tensor_tensor(diag, diag, causal.rearrange("p (o n) -> p o n", o=1).to_broadcast([P, 2, P]), ALU.add))
                dve.tensor_reduce(negmax[:, e, 0:1], ps[:, b, 0:P], AX_X, ALU.max, negate=True)
                dve.tensor_reduce(negmax[:, e, 1:2], ps[:, b, P:3 * P], AX_X, ALU.max, negate=True).then_inc(sem("negmax_ready"), 1)

            def difference(h):
                e = (2 * h) % 4
                wait("exp_done", 2)
                link(dve.reciprocal(zinv[:, e:e + 2, :], zsum[:, e:e + 2, :]))
                link(dve.tensor_scalar(zinv[:, e + 1, :], zinv[:, e + 1, :], lam[:, 4:5], None, ALU.mult))
                pa = [exps[:, e, 0:P], exps[:, e, P:3 * P]]
                pb = [exps[:, e + 1, 0:P], exps[:, e + 1, P:3 * P]]
                dve.tensor_scalar(pa[0], pa[0], zinv[:, e, 0:1], None, ALU.mult)
                link(dve.tensor_scalar(pa[1], pa[1], zinv[:, e, 1:2], None, ALU.mult))
                stt(pa[0], pb[0], zinv[:, e + 1, 0:1], pa[0])
                stt(pa[1], pb[1], zinv[:, e + 1, 1:2], pa[1]).then_inc(sem("probs_ready"), 1)

            for u in range(8):
                if u == 7:
                    negative_max(0)
                    negative_max(1)
                refill(u % 3)
                if u == 3:
                    ada_rows(7)
                if u == 4:
                    ada_mod(7)
                if u == 7:
                    ada_rows(8)
                if 1 <= u <= 4:
                    qk_norm(u - 1)
            for h in range(4):
                difference(h)
                if h < 3:
                    negative_max(2 * h + 2)
                    negative_max(2 * h + 3)
                if h == 0:
                    ada_mod(8)
            mix_low(slice(4, 6))
            mix_low(slice(6, 8))
            for j in range(2):
                wait("stat_read")
                link(dve.reciprocal(rstd[:, :], root[:, :]))
                stt(hf[:, 2 * j:2 * j + 2, :], hf[:, 2 * j:2 * j + 2, :], col("subln"), rstd[:, :].rearrange("p (n t) -> p n t", n=2),
                    ALU.mult, ALU.mult).then_inc(sem("o_normed"), 1)
            mix_low(slice(0, 2))
            mix_low(slice(2, 4))
            add_units("mix0", 8, mod(0, 5))
            norm(ng(0, 2), mod(0, 6), mod(0, 7), vectors=8)
            refill(2)
            chunked("ffn1", 9)
            add_output("ffn1", mod(0, 8), half=True, vectors=9)
            norm(ng(1, 0), mod(1, 0), mod(1, 1), vectors=11)
            refill(2)
            chunked("ffn2", 14, 4)
            add_output("ffn2", mod(1, 2), half=True, vectors=12)

            norm(ng(1, 1), mod(1, 3), mod(1, 4), vectors=18)
            refill(2)
            link(dve.memset(vconv[:, :, 0:2], 0.0))
            for j in range(4):
                refill(0)
                u = 3 * j + 1
                wait("evacuated")
                dve.wait_ge(used[1], first["mix1"][1] + j + 1)
                dve.tensor_tensor(vconv[:, :, 2:T + 2], cgate.rearrange("p (n t) -> p n t", n=2),
                                  ps[:, u % 2, :].rearrange("p (n t) -> p n t", n=2), ALU.mult).then_inc(sem("v_done"), 1)
                refill(1)
                dve.wait_ge(sem("v_done"), j + 1)
                for tap in range(3):
                    for m in range(2):
                        w = col("conv_w", tap * KT + 2 * j + m)
                        if tap == 0:
                            ins = dve.tensor_scalar(yconv[:, m, :], vconv[:, m, 0:T], w, None, ALU.mult)
                        else:
                            ins = stt(yconv[:, m, :], vconv[:, m, tap:tap + T], w, yconv[:, m, :])
                        if m:
                            link(ins)
                dve.wait_ge(used[2], first["mix1"][2] + j + 1)
                dve.tensor_tensor(hf[:, 2 * j:2 * j + 2, :], yconv, ps[:, (u + 1) % 2, :].rearrange("p (n t) -> p n t", n=2),
                                  ALU.mult).then_inc(sem("y_done"), 1)
                refill(2)
                mix_low(slice(2 * j, 2 * j + 2))
            add_units("mix1", 12, mod(1, 5))
            norm(ng(1, 2), mod(1, 6), mod(1, 7), vectors=18)
            refill(0)
            chunked("ffn3")
            add_output("ffn3", mod(1, 8), half=True, vectors=18)

            norm(col("attn_norm", 0, KT), None)
            refill(2)
            cos_b, sin_b, cos_a, sin_a = (c_(x) for x in ("cos_moba", "sin_moba", "cos_mla", "sin_mla"))

            def both(t, rows):
                return t[rows, :].rearrange("p (o t) -> p o t", o=1).to_broadcast([rows.stop - rows.start, 2, T])

            def rope(r):
                wait("rope_swapped")
                if r:
                    dve.wait_ge(sem("roped"), r)
                b = (7, 6)[r % 2]
                if r == 0:
                    rows = slice(64, 96)
                    dve.tensor_tensor(swapped[rows, 0, :], ps[rows, b, 0:T], sin_a[rows, :], ALU.mult).then_inc(sem("rope_read"), 1)
                    link(dve.tensor_tensor(krope[rows, :], krope[rows, :], cos_a[rows, :], ALU.mult))
                    dve.wait_ge(sem("rope_read"), r + 1)
                    link(dve.tensor_tensor(krope[rows, :], krope[rows, :], swapped[rows, 0, :], ALU.add))
                    dve.tensor_copy(kA[rows, :, :], krope[rows, :].rearrange("p (o t) -> p o t", o=1).to_broadcast([32, MLA_H, T])).then_inc(sem("roped"), 1)
                    return
                if r < 5:
                    rows, c, s = slice(0, P), cos_b, sin_b
                    x = q0[:, 2 * (r - 1):2 * r, :] if r < 3 else k0[:, 2 * (r - 3):2 * (r - 2), :]
                else:
                    rows, c, s = slice(64, 96), cos_a, sin_a
                    x = qA[rows, 2 * (r - 5):2 * (r - 4), :]
                sw = swapped[rows, :, :]
                dve.tensor_tensor(sw, ps[rows, b, :].rearrange("p (n t) -> p n t", n=2), both(s, rows), ALU.mult).then_inc(sem("rope_read"), 1)
                link(dve.tensor_tensor(x, x, both(c, rows), ALU.mult))
                dve.wait_ge(sem("rope_read"), r + 1)
                dve.tensor_tensor(x, x, sw, ALU.add).then_inc(sem("roped"), 1)

            def latent(j):
                wait("stat_read")
                sl = slice(j * T, (j + 1) * T)
                link(dve.reciprocal(rstd[:, sl], root[:, sl]))
                for k in range(*((0, 6) if j == 0 else (6, 8))):
                    g = col("q_norm", k) if j == 0 else col("kv_norm", k - 6)
                    ins = stt(hf[:, k, :], hf[:, k, :], g, rstd[:, sl], ALU.mult, ALU.mult)
                ins.then_inc(sem("latent_normed"), 1)

            def latent_low(j):
                wait("latent_high")
                sl = slice(0, 6) if j == 0 else slice(6, 8)
                dve.tensor_tensor(mlo[:, sl, :], hf[:, sl, :], mhi[:, sl, :].bitcast(F32), ALU.subtract).then_inc(sem("latent_split"), 1)

            for u in range(11):
                refill(u % 3)
                if u == 4:
                    latent(0)
                if u == 5:
                    latent(1)
                    rope(0)
                if 6 <= u < 10:
                    rope(u - 5)
                if u == 8:
                    latent_low(0)
                    latent_low(1)
            refill(2)
            for u in UQ_UNITS:
                refill(u % 3)
                if u > UQ_UNITS[0]:
                    rope(5 + u - UQ_UNITS[0] - 1)
            rope(8)

            def normalised(i):
                e = i % 4
                wait("exp_done")
                link(dve.reciprocal(zinv[:, e, :], zsum[:, e, :]))
                dve.tensor_scalar(exps[:, e, 0:P], exps[:, e, 0:P], zinv[:, e, 0:1], None, ALU.mult)
                dve.tensor_scalar(exps[:, e, P:3 * P], exps[:, e, P:3 * P], zinv[:, e, 1:2], None, ALU.mult).then_inc(sem("probs_ready"), 1)

            def o_low(j):
                tile_ = 4 + j if j < 4 else j - 4
                wait("o_high")
                dve.tensor_tensor(mlo[:, tile_, :], ps[:, 6, 0:T], mhi[:, tile_, :].bitcast(F32), ALU.subtract).then_inc(sem("o_split"), 1)

            negative_max(0)
            negative_max(1)
            normalised(0)
            for i in range(16):
                if i + 2 < 16:
                    negative_max(i + 2)
                if i + 1 < 16:
                    normalised(i + 1)
                if i % 2:
                    if i > 1:
                        o_low(i // 2 - 1)
                    refill((16 + i // 2) % 3)
            o_low(7)
            for j in range(2):
                banks = ((2, 4), (0, 6))[j]
                for which in range(2 - j):
                    refill((24 + 2 * j + which) % 3)
                for which in range(2):
                    u = 24 + 2 * j + which
                    dve.wait_ge(used[u % 3], first["blk2"][u % 3] + u // 3 + 1)
                    if which == 0:
                        wait("gates_ready")
                    g = gates[:, which, 4 * j:4 * j + 4, :]
                    src = ps[:, banks[which]:banks[which] + 2, :].rearrange("p b (n t) -> p (b n) t", n=2)
                    link(dve.tensor_tensor(hf[:, 4 * j:4 * j + 4, :] if which == 0 else g, g, src, ALU.mult))
                dve.tensor_tensor(hf[:, 4 * j:4 * j + 4, :], hf[:, 4 * j:4 * j + 4, :], gates[:, 1, 4 * j:4 * j + 4, :], ALU.add).then_inc(sem("mixed"), 1)
                wait("mixed_high")
                dve.tensor_tensor(hlo[:, 4 * j:4 * j + 4, :], hf[:, 4 * j:4 * j + 4, :], hhi[:, 4 * j:4 * j + 4, :].bitcast(F32),
                                  ALU.subtract).then_inc(sem("mixed_split"), 1)
            refill(27 % 3)
            add_units("blk2", 28, None)

            norm(col("ffn_norm", 0, KT), None)
            refill(1)
            wait("logits_ready")
            link(dve.tensor_copy(logit[:, :, :], ps[:, 7, 0:P].rearrange("p (t n) -> p t n", t=2)[:, :, 0:NG + NE]))
            rank = c_("rank")

            def r_(o, n):
                return rt[:, o:o + 2 * n].rearrange("p (t n) -> p t n", t=2)

            def spread(x, n):
                return x.to_broadcast([P, 2, n])

            def first_best(x, best, cand, hot, n):
                link(dve.tensor_reduce(best, x, AX_X, ALU.max))
                link(dve.tensor_tensor(cand, x, spread(best, n), ALU.is_equal))
                link(dve.tensor_tensor(cand, cand, rank[:, 8 - n:8].rearrange("p (o n) -> p o n", o=1).to_broadcast([P, 2, n]), ALU.mult))
                link(dve.tensor_reduce(r_(252, 1), cand, AX_X, ALU.max))
                link(dve.tensor_tensor(hot, cand, spread(r_(252, 1), n), ALU.is_equal))

            gl = logit[:, :, 0:NG]
            el = logit[:, :, NG:NG + NE].rearrange("p t (g e) -> p t g e", g=NG)
            gbest, ghot, gcand = r_(0, 1), r_(2, NG), r_(10, NG)
            first_best(gl, gbest, gcand, ghot, NG)
            dve.tensor_tensor(r_(56, NG), gl, spread(gbest, NG), ALU.subtract).then_inc(sem("router_max"), 1)
            wait("router_exp")
            pg = r_(18, 1)
            link(dve.tensor_reduce(pg, r_(64, NG), AX_X, ALU.add))
            link(dve.reciprocal(pg, pg))
            picked = r_(72, EG)
            link(dve.tensor_tensor(picked, el[:, :, 0, :], spread(ghot[:, :, 0:1], EG), ALU.mult))
            tmp = r_(88, EG)
            for g in range(1, NG):
                link(dve.tensor_tensor(tmp, el[:, :, g, :], spread(ghot[:, :, g:g + 1], EG), ALU.mult))
                link(dve.tensor_tensor(picked, picked, tmp, ALU.add))
            best1, hot1 = r_(20, 1), r_(104, EG)
            first_best(picked, best1, tmp, hot1, EG)
            rest = r_(136, EG)
            link(dve.tensor_scalar(rest, hot1, BIG, None, ALU.mult))
            link(dve.tensor_tensor(rest, rest, picked, ALU.add))
            best2, hot2 = r_(22, 1), r_(152, EG)
            first_best(rest, best2, tmp, hot2, EG)
            dve.tensor_tensor(r_(128, 1), best2, best1, ALU.subtract).then_inc(sem("router_two"), 1)
            wait("router_exp")
            w1, w2 = r_(24, 1), r_(26, 1)
            link(dve.tensor_scalar(w1, r_(130, 1), 1.0, None, ALU.add))
            link(dve.reciprocal(w1, w1))
            link(dve.tensor_tensor(w1, w1, pg, ALU.mult))
            link(dve.tensor_tensor(w2, w1, r_(130, 1), ALU.mult))
            link(dve.tensor_tensor(hot1, hot1, spread(w1, EG), ALU.mult))
            link(dve.tensor_tensor(hot2, hot2, spread(w2, EG), ALU.mult))
            link(dve.tensor_tensor(hot1, hot1, hot2, ALU.add))
            for g in range(NG):
                ins = dve.tensor_tensor(comb[:, :, EG * g:EG * g + EG], hot1, spread(ghot[:, :, g:g + 1], EG), ALU.mult)
            ins.then_inc(sem("comb_ready"), 1)

            chunked("moe", count=NE, moe=True)
            add_output("moe")
            norm(col("final_norm", 0, KT), None, final=True)


_INS = ["x", "c", "norm_g", "w_ada", "b_ada", "ffn_wg", "ffn_wu", "ffn_wd", "w_in_ab", "qk_norm_g", "lambda_q1",
        "lambda_k1", "lambda_q2", "lambda_k2", "subln_g", "pool_w", "pool_scale", "w_out_ab", "w_in_c", "conv_w",
        "w_out_c", "attn_norm_2", "w_in_2", "q_norm_2", "w_uq_2", "kv_norm_2", "w_ukv_2", "w_o_mla_2", "w_o_moba_2",
        "w_out_2", "ffn_norm_2", "w_router_group_2", "b_router_group_2", "w_router_expert_2", "b_router_expert_2",
        "w_exp_gate_2", "w_exp_up_2", "w_exp_down_2", "final_norm_2"]


def kernel(**inputs):
    import concourse.bacc as _bacc
    from concourse.bass_utils import run_bass_kernel_spmd as _run

    nc = _bacc.Bacc("TRN2", target_bir_lowering=False, num_devices=1)
    arrays, aps = {}, {}
    for name in _INS:
        a = np.ascontiguousarray(inputs[name])
        arrays[f"in_{name}_dram"] = a
        aps[name] = nc.dram_tensor(f"in_{name}_dram", a.shape, mybir.dt.from_np(a.dtype), kind="ExternalInput").ap()
    table, _ = constants()
    arrays["const_dram"] = table
    const_dram = nc.dram_tensor("const_dram", table.shape, F32, kind="ExternalInput").ap()
    out = nc.dram_tensor("out_0_dram", (1, T, D), F32, kind="ExternalOutput").ap()
    build(nc, aps, const_dram, out)
    r = _run(nc, [arrays], core_ids=[0])
    return r.results[0]["out_0_dram"]
```

```python
from contextlib import ExitStack

import numpy as np

import concourse.bass as bass
from concourse import mybir

F32 = mybir.dt.float32
F32R = mybir.dt.float32r
ALU = mybir.AluOpType
ACT = mybir.ActivationFunctionType
AX_X = mybir.AxisListType.X

P = 128
T = 256
D = 1024
KT = D // P
F = 2816
CH = 256
NCH = F // CH
NE = 32
NG = 4
EG = NE // NG
NMOD = 9
EPS = 1e-6
BIG = -3.0e38
LAM_INIT = 0.8 - 0.6 * 1.0
UW = 2048

MLA_H, MLA_NOPE, MLA_ROPE, MLA_V = 8, 64, 32, 64
MLA_Q = MLA_NOPE + MLA_ROPE
MOBA_H, MOBA_HD, MOBA_ROT = 8, 64, 16
QL, KVL = 768, 256
C_Q, C_KV, C_KR = 0, QL, QL + KVL
C_QB = C_KR + MLA_ROPE
C_KB, C_VB = C_QB + 512, C_QB + 1024
C_GA, C_GB = C_QB + 1536, C_QB + 1536 + D

STAGES = [
    ("ffn0", NCH), ("mix0", 12), ("ffn1", NCH), ("ffn2", NCH), ("mix1", 16), ("ffn3", NCH),
    ("blk2", 32), ("moe", NE),
]
CHUNKED = ("ffn0", "ffn1", "ffn2", "ffn3", "moe")
KR_UNIT, UQ_UNITS = 4, (12, 13, 14, 15)


def unit_width(stage, u):
    if stage == "blk2" and u == KR_UNIT:
        return KT * MLA_Q
    if stage == "blk2" and u in UQ_UNITS:
        return (QL // P) * 2 * MLA_Q
    return UW


def slot_plan():
    first, widths, chunks, n = {}, [[], [], []], {}, 0
    for stage, units in STAGES:
        first[stage] = [len(w) for w in widths]
        chunks[stage] = n
        if stage in CHUNKED:
            n += units
            for s in range(3):
                widths[s] += [UW] * units
        else:
            for u in range(units):
                widths[u % 3].append(unit_width(stage, u))
    return first, widths, chunks


def constants():
    parts, at = [], {}

    def put(name, a):
        a = np.asarray(a, np.float32)
        full = np.zeros((P, a.shape[1]), np.float32)
        full[: a.shape[0]] = a
        at[name] = (sum(x.shape[1] for x in parts), a.shape[1])
        parts.append(full)

    i = np.arange(P)
    put("ident", np.eye(P))
    put("ones", np.ones((P, P)))
    put("halves", (i[:, None] // 64 == i[None, :] // 64))
    moba = np.zeros((P, P))
    for o in (0, MOBA_HD):
        for r in range(MOBA_ROT // 2):
            moba[o + r + MOBA_ROT // 2, o + r] = -1
            moba[o + r, o + r + MOBA_ROT // 2] = 1
    put("swap_moba", moba)
    mla = np.zeros((P, MLA_ROPE))
    for r in range(MLA_ROPE // 2):
        mla[MLA_NOPE + r + MLA_ROPE // 2, r] = -1
        mla[MLA_NOPE + r, r + MLA_ROPE // 2] = 1
    put("swap_mla", mla)
    put("causal", np.where(i[None, :] <= i[:, None], 0.0, BIG))

    def rope(rot):
        half = rot // 2
        freq = np.power(np.float32(500000.0), -np.arange(half, dtype=np.float32) / np.float32(half)).astype(np.float32)
        ang = (np.arange(T, dtype=np.float32)[:, None] * freq[None, :]).astype(np.float32)
        return np.cos(ang).T, np.sin(ang).T

    cos, sin = rope(MOBA_ROT)
    c, s = np.ones((P, T)), np.zeros((P, T))
    for o in (0, MOBA_HD):
        c[o:o + MOBA_ROT] = np.concatenate([cos, cos])
        s[o:o + MOBA_ROT] = np.concatenate([sin, sin])
    put("cos_moba", c)
    put("sin_moba", s)
    cos, sin = rope(MLA_ROPE)
    c, s = np.ones((P, T)), np.zeros((P, T))
    c[MLA_NOPE:MLA_Q] = np.concatenate([cos, cos])
    s[MLA_NOPE:MLA_Q] = np.concatenate([sin, sin])
    put("cos_mla", c)
    put("sin_mla", s)
    t = np.arange(16)
    put("inv_count", np.tile(np.concatenate([1.0 / np.minimum(t + 1, w) for w in (2, 4, 8, 16)]).astype(np.float32), (P, 1)))
    put("rank", np.tile(np.arange(8, 0, -1), (P, 1)))
    put("iota", np.tile(i, (P, 1)))
    put("before", (i[:, None] < i[None, :]))
    put("group_base", np.tile(np.arange(NG) * EG, (P, 1)))
    return np.concatenate(parts, axis=1), at


ROWS = {}
_n = 0
for _name, _k in (("c", 8), ("norm_g", 48), ("conv_w", 24), ("pool_scale", 4), ("attn_norm", 8), ("q_norm", 6),
                  ("kv_norm", 2), ("ffn_norm", 8), ("final_norm", 8), ("subln", 1), ("qk_g", 2), ("lam", 4)):
    ROWS[_name] = (_n, _k)
    _n += _k
NROWS = _n


def build(nc, a, const_dram, out):
    first, widths, chunk0 = slot_plan()
    const_np, const_at = constants()
    late_at = const_at["iota"][0]

    ctx = ExitStack()
    with ctx:
        offset_of = {}

        def sb(name, shape, dt=F32):
            offset_of[name] = nc.sbuf_base
            return ctx.enter_context(nc.sbuf_tensor(name, shape, dt))


        def sb_over(name, under, column, shape):
            return nc.alloc_sbuf_tensor_at(name, shape, F32R, offset=offset_of[under] + 4 * column)

        sem_of = {}

        def sem(name):
            if name not in sem_of:
                sem_of[name] = ctx.enter_context(nc.semaphore(name))
            return sem_of[name]

        raw = [sb(f"raw{s}", [P, UW]) for s in range(3)]
        whi = [sb(f"whi{s}", [P, UW], F32R) for s in range(3)]
        wlo = [sb(f"wlo{s}", [P, UW], F32R) for s in range(3)]
        ada_raw = sb("ada_raw", [P, 2, UW])
        xT = sb("xT", [P, KT, T])
        hf = sb("hf", [P, KT, T])
        hhi = sb("hhi", [P, KT, T], F32R)
        hlo = sb("hlo", [P, KT, T], F32R)
        mhi = sb("mhi", [P, KT, T], F32R)
        mlo = sb("mlo", [P, KT, T], F32R)
        act_tile = sb("act_tile", [P, 4 * T])
        silu, hid = act_tile[:, 0:2 * T], act_tile[:, 2 * T:4 * T]
        sq = act_tile[:, :].rearrange("p (i n) -> p i n", i=2)
        hidhi = [sb(f"hidhi{i}", [P, 2, T], F32R) for i in range(2)]
        hidlo = [sb(f"hidlo{i}", [P, 2, T], F32R) for i in range(2)]
        arena = sb("arena", [P, 8192])
        exps = sb("exps", [P, 4, 384])
        probsT = sb("probsT", [P, 2, 384])
        root = sb("root", [P, 2 * T])
        rstd = sb("rstd", [P, 2 * T])
        swapped = exps[:, 0:2, 0:T]
        cst = sb("cst", [P, late_at])
        zeros = sb("zeros", [P, P], F32R)
        vcols = sb("vcols", [P, NROWS])
        bada = sb("bada", [P, 2 * NMOD * KT])
        modv = sb("modv", [P, 2 * NMOD * KT])
        adarow = sb("adarow", [P, T])
        cact = sb("cact", [P, KT])
        gmod = sb("gmod", [P, KT])
        ghalf = sb("ghalf", [P, KT])
        lam = sb("lam", [P, 8])
        negmax = sb("negmax", [P, 4, 2])
        zsum = sb("zsum", [P, 4, 2])
        zinv = sb("zinv", [P, 4, 2])
        wrout = sb("wrout", [P, KT, NG + NE])
        brout = sb("brout", [1, NG + NE])

        def c_(name, rows=slice(0, P)):
            o, n = const_at[name]
            return cst[rows, o:o + n] if o < late_at else late[rows, o - late_at:o - late_at + n]

        def col(name, k=0, n=1):
            o, _ = ROWS[name]
            return vcols[:, o + k:o + k + n]

        def mod(layer, v, k=None):
            o = (layer * NMOD + v) * KT
            return modv[:, o:o + KT] if k is None else modv[:, o + k:o + k + 1]

        ident, ones = c_("ident"), c_("ones")
        ar = lambda o, n: arena[:, o:o + n]
        xin = ar(0, 2048).rearrange("p (t d) -> p t d", t=2)
        q0 = ar(0, 1024).rearrange("p (h t) -> p h t", h=4)
        k0 = ar(1024, 1024).rearrange("p (h t) -> p h t", h=4)
        v0 = ar(2048, 1024).rearrange("p (t n) -> p t n", t=2)
        PADT = T + 16
        pool_in = ar(3072, 4 * PADT).rearrange("p (g t) -> p g t", g=4)
        pool_a = ar(3072 + 4 * PADT, 4 * PADT).rearrange("p (g t) -> p g t", g=4)
        pool_b = ar(3072 + 8 * PADT, 4 * PADT).rearrange("p (g t) -> p g t", g=4)
        pool_d = ar(3072 + 12 * PADT, 4 * T).rearrange("p (g t) -> p g t", g=4)
        cgate = ar(0, 2 * T)
        vconv = ar(512, 2 * (T + 2)).rearrange("p (g t) -> p g t", g=2)
        yconv = ar(1040, 2 * T).rearrange("p (g t) -> p g t", g=2)
        vA = ar(3072, 1024).rearrange("p (t n) -> p t n", t=2)
        qA = ar(4096, 2048).rearrange("p (h t) -> p h t", h=8)
        kA = ar(6144, 2048).rearrange("p (h t) -> p h t", h=8)
        krope = adarow[:, :]
        poolw = ar(7424, 4 * P).rearrange("p (g n) -> p g n", g=4)
        vrows = ar(2048, P)
        brows = arena[0:72, 2048 + P:2048 + 3 * P].rearrange("p (l n) -> p l n", l=2)
        htok_hi = sb_over("htok_hi", "arena", 0, [P, 2, D])
        rt = ar(2048, 256)
        logit = ar(2304, 2 * (NG + NE)).rearrange("p (t n) -> p t n", t=2)
        slot_w = ar(2376, (NG + 1) * EG)
        place = ar(2416, 32)
        late = ar(2448, 260)
        pick = sb_over("pick", "arena", 2712, [P, 2, NG + 1, P])
        htok_lo = sb_over("htok_lo", "arena", 4096, [P, 2, D])
        pickT = sb_over("pickT", "exps", 0, [P, NG + 1, T])
        raw_odd = [ada_raw[:, 0, :], ada_raw[:, 1, :], ar(6144, 2048)]
        silu2 = act_tile[:, 0:2 * T].rearrange("p (i n) -> p i n", i=2)
        hid2 = act_tile[:, 2 * T:4 * T].rearrange("p (i n) -> p i n", i=2)
        y_hi = sb_over("y_hi", "hf", 0, [P, D])
        y_lo = sb_over("y_lo", "hf", D, [P, D])
        gates = ada_raw[:, :, :].rearrange("p g (k t) -> p g k t", k=KT)
        xout = xin

        ps = ctx.enter_context(nc.psum_tensor("ps", [P, 8, 512], F32))
        overflow = sb("overflow", [P, 2], mybir.dt.int32)

        landed = [sem(f"landed{s}") for s in range(3)]
        high = [sem(f"high{s}") for s in range(3)]
        split = [sem(f"split{s}") for s in range(3)]
        used = [sem(f"used{s}") for s in range(3)]
        landed_odd = [sem(f"landed_odd{s}") for s in range(3)]
        ada_landed = [sem(f"ada_landed{i}") for i in range(2)]
        ada_used = [sem(f"ada_used{i}") for i in range(2)]

        class Tally:

            def __init__(self, eng):
                self.eng, self.n = eng, {}

            def __call__(self, name, k=1):
                self.n[name] = self.n.get(name, 0) + k
                self.eng.wait_ge(sem(name), self.n[name])

        def experts_of(eng, g, step, ends):
            head, tail, e0 = 3, (5 if ends else 7), g * EG
            for j in range(head):
                step(e0 + j, j % 2, j)
            with eng.Fori(0, (tail - head) // 2) as i:
                for half in range(2):
                    step(i * 2 + (e0 + head + half), (head + half) % 2, None)
            for j in range(tail, EG):
                step(e0 + j, j % 2, j)

        def weights_of(s, parity):
            return raw_odd[s] if parity else raw[s][:, :]

        BESIDE = {0: (0,), 1: (1,), 2: (2, 3)}

        def follows(j, ends, n):
            return j is None or not ends or j + n < EG

        b_moe = first["moe"]

        block = ctx.enter_context(nc.Block())

        def columns(t, half):
            return t[:, :].rearrange("p (k n) -> p k n", k=2)[:, :, half * UW // 4:(half + 1) * UW // 4]

        def kxn(w, c0, n):
            return w[:, c0:c0 + n].rearrange("(k p) n -> p k n", p=P)

        def dyn(w, c, n=CH):
            return w[:, bass.ds(c * n, n)].rearrange("(k p) n -> p k n", p=P)

        def unit_source(stage, u):
            if stage == "mix0":
                if u < 8:
                    return kxn(a["w_in_ab"][0], (0, 256, 512, 768, 1536, 1792, 1024, 1280)[u], 256)
                return kxn(a["w_out_ab"][0], (u - 8) * 256, 256)
            if stage == "mix1":
                if u < 12:
                    return kxn(a["w_in_c"][0], (D, 2 * D, 0)[u % 3] + (u // 3) * 256, 256)
                return kxn(a["w_out_c"][0], (u - 12) * 256, 256)
            w = a["w_in_2"][0]
            if u < 4:
                return kxn(w, u * 256, 256)
            if u == KR_UNIT:
                return kxn(w, C_KR - MLA_NOPE, MLA_Q)
            if u < 11:
                return kxn(w, C_QB + (u - 5) * 256, 256)
            if u == 11:
                return kxn(a["w_ukv_2"][0], 0, D)
            if u < 16:
                return kxn(a["w_uq_2"][0], (u - 12) * 2 * MLA_Q, 2 * MLA_Q)
            if u < 24:
                return kxn(w, C_GA + (u - 16) * 256, 256)
            if u < 28:
                return kxn(a[("w_o_mla_2", "w_o_moba_2")[u % 2]][0], ((u - 24) // 2) * 512, 512)
            return kxn(a["w_out_2"][0], (u - 28) * 256, 256)

        @block.sync
        def _(sp):
            def small(dst, src, name="small_landed"):
                sp.dma_start(dst, src).then_inc(sem(name), 16)

            small(xin, a["x"][0].rearrange("(t p) d -> p t d", p=P), "x_landed")
            small(cst[:, :], const_dram[:, 0:late_at], "const_landed")
            sp.wait_ge(sem("rows_cleared"), 1)

            def rows(name, src, cols=slice(0, P)):
                o, n = ROWS[name]
                small(vrows[o:o + n, cols], src, "rows_landed")

            rows("c", a["c"].rearrange("a (k p) -> (a k) p", p=P))
            rows("norm_g", a["norm_g"].rearrange("l n (k p) -> (l n k) p", p=P))
            rows("conv_w", a["conv_w"].rearrange("l n (k p) -> (l n k) p", p=P))
            rows("pool_scale", a["pool_scale"].rearrange("l (k p) -> (l k) p", p=P))
            rows("attn_norm", a["attn_norm_2"].rearrange("l (k p) -> (l k) p", p=P))
            rows("q_norm", a["q_norm_2"].rearrange("l (k p) -> (l k) p", p=P))
            rows("kv_norm", a["kv_norm_2"].rearrange("l (k p) -> (l k) p", p=P))
            rows("ffn_norm", a["ffn_norm_2"].rearrange("l (k p) -> (l k) p", p=P))
            rows("final_norm", a["final_norm_2"].rearrange("(k p) -> k p", p=P))
            rows("subln", a["subln_g"])
            for half in range(2):
                rows("qk_g", a["qk_norm_g"][0], slice(64 * half, 64 * half + 64))
            o, _ = ROWS["lam"]
            for i, name in enumerate(("lambda_q1", "lambda_k1", "lambda_q2", "lambda_k2")):
                small(vrows[o + i:o + i + 1, 0:64], a[name], "rows_landed")
            small(brows[:, :, :], a["b_ada"].rearrange("l (r p) -> r l p", p=P), "rows_landed")

            def ada_load(layer, v, r, n):
                i = r % 2
                if not isinstance(n, int) or n > 0:
                    sp.wait_ge(ada_used[i], n)
                rows_ = a["w_ada"][layer][r * 256:(r + 1) * 256, :]
                src = rows_[:, bass.ds(v * D, D)] if not isinstance(v, int) else rows_[:, v * D:(v + 1) * D]
                sp.dma_start(ada_raw[:, i, :].rearrange("p (k n) -> p k n", k=2),
                             src.rearrange("(k p) n -> p k n", p=P)).then_inc(ada_landed[i], 16)

            last_down = []

            def load(s, n, src, width=UW):
                if s == 2 and last_down:
                    load_last = last_down.pop()
                    load_last()
                if not isinstance(n, int) or n > 0:
                    sp.wait_ge(split[s], n)
                k = src.shape[1]
                sp.dma_start(raw[s][:, 0:width].rearrange("p (k n) -> p k n", k=k), src).then_inc(landed[s], 16)

            def load_unit(stage, u):
                s = u % 3
                load(s, first[stage][s] + u // 3, unit_source(stage, u), unit_width(stage, u))

            def chunk_loads(stage, wg, wu, wd, ada=None):
                b = first[stage]

                def pair(c):
                    load(0, c + b[0], wg(c))
                    load(1, c + b[1], wu(c))

                def down(c):
                    load(2, c + b[2], wd(c))

                layer, v0_, nv = ada if ada else (0, 0, 0)

                def quarters(half, i):
                    if ada:
                        for r in (2 * half, 2 * half + 1):
                            ada_load(layer, i + v0_, r, i * 2 + 2 * (layer * NMOD + v0_) + r // 2)

                if stage != "ffn0":
                    pair(0)
                    down(0)
                pair(1)
                quarters(0, 0)
                full = (NCH - 1) // 2 - 1
                looped = min(full, nv - 1) if nv else full
                with sp.Fori(0, looped) as i:
                    for half in range(2):
                        pair(i * 2 + 2 + half)
                        quarters(1 - half, i + half)
                        down(i * 2 + 1 + half)
                for c in range(2 * looped + 1, NCH - 1):
                    pair(c + 1)
                    if c == 2 * nv - 1:
                        quarters(1, nv - 1)
                    down(c)
                last_down.append(lambda: down(NCH - 1))

            ADA_BEHIND = {4: (7, (0, 1)), 6: (7, (2, 3)), 8: (8, (0, 1)), 10: (8, (2, 3))}

            def vector_loads(v, quarters=(0, 1, 2, 3)):
                for r in quarters:
                    ada_load(v // NMOD, v % NMOD, r, 2 * v + r // 2)

            for v in range(2):
                vector_loads(v, (0, 1))
                load(v, 0, kxn((a["ffn_wg"], a["ffn_wu"])[v][0, 0], 0, CH))
                vector_loads(v, (2, 3))
            load(2, 0, a["ffn_wd"][0, 0][0:CH, :].rearrange("(k p) n -> p k n", p=P))
            small(poolw[:, :, :], a["pool_w"][0].rearrange("g c d -> c g d"))
            small(wrout[:, :, 0:NG], a["w_router_group_2"][0].rearrange("(k p) g -> p k g", p=P))
            for g in range(NG):
                small(wrout[:, :, NG + EG * g:NG + EG * g + EG],
                      a["w_router_expert_2"][0, g].rearrange("(k p) e -> p k e", p=P))
            small(brout[:, 0:NG], a["b_router_group_2"])
            small(brout[:, NG:NG + NE], a["b_router_expert_2"].rearrange("l g e -> l (g e)"))

            def dense(stage, layer, j, ada):
                wg, wu, wd = a["ffn_wg"][layer, j], a["ffn_wu"][layer, j], a["ffn_wd"][layer, j]

                def down(c):
                    w = wd[bass.ds(c * CH, CH), :] if not isinstance(c, int) else wd[c * CH:(c + 1) * CH, :]
                    return w.rearrange("(k p) n -> p k n", p=P)

                chunk_loads(stage, lambda c: dyn(wg, c) if not isinstance(c, int) else kxn(wg, c * CH, CH),
                            lambda c: dyn(wu, c) if not isinstance(c, int) else kxn(wu, c * CH, CH), down, ada)

            dense("ffn0", 0, 0, (0, 2, 5))
            for u in range(12):
                load_unit("mix0", u)
                if u in ADA_BEHIND:
                    vector_loads(*ADA_BEHIND[u])
            dense("ffn1", 0, 1, (1, 0, 5))
            dense("ffn2", 1, 0, (1, 5, 4))
            for u in range(16):
                load_unit("mix1", u)
            dense("ffn3", 1, 1, None)
            for u in range(32):
                load_unit("blk2", u)

            def expert(e, parity, src_e=None):
                src_e = e if src_e is None else src_e
                for s, w in enumerate((a["w_exp_gate_2"], a["w_exp_up_2"], a["w_exp_down_2"])):
                    w = w[0, src_e] if isinstance(src_e, int) else w[0, bass.ds(src_e, 1)].rearrange("e k n -> (e k) n")
                    w = w.rearrange("(k p) n -> p k n", p=P)
                    if isinstance(e, int) and e == 0:
                        load(s, b_moe[s], w)
                        continue
                    if not isinstance(e, int) or e > 1:
                        sp.wait_ge(split[s], e + (b_moe[s] - 1))
                    sp.dma_start(weights_of(s, parity).rearrange("p (k n) -> p k n", k=w.shape[1]),
                                 w).then_inc((landed_odd if parity else landed)[s], 16)

            expert(0, 0)
            sp.wait_ge(sem("mixed"), 2)
            small(late, const_dram[:, late_at:], "late_landed")
            expert(1, 1)
            with sp.Fori(0, (NE - 2) // 2) as i:
                for half in range(2):
                    expert(i * 2 + 2 + half, half)
            sp.wait_ge(sem("overflow_known"), 1)
            has_fifth = sp.value_load(overflow[0:1, 0:1], min_val=0, max_val=1)
            base = sp.value_load(overflow[0:1, 1:2], min_val=0, max_val=NE - EG)
            with sp.If(has_fifth > 0):
                with sp.Fori(0, EG // 2) as i:
                    for half in range(2):
                        expert(i * 2 + NE + half, half, base + (i * 2 + half))

            for t in range(2):
                sp.wait_ge(sem("out_ready"), t + 1)
                sp.dma_start(out[0, t * P:(t + 1) * P, :], xout[:, t, :]).then_inc(sem("out_stored"), 16)
            sp.wait_ge(sem("out_stored"), 32)

        @block.gpsimd
        def _(pool):
            wait = Tally(pool)
            n = [0]

            def link(ins):
                n[0] += 1
                ins.then_inc(sem("pool_self"), 1)
                pool.wait_ge(sem("pool_self"), n[0])

            pool.memset(zeros[:, :].bitcast(F32), 0.0).then_inc(sem("zeros_ready"), 1)
            wait("const_landed", 16)
            link(pool.memset(pool_in[:, :, 0:16], 0.0))
            link(pool.memset(pool_a[:, :, 0:16], 0.0))
            link(pool.memset(pool_b[:, :, 0:16], 0.0))
            wait("pool_in_ready", 2)
            src, dst = pool_in, pool_a
            for g, w in enumerate((2, 4, 8, 16)):
                h = w // 2
                link(pool.tensor_tensor(dst[:, g:4, 16:PADT], src[:, g:4, 16:PADT], src[:, g:4, 16 - h:PADT - h], ALU.add))
                o, _ = const_at["inv_count"]
                link(pool.tensor_tensor(pool_d[:, g, 0:16], dst[:, g, 16:32], cst[:, o + g * 16:o + g * 16 + 16], ALU.mult))
                link(pool.tensor_scalar(pool_d[:, g, 16:T], dst[:, g, 32:PADT], 1.0 / w, None, ALU.mult))
                ins = pool.tensor_tensor(pool_d[:, g, :], pool_d[:, g, :], pool_in[:, g, 16:PADT], ALU.subtract)
                if g < 3:
                    link(ins)
                else:
                    ins.then_inc(sem("pooled"), 1)
                if g == 0:
                    src, dst = pool_a, pool_b
                else:
                    src, dst = dst, src

        @block.tensor
        def _(pe):
            wait = Tally(pe)
            freed = {}

            def own(bank):
                if bank in freed:
                    pe.wait_ge(*freed.pop(bank))

            counts = {}

            def frees(bank, name):
                counts[name] = counts.get(name, 0) + 1
                freed[bank] = (sem(name), counts[name])

            def three(o, wh, wl, xh, xl, start, stop, shared=False):
                pe.matmul(o, wh, xh, start=start, stop=False, skip_group_check=shared)
                pe.matmul(o, wh, xl, start=False, stop=False, skip_group_check=shared)
                return pe.matmul(o, wl, xh, start=False, stop=stop, skip_group_check=shared)

            turn = [0, 0, 0]

            def slot_ready(s):
                turn[s] += 1
                pe.wait_ge(split[s], turn[s])

            def feature_major(s, outs, nk, m, xh, xl, k0_=0, step=None, ready=None):
                cols = widths[s][turn[s] - 1] // nk
                wh = whi[s][:, 0:nk * cols].rearrange("p (k n) -> p k n", k=nk)
                wl = wlo[s][:, 0:nk * cols].rearrange("p (k n) -> p k n", k=nk)
                for n, o in enumerate(outs):
                    c = slice(n * (step or m), n * (step or m) + m)
                    for j in range(nk):
                        k = j
                        if ready and n == 0:
                            ready(j)
                        mm = three(o, wh[:, k, c], wl[:, k, c], xh[:, k0_ + k, :], xl[:, k0_ + k, :], j == 0, j == nk - 1)
                mm.then_inc(used[s], 1)

            def first_two():
                def product(s, k, m):
                    c = slice(k * 2 * P + m * P, k * 2 * P + (m + 1) * P)
                    return three(ps[:, s, m * T:(m + 1) * T], whi[s][:, c], wlo[s][:, c], hhi[:, k, :], hlo[:, k, :],
                                 k == 0, k == KT - 1)

                for k in range(KT):
                    wait("h_ready")
                    for s in range(2):
                        product(s, k, 0)
                for s in range(2):
                    for k in range(KT):
                        mm = product(s, k, 1)
                    mm.then_inc(used[s], 1)

            def first_units(freed_by):
                for s in range(2):
                    slot_ready(s)
                    own(s)
                first_two()
                for s in range(2):
                    frees(s, freed_by[s])

            def bank_pair(b, m=P):
                return [ps[0:m, b, 0:T], ps[0:m, b, T:2 * T]]

            def one_tile(s, n, o, xh=hhi, xl=hlo):
                for k in range(KT):
                    c = slice(k * 2 * P + n * P, k * 2 * P + (n + 1) * P)
                    mm = three(o, whi[s][:, c], wlo[s][:, c], xh[:, k, :], xl[:, k, :], k == 0, k == KT - 1)
                return mm

            def linear(stage, u, freed_by=None, xh=hhi, xl=hlo, ready=None, b=None):
                s, b = u % 3, u % 2 if b is None else b
                slot_ready(s)
                own(b)
                feature_major(s, bank_pair(b), KT, P, xh, xl, ready=ready)
                if freed_by:
                    frees(b, freed_by)

            def token_major(stage, u, freed_by):
                s, b = u % 3, u % 2
                slot_ready(s)
                own(b)
                wh = whi[s][:, :].rearrange("p (k n) -> p k n", k=KT)
                wl = wlo[s][:, :].rearrange("p (k n) -> p k n", k=KT)
                for t in range(2):
                    tt = slice(t * P, t * P + P)
                    for k in range(KT):
                        o = ps[:, b, t * T:(t + 1) * T]
                        pe.matmul(o, hhi[:, k, tt], wh[:, k, :], start=(k == 0), stop=False)
                        pe.matmul(o, hhi[:, k, tt], wl[:, k, :], start=False, stop=False)
                        mm = pe.matmul(o, hlo[:, k, tt], wh[:, k, :], start=False, stop=(k == KT - 1))
                mm.then_inc(used[s], 1)
                frees(b, freed_by)

            wait("x_landed", 16)
            wait("const_landed", 16)
            for k in range(KT):
                for t in range(2):
                    mm = pe.transpose(ps[:, 2 + k // 2, (k % 2) * T + t * P:(k % 2) * T + (t + 1) * P],
                                      xin[:, t, k * P:(k + 1) * P], ident)
                if k % 2:
                    mm.then_inc(sem("xT_ready"), 1)
            wait("rows_landed", 16 * 17)
            pe.transpose(ps[:, 7, 0:NROWS], vrows[0:NROWS, :], ident[0:NROWS, 0:NROWS])
            for l in range(2):
                mm = pe.transpose(ps[:, 7, P + 72 * l:P + 72 * l + 72], brows[:, l, :], ident[0:72, 0:72])
            mm.then_inc(sem("vcols_ready"), 1)
            wait("lam_prod")
            pe.matmul(ps[:, 7, 400:402], ones, lam[:, 0:2], start=True, stop=True).then_inc(sem("lam_sum"), 1)

            norms = [0]

            def norm_sums():
                norms[0] += 1
                counts["x_ready"] = 4 * norms[0]
                own(7)
                for k in range(KT):
                    if k % 2 == 0:
                        wait("sq_ready")
                    mm = pe.matmul(ps[:, 7, 0:T], ones, hf[:, k, :], start=(k == 0), stop=(k == KT - 1))
                mm.then_inc(sem("stat_ready"), 1)
                frees(7, "stat_read")

            def ada_quarter(r, n, v_before=None):
                i = r % 2
                pe.wait_ge(ada_landed[i], (n + 1) * 16)
                if r == 0:
                    if not isinstance(v_before, int) or v_before > 0:
                        pe.wait_ge(sem("mod_ready"), v_before)
                for kk in range(2):
                    k = 2 * r + kk
                    for j in range(4):
                        mm = pe.matmul(ps[32 * j:32 * j + 32, 6, 0:T], cact[:, k:k + 1].to_broadcast([P, 32]),
                                       ada_raw[:, i, kk * D + j * T:kk * D + (j + 1) * T],
                                       start=(k == 0), stop=(k == KT - 1))
                mm.then_inc(ada_used[i], 1)

            def ada_turn(v):
                pe.wait_ge(sem("adarow_ready"), v + 1)
                for b in range(2):
                    mm = pe.transpose(ps[:, 6, T + b * P:T + (b + 1) * P], adarow[:, b * P:(b + 1) * P], ident)
                mm.then_inc(sem("adacol_ready"), 1)
                if isinstance(v, int):
                    freed[6] = (sem("mod_ready"), v + 1)

            def ada_half(v, half):
                for r in (2 * half, 2 * half + 1):
                    ada_quarter(r, 2 * v + half, v)

            def ada_vector(v):
                ada_half(v, 0)
                ada_half(v, 1)

            wait("cact_ready")
            ada_half(0, 0)
            pe.wait_ge(sem("lam_exp"), 1)
            norm_sums()
            ada_half(0, 1)
            ada_turn(0)
            ada_vector(1)
            ada_turn(1)

            def chunked(stage, layer_v=None, nv=5):
                b0, ch, count = first[stage], chunk0[stage], NCH

                def gate(c):
                    pe.wait_ge(split[0], c + b0[0] + 1)
                    if not (isinstance(c, int) and c + ch == 0):
                        pe.wait_ge(sem("silu_done"), c + ch)
                    halves(0, ps[:, 0, :])

                def up(c):
                    pe.wait_ge(split[1], c + b0[1] + 1)
                    if not (isinstance(c, int) and c + ch == 0):
                        pe.wait_ge(sem("hid_done"), c + ch)
                    halves(1, ps[:, 1, :])

                def halves(s, o):
                    wh = whi[s][:, :].rearrange("p (k n) -> p k n", k=KT)
                    wl = wlo[s][:, :].rearrange("p (k n) -> p k n", k=KT)
                    for m in range(2):
                        for k in range(KT):
                            mm = three(o[:, m * T:(m + 1) * T], wh[:, k, m * P:(m + 1) * P], wl[:, k, m * P:(m + 1) * P],
                                       hhi[:, k, :], hlo[:, k, :], k == 0, k == KT - 1)
                    mm.then_inc(used[s], 1)

                def down(c, parity, last=False):
                    if last:
                        wait("last_split")
                    else:
                        pe.wait_ge(split[2], c + b0[2] + 1)
                    pe.wait_ge(sem("hid_split"), c + ch + 1)
                    wh = whi[2][:, :].rearrange("p (k n) -> p k n", k=2)
                    wl = wlo[2][:, :].rearrange("p (k n) -> p k n", k=2)
                    for m in range(KT):
                        if last and m == 4:
                            pe.wait_ge(split[2], c + b0[2] + 1)
                        o = ps[:, 2 + m // 2, (m % 2) * T:(m % 2 + 1) * T]
                        for k in range(2):
                            mm = three(o, wh[:, k, m * P:(m + 1) * P], wl[:, k, m * P:(m + 1) * P],
                                       hidhi[parity][:, k, :], hidlo[parity][:, k, :], False, last and k == 1, shared=True)
                        if last and m in (1, 3, 5):
                            mm.then_inc(sem("out_pair"), 1)
                        if m == 3 and not last:
                            mm.then_inc(sem("down_half"), 1)
                    mm.then_inc(used[2], 1)

                for o in range(16):
                    pe.matmul(ps[:, 2 + o // 4, (o % 4) * P:(o % 4 + 1) * P], zeros[:, :], zeros[:, :], start=True, stop=True)
                pe.wait_ge(split[0], b0[0] + 1)
                if ch:
                    pe.wait_ge(sem("silu_done"), ch)
                pe.wait_ge(split[1], b0[1] + 1)
                if ch:
                    pe.wait_ge(sem("hid_done"), ch)
                first_two()

                def pair(i, v=None):
                    for half in range(2):
                        c = i * 2 + half
                        gate(c + 1)
                        up(c + 1)
                        if v is not None:
                            for r in (2 * half, 2 * half + 1):
                                ada_quarter(r, i * 2 + 2 * layer_v + r // 2, v)
                        down(c, half)
                    if v is not None:
                        ada_turn(v)

                pairs = (count - 1) // 2
                if layer_v is None:
                    nv = 0
                else:
                    with pe.Fori(0, nv) as i:
                        pair(i, i + layer_v)
                if nv < pairs:
                    with pe.Fori(nv, pairs) as i:
                        pair(i)
                down(count - 1, (count - 1) % 2, last=True)
                for s in range(3):
                    turn[s] = b0[s] + count

            wait("zeros_ready")
            chunked("ffn0", 2)

            def square_sums(weights, i, b, n=2 * T, start=True, stop=True, o=0):
                own(b)
                return pe.matmul(ps[:, b, o:o + n], weights, sq[:, i, 0:n], start=start, stop=stop)

            def qk_sums(i):
                wait("sq_done")
                square_sums(c_("halves"), i % 2, 7).then_inc(sem("stat_ready"), 1)
                frees(7, "stat_read")

            def scores(i, q, k):
                b = 2 + i % 4
                own(b)
                pe.matmul(ps[:, b, 0:P], q[:, 0:P], k[:, 0:P], start=True, stop=True)
                pe.matmul(ps[:, b, P:3 * P], q[:, P:2 * P], k[:, 0:2 * P], start=True, stop=True).then_inc(sem("scores_ready"), 1)
                frees(b, "exp_done")

            def probs_turn(e):
                own(7)
                wait("probs_ready")
                for j in range(3):
                    mm = pe.transpose(ps[:, 7, j * P:(j + 1) * P], exps[:, e, j * P:(j + 1) * P], ident)
                mm.then_inc(sem("turned"), 1)
                frees(7, "probsT_ready")

            def values(i, o, v):
                wait("probsT_ready")
                p = probsT[:, i % 2, :]
                pe.matmul(o, v[0], p[:, 0:T], start=True, stop=False)
                return pe.matmul(o[:, P:T], v[1], p[:, T:3 * P], start=False, stop=True)

            def diff_scores(h):
                for half in range(2):
                    rows = slice(64 * half, 64 * half + 64)
                    scores(2 * h + half, q0[rows, h, :], k0[rows, h, :])

            norm_sums()
            first_units(("sq_done", "sq_done"))
            for u in range(8):
                if 1 < u < 6:
                    linear("mix0", u, "sq_done" if u < 4 else "pool_in_ready")
                elif u < 2:
                    pass
                else:
                    token_major("mix0", u, "v_ready")
                if u in (2, 3):
                    ada_half(7, u - 2)
                if u == 4:
                    ada_turn(7)
                if u in (5, 7):
                    ada_half(8, (u - 5) // 2)
                if 1 <= u <= 4:
                    qk_sums(u - 1)
                if u == 6:
                    wait("qk_ready", 4)
                    diff_scores(0)

            wait("v_ready", 2)
            for h in range(5):
                if h < 3:
                    diff_scores(h + 1)
                if h == 0:
                    ada_turn(8)
                if h < 4:
                    probs_turn((2 * h) % 4)
                if h == 4:
                    own(2)
                    wait("o_read")
                    square_sums(ones, 0, 2).then_inc(sem("stat_ready"), 1)
                    frees(2, "stat_read")
                if h:
                    g = h - 1
                    if g % 2 == 0:
                        own(6)
                    mm = values(g, ps[:, 6, (g % 2) * T:(g % 2 + 1) * T], [v0[:, t, g * P:(g + 1) * P] for t in range(2)])
                    if g % 2:
                        mm.then_inc(sem("o_ready"), 1)
                        frees(6, "o_read")
                if h == 3:
                    wait("pooled")
                    wait("small_landed", 16 * 8)
                    for j in range(2):
                        own(j)
                        for g in range(2):
                            mm = pe.matmul(ps[:, j, g * T:(g + 1) * T], poolw[:, 2 * j + g, :], pool_d[:, 2 * j + g, :], start=True, stop=True)
                        mm.then_inc(sem("pool_out"), 1)
                        frees(j, "pool_read")

            def open_bank(b):
                own(b)
                for o in range(4):
                    pe.matmul(ps[:, b, o * P:(o + 1) * P], zeros[:, :], zeros[:, :], start=True, stop=True)

            def output_part(s, b, k, xh, xl, last=False):
                for m in range(2):
                    c = slice(k * 2 * P + m * P, k * 2 * P + (m + 1) * P)
                    mm = three(ps[:, b, m * T:(m + 1) * T], whi[s][:, c], wlo[s][:, c], xh[:, k, :], xl[:, k, :],
                               False, last, shared=True)
                if last:
                    mm.then_inc(used[s], 1)

            for s, b in ((2, 0), (0, 1)):
                open_bank(b)
                slot_ready(s)
                for k in range(4, 8):
                    if b == 0 and k % 2 == 0:
                        wait("mix_split")
                    output_part(s, b, k, mhi, mlo)
                if b == 0:
                    own(3)
                    wait("o_read")
                    square_sums(ones, 1, 3).then_inc(sem("stat_ready"), 1)
                    frees(3, "stat_read")
            for s, b in ((2, 0), (0, 1)):
                for k in range(4):
                    if b == 0 and k % 2 == 0:
                        wait("mix_split")
                    output_part(s, b, k, mhi, mlo, last=(k == 3))
                frees(b, "x_ready")
            for u in (10, 11):
                linear("mix0", u, "x_ready", mhi, mlo)

            def outputs(stage, u0, ready=None):
                for j in range(4):
                    linear(stage, u0 + j, "x_ready", mhi, mlo, ready if j == 0 else None)

            norm_sums()
            chunked("ffn1", 9)
            norm_sums()
            chunked("ffn2", 14, 4)

            norm_sums()
            first_units(("evacuated", "v_done"))
            for u in range(2, 12):
                linear("mix1", u, ("evacuated", "v_done", "y_done")[u % 3])
            outputs("mix1", 12, lambda k: wait("mix_split") if k % 2 == 0 else None)
            norm_sums()
            chunked("ffn3")

            norm_sums()

            def rope(r):
                b = (7, 6)[r % 2]
                own(b)
                wait("rope_in")
                if r == 0:
                    mm = pe.matmul(ps[64:96, b, 0:T], c_("swap_mla", slice(64, 96)), krope[64:96, :], start=True, stop=True)
                elif r < 5:
                    src = q0[:, 2 * (r - 1):2 * r, :] if r < 3 else k0[:, 2 * (r - 3):2 * (r - 2), :]
                    mm = pe.matmul(ps[:, b, :], c_("swap_moba"), src, start=True, stop=True)
                else:
                    mm = pe.matmul(ps[64:96, b, :], c_("swap_mla", slice(64, 96)), qA[64:96, 2 * (r - 5):2 * (r - 4), :],
                                   start=True, stop=True)
                mm.then_inc(sem("rope_swapped"), 1)
                frees(b, "rope_read")

            def latent_sums(j):
                wait("sq_done")
                b = 7 if j < 3 else 6
                if j in (0, 3):
                    own(b)
                for n in range(2):
                    mm = pe.matmul(ps[:, b, 0:T], ones, sq[:, j % 2, n * T:(n + 1) * T],
                                   start=(j in (0, 3) and n == 0), stop=(j >= 2 and n == 1))
                mm.then_inc(sem("sums_done"), 1)
                if j >= 2:
                    frees(b, "stat_read")

            first_units(("sq_done", "sq_done"))
            for u in range(4):
                if u > 1:
                    linear("blk2", u, "sq_done")
                if u:
                    latent_sums(u - 1)
            slot_ready(1)
            own(0)
            feature_major(1, [ps[0:MLA_Q, 0, 0:T]], KT, MLA_Q, hhi, hlo)
            frees(0, "rope_in")
            latent_sums(3)
            linear("blk2", 5, "rope_in")
            rope(0)
            for u in range(6, 9):
                linear("blk2", u, "rope_in")
                rope(u - 5)
            token_major("blk2", 9, "v_ready")
            rope(4)
            token_major("blk2", 10, "v_ready")
            slot_ready(2)
            wait("latent_split", 2)
            wh = whi[2][:, :].rearrange("p (k h n) -> p k h n", k=2, h=MLA_H)
            wl = wlo[2][:, :].rearrange("p (k h n) -> p k h n", k=2, h=MLA_H)
            for h in range(MLA_H):
                for k in range(2):
                    three(ps[:, 2 + h // 2, (h % 2) * T:(h % 2 + 1) * T], wh[:, k, h, :], wl[:, k, h, :],
                          mhi[:, 6 + k, :], mlo[:, 6 + k, :], k == 0, k == 1)
            for t in range(2):
                own(t)
                tt = slice(t * P, t * P + P)
                for k in range(2):
                    pe.matmul(ps[:, t, :], mhi[:, 6 + k, tt], wh[:, k, :, 64:], start=(k == 0), stop=False)
                    pe.matmul(ps[:, t, :], mhi[:, 6 + k, tt], wl[:, k, :, 64:], start=False, stop=False)
                    mm = pe.matmul(ps[:, t, :], mlo[:, 6 + k, tt], wh[:, k, :, 64:], start=False, stop=(k == 1))
                frees(t, "ukv_v_read")
            mm.then_inc(used[2], 1)
            for u in UQ_UNITS:
                s, b = u % 3, u % 2
                slot_ready(s)
                own(b)
                feature_major(s, bank_pair(b, MLA_Q), QL // P, MLA_Q, mhi, mlo)
                frees(b, "rope_in")
                if u > UQ_UNITS[0]:
                    rope(5 + u - UQ_UNITS[0] - 1)
            rope(8)
            wait("ukv_k_read", 1)
            wait("v_ready", 2)
            wait("roped", 5)

            def head(i):
                if i < MOBA_H:
                    r = slice(64 * (i % 2), 64 * (i % 2) + 64)
                    scores(i, q0[r, i // 2, :], k0[r, i // 2, :])
                else:
                    if i == MOBA_H:
                        wait("roped", 4)
                    scores(i, qA[0:MLA_Q, i - 8, :], kA[0:MLA_Q, i - 8, :])

            head(0)
            head(1)
            for i in range(17):
                if i + 2 < 16:
                    head(i + 2)
                if i < 16:
                    u, n = 16 + i // 2, i % 2
                    if n == 0:
                        slot_ready(u % 3)
                        own(u % 2)
                    mm = one_tile(u % 3, n, bank_pair(u % 2)[n])
                    if n == 1:
                        mm.then_inc(used[u % 3], 1)
                        frees(u % 2, "evacuated")
                    probs_turn(i % 4)
                if i:
                    h = i - 1
                    if h % 2 == 0:
                        own(6)
                    r = slice(64 * (h % 2), 64 * (h % 2) + 64)
                    v, c = (v0, h) if h < MOBA_H else (vA, h - 8)
                    mm = values(h, ps[r, 6, 0:T], [v[:, t, c * 64:(c + 1) * 64] for t in range(2)])
                    mm.then_inc(sem("o_ready"), 1)
                    if h % 2:
                        frees(6, "o_split")
            wait("o_split", 8)
            for j in range(2):
                for which in range(2):
                    u = 24 + 2 * j + which
                    s = u % 3
                    b = (2, 4, 0, 6)[2 * j + which]
                    slot_ready(s)
                    own(b)
                    own(b + 1)
                    feature_major(s, bank_pair(b) + bank_pair(b + 1), 4, P, mhi, mlo, k0_=4 * which)
                if j == 0:
                    for b in (2, 3):
                        freed[b] = (sem("mixed"), 1)
            for u in (28, 29):
                open_bank(2 + u % 2)
                slot_ready(u % 3)
            for half in range(2):
                wait("mixed_split")
                for u in (28, 29):
                    for k in range(4 * half, 4 * half + 4):
                        output_part(u % 3, 2 + u % 2, k, hhi, hlo, last=(k == KT - 1))
                    if half:
                        frees(2 + u % 2, "x_ready")
            for u in (30, 31):
                linear("blk2", u, "x_ready", b=2 + u % 2)

            norm_sums()
            own(7)
            pe.matmul(ps[0:NG + NE, 7, 0:T], brout[:, :], ones[0:1, 0:1].to_broadcast([1, T]), start=True, stop=False)
            for k in range(KT):
                pe.wait_ge(sem("t_ready"), 7 * KT + k + 1)
                for t in range(2):
                    mm = pe.transpose(ps[:, 2 * t + k // 4, (k % 4) * P:(k % 4 + 1) * P], hf[:, k, t * P:(t + 1) * P], ident)
                if k % 4 == 3:
                    mm.then_inc(sem("h_turned"), 1)
                mm = pe.matmul(ps[0:NG + NE, 7, 0:T], wrout[:, k, :], hf[:, k, :], start=False, stop=(k == KT - 1))
            mm.then_inc(sem("logits_ready"), 1)
            wait("logits_copied")
            for t in range(2):
                mm = pe.transpose(ps[:, 6, t * 64:t * 64 + NG + NE], adarow[0:NG + NE, t * P:(t + 1) * P], ident[0:NG + NE, 0:NG + NE])
            mm.then_inc(sem("logits_turned"), 1)
            wait("router_max")
            wait("late_landed", 16)
            hot = rt[:, 2:2 + 2 * NG].rearrange("p (t n) -> p t n", t=2)
            pe.matmul(ps[:, 4, 0:NG], c_("before"), hot[:, 0, :], start=True, stop=True)
            pe.matmul(ps[:, 4, NG:2 * NG], ones, hot[:, 0, :], start=True, stop=False)
            pe.matmul(ps[:, 4, NG:2 * NG], c_("before"), hot[:, 1, :], start=False, stop=True)
            pe.matmul(ps[:, 4, 2 * NG:3 * NG], ones, hot[:, 0, :], start=True, stop=False)
            pe.matmul(ps[:, 4, 2 * NG:3 * NG], ones, hot[:, 1, :], start=False, stop=True).then_inc(sem("ranked"), 1)
            wait("picked")
            wait("htok_split", 2)
            for k in range(KT):
                n = 0
                for t in range(2):
                    for part in (htok_hi, htok_lo):
                        mm = pe.matmul(ps[:, k, :], part[:, t, k * P:(k + 1) * P],
                                       pick[:, t, 0:NG, :], start=(n == 0), stop=(n == 3))
                        n += 1
                mm.then_inc(sem("gathered"), 1)

            def block_h(g):
                hi, lo = (mhi, mlo) if g in (2, 3) else (hhi, hlo)
                sl = slice((g % 2) * P, (g % 2) * P + P)
                return hi[:, :, sl], lo[:, :, sl]

            def into_hidden(s, e, p, g):
                pe.wait_ge(split[s], e + (b_moe[s] + 1))
                if s == 0 and (not isinstance(e, int) or e >= 2):
                    pe.wait_ge(sem("moe_hidden"), e - 1)
                hi, lo = block_h(g)
                o = ps[:, p, s * CH:(s + 1) * CH]
                for k in range(KT):
                    if isinstance(e, int) and e == 0 and s == 0:
                        wait("gathered_split")
                    c = slice(k * CH, (k + 1) * CH)
                    pe.matmul(o, hi[:, k, :], whi[s][:, c], start=(k == 0), stop=False)
                    pe.matmul(o, hi[:, k, :], wlo[s][:, c], start=False, stop=False)
                    mm = pe.matmul(o, lo[:, k, :], whi[s][:, c], start=False, stop=(k == KT - 1))
                mm.then_inc(used[s], 1)

            def hidden_turn(e, p):
                pe.wait_ge(sem("moe_hidden"), e + 1)
                if not isinstance(e, int) or e >= 1:
                    pe.wait_ge(sem("moe_split"), e)
                for k in range(2):
                    mm = pe.transpose(ps[:, 2, p * T + k * P:p * T + (k + 1) * P], hid2[:, p, k * P:(k + 1) * P], ident)
                mm.then_inc(sem("moe_turned"), 1)

            def out_of_hidden(e, p, g, j):
                pe.wait_ge(split[2], e + (b_moe[2] + 1))
                pe.wait_ge(sem("moe_split"), e + 1)
                if j == 0 and g:
                    pe.wait_ge(sem("y_split"), g)
                for n in range(2):
                    for k in range(2):
                        hi, lo = (x[p][:, 0, k * P:(k + 1) * P] for x in (hidhi, hidlo))
                        c = slice(k * D + n * 512, k * D + (n + 1) * 512)
                        o = ps[:, 6 + n, :]
                        pe.matmul(o, hi, whi[2][:, c], start=(j == 0 and k == 0), stop=False, skip_group_check=True)
                        pe.matmul(o, hi, wlo[2][:, c], start=False, stop=False, skip_group_check=True)
                        mm = pe.matmul(o, lo, whi[2][:, c], start=False, stop=(j == EG - 1 and k == 1), skip_group_check=True)
                mm.then_inc(used[2], 1)

            def scatter(g, pairs=range(4)):
                pe.wait_ge(sem("y_split"), g + 1)
                for pr in pairs:
                    q = 4 * g + pr
                    if q >= 3:
                        pe.wait_ge(sem("x_added"), q - 2)
                    for f in range(2):
                        c = slice((2 * pr + f) * P, (2 * pr + f + 1) * P)
                        o = ps[:, 3 + q % 3, f * T:(f + 1) * T]
                        pe.matmul(o, y_hi[:, c], pickT[:, g, :], start=True, stop=False)
                        mm = pe.matmul(o, y_lo[:, c], pickT[:, g, :], start=False, stop=True)
                    mm.then_inc(sem("scattered"), 1)

            def expert_block(g, ends):
                def step(e, p, j):
                    more = follows(j, ends, 1)
                    g1 = g + 1 if j == EG - 1 else g
                    if more:
                        into_hidden(0, e + 1, 1 - p, g1)
                    hidden_turn(e, p)
                    if more:
                        into_hidden(1, e + 1, 1 - p, g1)
                    if j in BESIDE and 0 < g < NG:
                        scatter(g - 1, BESIDE[j])
                    out_of_hidden(e, p, g, j)

                experts_of(pe, g, step, ends)
                if ends:
                    scatter(g)

            into_hidden(0, 0, 0, 0)
            into_hidden(1, 0, 0, 0)
            wait("slot_weights")
            two = rt[:, 104:104 + 2 * EG].rearrange("p (t n) -> p t n", t=2)
            for b in range(NG + 1):
                for t in range(2):
                    mm = pe.matmul(ps[:, 7, b * EG:(b + 1) * EG], pick[:, t, b, :].bitcast(F32), two[:, t, :], start=(t == 0), stop=(t == 1))
            mm.then_inc(sem("slot_weights_out"), 1)
            for b in range(NG + 1):
                for t in range(2):
                    bank, o = (3, T) if b == NG else (4 + b // 2, (b % 2) * T)
                    mm = pe.transpose(ps[:, bank, o + t * P:o + (t + 1) * P], pick[:, t, b, :].bitcast(F32), ident)
            mm.then_inc(sem("pick_turned"), 1)
            for g in range(NG):
                if g == 1:
                    wait("pickT_ready")
                expert_block(g, g == NG - 1)
            pe.wait_ge(sem("overflow_known"), 1)
            has_fifth = pe.value_load(overflow[0:1, 0:1], min_val=0, max_val=1)
            with pe.If(has_fifth > 0):
                pe.wait_ge(sem("moe_hidden"), NE)
                for k in range(KT):
                    n = 0
                    for t in range(2):
                        for part in (htok_hi, htok_lo):
                            mm = pe.matmul(ps[:, k // 4, (k % 4) * P:(k % 4 + 1) * P], part[:, t, k * P:(k + 1) * P],
                                           pick[:, t, NG, :], start=(n == 0), stop=(n == 3))
                            n += 1
                    if k % 4 == 3:
                        mm.then_inc(sem("fifth_gathered"), 1)
                pe.wait_ge(sem("fifth_split"), 2)
                into_hidden(0, NE, 0, NG)
                into_hidden(1, NE, 0, NG)
                expert_block(NG, True)

            norm_sums()
            for k in range(KT):
                pe.wait_ge(sem("t_ready"), 8 * KT + k + 1)
                for t in range(2):
                    b = 2 * t + k // 4
                    mm = pe.transpose(ps[:, b, (k % 4) * P:(k % 4 + 1) * P], hf[:, k, t * P:(t + 1) * P], ident)
            mm.then_inc(sem("out_turned"), 1)

        @block.scalar
        def _(act):
            wait = Tally(act)
            turn = [0, 0, 0]

            def split_high(s, n, width=UW):
                act.wait_ge(landed[s], (n + 1) * 16)
                if not isinstance(n, int) or n > 0:
                    act.wait_ge(used[s], n)
                act.activation(whi[s][:, 0:width], raw[s][:, 0:width], ACT.Copy).then_inc(high[s], 1)

            def refill(s):
                n = turn[s]
                if n < len(widths[s]):
                    split_high(s, n, widths[s][n])
                    turn[s] += 1

            def copy(o, i, scale=1.0):
                return act.activation(o, i, ACT.Copy, scale=scale)

            def norm(slots=()):
                if stats[0]:
                    act.wait_ge(sem("table_in"), stats[0])
                stats[0] += 1
                act.activation(lam[:, 6:7], eps, ACT.Sqrt).then_inc(sem("table_in"), 1)
                for pr in range(4):
                    if pr < len(slots):
                        refill(slots[pr])
                    wait("x_ready")
                    act.activation(hf[:, 2 * pr:2 * pr + 2, :], xT[:, 2 * pr:2 * pr + 2, :], ACT.Square).then_inc(sem("sq_ready"), 1)
                roots(D, T)

            def roots(width, n, b=7, o=0):
                wait("stat_ready")
                act.activation(root[:, o:o + n], ps[:, b, 0:n], ACT.Sqrt, bias=eps[:, 0:1], scale=1.0 / width).then_inc(sem("stat_read"), 1)

            def norm_high(shift):
                for k in range(KT):
                    wait("t_ready")
                    if shift is None:
                        copy(hhi[:, k, :], hf[:, k, :]).then_inc(sem("h_high"), 1)
                    else:
                        act.activation(hhi[:, k, :], hf[:, k, :], ACT.Identity, bias=shift[:, k:k + 1]).then_inc(sem("h_high"), 1)

            eps = lam[:, 7:8]
            stats = [0]
            wait("vcols_done")
            act.activation(cact[:, :], col("c", 0, KT), ACT.Silu).then_inc(sem("cact_ready"), 1)
            wait("lam_sum")
            act.activation(lam[:, 2:4], ps[:, 7, 400:402], ACT.Exp).then_inc(sem("lam_exp"), 1)
            norm()
            refill(0)
            refill(1)
            norm_high(mod(0, 0))
            refill(2)

            def chunked(stage):
                b0, ch, count = first[stage], chunk0[stage], NCH

                def gate(c):
                    act.wait_ge(used[0], c + b0[0] + 1)
                    if not (isinstance(c, int) and c + ch == 0):
                        act.wait_ge(sem("hid_done"), c + ch)
                    act.activation(silu[:, :], ps[:, 0, :], ACT.Silu).then_inc(sem("silu_done"), 1)

                def high_hidden(c, parity):
                    act.wait_ge(sem("hid_done"), c + ch + 1)
                    if not (isinstance(c, int) and c < 2):
                        act.wait_ge(used[2], c + b0[2] - 1)
                    act.activation(hidhi[parity][:, :, :], hid[:, :].rearrange("p (k t) -> p k t", k=2), ACT.Copy).then_inc(sem("hid_high"), 1)

                def last_halves():
                    n = b0[2] + count - 1
                    act.wait_ge(landed[2], (n + 1) * 16)
                    act.wait_ge(sem("down_half"), ch + count - 1 - CHUNKED.index(stage))
                    act.activation(columns(whi[2], 0), columns(raw[2], 0), ACT.Copy).then_inc(sem("last_high"), 1)
                    act.wait_ge(used[2], n)
                    act.activation(columns(whi[2], 1), columns(raw[2], 1), ACT.Copy).then_inc(high[2], 1)

                def chunk(c, parity, down=True, last=False):
                    if down:
                        gate(c)
                    split_high(0, c + b0[0] + 1)
                    if not down:
                        gate(c)
                    high_hidden(c, parity)
                    split_high(1, c + b0[1] + 1)
                    if last:
                        last_halves()
                    elif down:
                        split_high(2, c + b0[2])

                chunk(0, 0, down=False)
                with act.Fori(0, (count - 2) // 2) as i:
                    for half in range(2):
                        chunk(i * 2 + 1 + half, (1 + half) % 2)
                for c in range((count - 2) // 2 * 2 + 1, count):
                    chunk(c, c % 2, last=(c == count - 1))
                for s in range(3):
                    turn[s] = b0[s] + count + (s < 2)

            chunked("ffn0")
            norm()
            norm_high(mod(0, 3))
            refill(2)

            def pair(b, rows=P):
                return ps[0:rows, b, :].rearrange("p (n t) -> p n t", n=2)

            def exps_of(i):
                wait("negmax_ready")
                e, b = i % 4, 2 + i % 4
                act.activation(exps[:, e, 0:P], ps[:, b, 0:P], ACT.Exp, bias=negmax[:, e, 0:1], accum_out=zsum[:, e, 0:1])
                act.activation(exps[:, e, P:3 * P], ps[:, b, P:3 * P], ACT.Exp, bias=negmax[:, e, 1:2],
                               accum_out=zsum[:, e, 1:2]).then_inc(sem("exp_done"), 1)

            def probsT_of(i):
                wait("turned")
                copy(probsT[:, i % 2, :], ps[:, 7, 0:3 * P]).then_inc(sem("probsT_ready"), 1)

            def o_out(j):
                wait("o_ready")
                copy(hf[:, 2 * j:2 * j + 2, :], pair(6))
                act.activation(sq[:, j, :], ps[:, 6, :], ACT.Square).then_inc(sem("o_read"), 1)

            for u in range(8):
                s, b = u % 3, u % 2
                if u == 7:
                    exps_of(0)
                    exps_of(1)
                act.wait_ge(used[s], first["mix0"][s] + u // 3 + 1)
                if u < 4:
                    dst = (q0 if u < 2 else k0)[:, 2 * (u % 2):2 * (u % 2) + 2, :]
                    copy(dst, pair(b))
                    act.activation(sq[:, u % 2, :], ps[:, b, :], ACT.Square).then_inc(sem("sq_done"), 1)
                elif u < 6:
                    copy(pool_in[:, 2 * (u - 4):2 * (u - 4) + 2, 16:PADT], pair(b)).then_inc(sem("pool_in_ready"), 1)
                else:
                    copy(v0[:, :, 256 * (u - 6):256 * (u - 5)], pair(b)).then_inc(sem("v_ready"), 1)
                refill(s)
                if 1 <= u <= 4:
                    if u > 1:
                        wait("qk_ready")
                    roots(64, 2 * T)

            for h in range(4):
                if h < 3:
                    exps_of(2 * h + 2)
                    exps_of(2 * h + 3)
                probsT_of(h)
                if h == 2:
                    o_out(0)
            for j in range(2):
                wait("pool_out")
                for g in range(2):
                    k = 2 * j + g
                    act.activation(hf[:, 4 + k, :], ps[:, j, g * T:(g + 1) * T], ACT.Copy,
                                   scale=col("pool_scale", k)).then_inc(sem("pool_read_half" if g == 0 else "pool_read"), 1)
            for j in range(2):
                act.wait_ge(sem("pool_read_half"), j + 1)
                act.wait_ge(sem("pool_read"), j + 1)
                copy(mhi[:, 4 + 2 * j:6 + 2 * j, :], hf[:, 4 + 2 * j:6 + 2 * j, :]).then_inc(sem("mix_high"), 1)
            o_out(1)
            roots(P, 2 * T, b=2)
            wait("o_normed")
            copy(mhi[:, 0:2, :], hf[:, 0:2, :]).then_inc(sem("mix_high"), 1)
            roots(P, 2 * T, b=3)
            wait("o_normed")
            copy(mhi[:, 2:4, :], hf[:, 2:4, :]).then_inc(sem("mix_high"), 1)
            norm((2, 0, 1))
            norm_high(mod(0, 6))
            refill(2)
            chunked("ffn1")
            norm()
            norm_high(mod(1, 0))
            refill(2)
            chunked("ffn2")

            norm()
            norm_high(mod(1, 3))
            refill(2)
            for u in range(12):
                s, b = u % 3, u % 2
                act.wait_ge(used[s], first["mix1"][s] + u // 3 + 1)
                if u % 3 == 0:
                    if u:
                        wait("v_done")
                    copy(cgate, ps[:, b, :]).then_inc(sem("evacuated"), 1)
                refill(s)
                if u % 3 == 2:
                    j = u // 3
                    wait("y_done")
                    copy(mhi[:, 2 * j:2 * j + 2, :], hf[:, 2 * j:2 * j + 2, :]).then_inc(sem("mix_high"), 1)
            norm((0, 1, 2))
            refill(0)
            norm_high(mod(1, 6))
            chunked("ffn3")

            norm()
            norm_high(None)
            refill(2)

            def latent_high(j):
                wait("latent_normed")
                sl = slice(0, 6) if j == 0 else slice(6, 8)
                copy(mhi[:, sl, :], hf[:, sl, :]).then_inc(sem("latent_high"), 1)

            for u in range(11):
                s, b = u % 3, u % 2
                act.wait_ge(used[s], first["blk2"][s] + u // 3 + 1)
                if u < 4:
                    if u >= 2:
                        wait("sums_done")
                    copy(hf[:, 2 * u:2 * u + 2, :], pair(b))
                    act.activation(sq[:, u % 2, :], ps[:, b, :], ACT.Square).then_inc(sem("sq_done"), 1)
                elif u == KR_UNIT:
                    copy(krope[64:96, :], ps[64:96, b, 0:T]).then_inc(sem("rope_in"), 1)
                elif u < 9:
                    j = u - 5
                    dst = (q0 if j < 2 else k0)[:, 2 * (j % 2):2 * (j % 2) + 2, :]
                    copy(dst, pair(b), MOBA_HD ** -0.5 if j < 2 else 1.0).then_inc(sem("rope_in"), 1)
                else:
                    copy(v0[:, :, 256 * (u - 9):256 * (u - 8)], pair(b)).then_inc(sem("v_ready"), 1)
                refill(s)
                if u == 4:
                    wait("sums_done")
                    act.activation(root[:, 0:T], ps[:, 7, 0:T], ACT.Sqrt, bias=eps, scale=1.0 / QL).then_inc(sem("stat_read"), 1)
                if u == 5:
                    wait("sums_done")
                    act.activation(root[:, T:2 * T], ps[:, 6, 0:T], ACT.Sqrt, bias=eps, scale=1.0 / KVL).then_inc(sem("stat_read"), 1)
                if u == 7:
                    latent_high(0)
                    latent_high(1)
            act.wait_ge(used[2], first["blk2"][2] + 11 // 3 + 1)
            for j in range(4):
                ins = copy(kA[0:64, 2 * j:2 * j + 2, :], pair(2 + j, 64))
            ins.then_inc(sem("ukv_k_read"), 1)
            for t in range(2):
                copy(vA[:, t, :], ps[:, t, :]).then_inc(sem("ukv_v_read"), 1)
            refill(2)
            for u in UQ_UNITS:
                s, b = u % 3, u % 2
                act.wait_ge(used[s], first["blk2"][s] + u // 3 + 1)
                i = u - UQ_UNITS[0]
                copy(qA[0:MLA_Q, 2 * i:2 * i + 2, :], pair(b, MLA_Q), MLA_Q ** -0.5).then_inc(sem("rope_in"), 1)
                refill(s)

            exps_of(0)
            exps_of(1)
            for i in range(17):
                if i + 2 < 16:
                    exps_of(i + 2)
                if i % 2:
                    g = i // 2
                    u = 16 + g
                    act.wait_ge(used[u % 3], first["blk2"][u % 3] + u // 3 + 1)
                    copy(gates[:, g // 4, 2 * (g % 4):2 * (g % 4) + 2, :], pair(u % 2)).then_inc(sem("evacuated"), 1)
                    refill(u % 3)
                if i < 16:
                    probsT_of(i)
                if i and i % 2 == 0:
                    j = i // 2 - 1
                    wait("o_ready", 2)
                    tile_ = 4 + j if j < 4 else j - 4
                    copy(mhi[:, tile_, :], ps[:, 6, 0:T]).then_inc(sem("o_high"), 1)
            for j in range(2):
                act.wait_ge(sem("evacuated"), 4 + 8)
                g = gates[:, :, 4 * j:4 * j + 4, :]
                act.activation(g, g, ACT.Sigmoid).then_inc(sem("gates_ready"), 1)
            for j in range(2):
                for which in range(2 - j):
                    refill((24 + 2 * j + which) % 3)
                wait("mixed")
                copy(hhi[:, 4 * j:4 * j + 4, :], hf[:, 4 * j:4 * j + 4, :]).then_inc(sem("mixed_high"), 1)
            refill(27 % 3)
            norm((1, 2, 0))
            refill(1)
            for j in range(2):
                wait("h_turned")
                for t in range(2):
                    copy(htok_hi[:, t, j * 512:(j + 1) * 512], ps[:, 2 * t + j, :]).then_inc(sem("htok_high"), 1)
            wait("router_max")
            act.activation(rt[:, 64:72], rt[:, 56:64], ACT.Exp).then_inc(sem("router_exp"), 1)
            def expert_high(s, e, p):
                if p:
                    act.wait_ge(landed_odd[s], e * 8 + 8)
                else:
                    act.wait_ge(landed[s], e * 8 + (b_moe[s] + 1) * 16)
                act.wait_ge(used[s], e + b_moe[s])
                copy(whi[s][:, :], weights_of(s, p)).then_inc(high[s], 1)

            for k in range(KT):
                wait("gathered")
                copy(hhi[:, k, :], ps[:, k, 0:T])
                copy(mhi[:, k, :], ps[:, k, T:2 * T]).then_inc(sem("gathered_high"), 1)
            expert_high(0, 1, 1)
            wait("router_two")
            act.activation(rt[:, 130:132], rt[:, 128:130], ACT.Exp).then_inc(sem("router_exp"), 1)

            def expert_silu(e, p):
                act.wait_ge(used[1], e + (b_moe[1] + 1))
                if not isinstance(e, int) or e >= 2:
                    act.wait_ge(sem("moe_hidden"), e - 1)
                act.activation(silu2[:, p, :], ps[:, p, 0:CH], ACT.Silu).then_inc(sem("moe_silu"), 1)

            def hidden_high(e, p):
                act.wait_ge(sem("moe_turned"), e + 1)
                if not isinstance(e, int) or e >= 2:
                    act.wait_ge(used[2], e + (b_moe[2] - 1))
                copy(hidhi[p][:, 0, :], ps[:, 2, p * T:(p + 1) * T]).then_inc(sem("moe_high"), 1)

            def output_high(g):
                act.wait_ge(used[2], b_moe[2] + (g + 1) * EG)
                if g:
                    act.wait_ge(sem("scattered"), 4 * g)
                copy(y_hi[:, :].rearrange("p (b n) -> p b n", b=2), ps[:, 6:8, :]).then_inc(sem("y_high"), 1)

            def expert_block(g, ends):
                def step(e, p, j):
                    hidden_high(e, p)
                    if follows(j, ends, 2):
                        expert_high(0, e + 2, p)
                    if follows(j, ends, 1):
                        expert_silu(e + 1, 1 - p)
                    if follows(j, ends, 2):
                        expert_high(1, e + 2, p)
                    if j == EG - 1:
                        output_high(g)
                    if follows(j, ends, 1):
                        expert_high(2, e + 1, 1 - p)

                experts_of(act, g, step, ends)

            expert_silu(0, 0)
            wait("pick_turned")
            copy(pickT[:, 0:NG, :].rearrange("p (i b) t -> p i (b t)", i=2), ps[:, 4:6, :])
            copy(pickT[:, NG, :], ps[:, 3, T:2 * T]).then_inc(sem("pickT_ready"), 1)
            expert_high(1, 1, 1)
            for g in range(NG):
                expert_block(g, g == NG - 1)
            act.wait_ge(sem("overflow_known"), 1)
            has_fifth = act.value_load(overflow[0:1, 0:1], min_val=0, max_val=1)
            with act.If(has_fifth > 0):
                for j in range(2):
                    act.wait_ge(sem("fifth_gathered"), j + 1)
                    copy(hhi[:, 4 * j:4 * j + 4, 0:P], ps[:, j, :].rearrange("p (k n) -> p k n", k=4)).then_inc(sem("fifth_high"), 1)
                for s in range(3):
                    expert_high(s, NE, 0)
                expert_high(0, NE + 1, 1)
                expert_silu(NE, 0)
                expert_high(1, NE + 1, 1)
                expert_block(NG, True)
            norm()
            wait("out_turned")
            for t in range(2):
                ins = copy(xout[:, t, :].rearrange("p (b n) -> p b n", b=2), ps[:, 2 * t:2 * t + 2, :]).then_inc(sem("out_ready"), 1)

        @block.vector
        def _(dve):
            wait = Tally(dve)
            turn = [0, 0, 0]
            n_self = [0]

            def link(ins):
                n_self[0] += 1
                ins.then_inc(sem("dve_self"), 1)
                dve.wait_ge(sem("dve_self"), n_self[0])

            def split_low(s, n, width=UW):
                dve.wait_ge(high[s], n + 1)
                dve.tensor_tensor(wlo[s][:, 0:width], raw[s][:, 0:width], whi[s][:, 0:width].bitcast(F32),
                                  ALU.subtract).then_inc(split[s], 1)

            def refill(s):
                n = turn[s]
                if n < len(widths[s]):
                    split_low(s, n, widths[s][n])
                    turn[s] += 1

            def stt(o, i0, s, i1, op0=ALU.mult, op1=ALU.add):
                return dve.scalar_tensor_tensor(out=o, in0=i0, scalar=s, in1=i1, op0=op0, op1=op1)

            link(dve.memset(lam[:, :], EPS))
            dve.memset(vrows[:, :], 0.0).then_inc(sem("rows_cleared"), 1)
            for pr in range(4):
                wait("xT_ready")
                dve.tensor_copy(xT[:, 2 * pr:2 * pr + 2, :], ps[:, 2 + pr, :].rearrange("p (n t) -> p n t", n=2)).then_inc(sem("x_ready"), 1)
            wait("vcols_ready")
            link(dve.tensor_copy(bada[:, :], ps[:, 7, P:P + 144]))
            link(dve.tensor_copy(vcols[:, :], ps[:, 7, 0:NROWS]))
            link(dve.tensor_scalar(col("subln"), col("subln"), 1.0 - LAM_INIT, None, ALU.mult))
            dve.tensor_scalar(col("lam", 0), col("lam", 0), 1.0, None, ALU.mult).then_inc(sem("vcols_done"), 1)
            dve.wait_ge(sem("vcols_done"), 1)
            link(dve.tensor_tensor(lam[:, 0:1], col("lam", 0), col("lam", 1), ALU.mult))
            dve.tensor_tensor(lam[:, 1:2], col("lam", 2), col("lam", 3), ALU.mult).then_inc(sem("lam_prod"), 1)
            wait("lam_exp")
            link(dve.tensor_tensor(lam[:, 4:5], lam[:, 3:4], lam[:, 2:3], ALU.subtract))
            link(dve.tensor_scalar(lam[:, 4:5], lam[:, 4:5], LAM_INIT, None, ALU.subtract))

            def ada_rows(v):
                dve.wait_ge(ada_used[1], v * 2 + 2)
                dve.tensor_copy(adarow[:, :], ps[:, 6, 0:T]).then_inc(sem("adarow_ready"), 1)

            def ada_mod(v):
                dve.wait_ge(sem("adacol_ready"), v + 1)
                src = ps[:, 6, T:2 * T].rearrange("p (b j r) -> p j b r", b=2, j=4)[:, :, :, 0]
                sl = bass.ds(v * KT, KT) if not isinstance(v, int) else slice(v * KT, (v + 1) * KT)
                dve.tensor_tensor(modv[:, sl].rearrange("p (j b) -> p j b", j=4), src,
                                  bada[:, sl].rearrange("p (j b) -> p j b", j=4), ALU.add).then_inc(sem("mod_ready"), 1)

            def root_inverse():
                wait("stat_read")
                link(dve.reciprocal(rstd[:, 0:T], root[:, 0:T]))

            root_inverse()
            refill(0)
            ada_rows(0)
            ada_mod(0)
            refill(1)
            ada_rows(1)
            ada_mod(1)

            def norm(gain, shift, scale=None, final=False, vectors=0, inverted=False, slot=None):
                if scale is not None:
                    dve.wait_ge(sem("mod_ready"), vectors)
                    link(stt(gmod[:, :], scale, 1.0, gain, ALU.add, ALU.mult))
                    gain = gmod
                if not inverted:
                    root_inverse()
                if slot is not None:
                    refill(slot)

                def scaled(k):
                    stt(hf[:, k, :], xT[:, k, :], gain[:, k:k + 1], rstd[:, 0:T], ALU.mult, ALU.mult).then_inc(sem("t_ready"), 1)

                def low(k):
                    wait("h_high")
                    if shift is None:
                        ins = dve.tensor_tensor(hlo[:, k, :], hf[:, k, :], hhi[:, k, :].bitcast(F32), ALU.subtract)
                    else:
                        ins = stt(hlo[:, k, :], hf[:, k, :], shift[:, k:k + 1], hhi[:, k, :].bitcast(F32), ALU.add, ALU.subtract)
                    ins.then_inc(sem("h_ready"), 1)

                for k in range(KT):
                    scaled(k)
                    if k and not final:
                        low(k - 1)
                if not final:
                    low(KT - 1)

            def ng(l, i):
                return col("norm_g", (l * 3 + i) * KT, KT)

            norm(ng(0, 0), mod(0, 0), mod(0, 1), vectors=2, inverted=True)
            refill(2)

            def chunked(stage, vec=None, nv=5):
                b0, ch, count = first[stage], chunk0[stage], NCH

                def hidden(c, parity):
                    dve.wait_ge(sem("silu_done"), c + ch + 1)
                    dve.wait_ge(used[1], c + b0[1] + 1)
                    dve.tensor_tensor(hid[:, :], silu[:, :], ps[:, 1, :], ALU.mult).then_inc(sem("hid_done"), 1)

                def hidden_low(c, parity):
                    dve.wait_ge(sem("hid_high"), c + ch + 1)
                    dve.tensor_tensor(hidlo[parity][:, :, :], hid[:, :].rearrange("p (k t) -> p k t", k=2),
                                      hidhi[parity][:, :, :].bitcast(F32), ALU.subtract).then_inc(sem("hid_split"), 1)

                def last_halves():
                    wait("last_high")
                    dve.tensor_tensor(columns(wlo[2], 0), columns(raw[2], 0), columns(whi[2], 0).bitcast(F32),
                                      ALU.subtract).then_inc(sem("last_split"), 1)
                    dve.wait_ge(high[2], b0[2] + count)
                    dve.tensor_tensor(columns(wlo[2], 1), columns(raw[2], 1), columns(whi[2], 1).bitcast(F32),
                                      ALU.subtract).then_inc(split[2], 1)

                def chunk(c, parity, down=True, v=None, last=False):
                    split_low(0, c + b0[0] + 1)
                    hidden(c, parity)
                    hidden_low(c, parity)
                    split_low(1, c + b0[1] + 1)
                    if v is not None:
                        ada_rows(v)
                    if last:
                        last_halves()
                    elif down:
                        split_low(2, c + b0[2])
                    if v is not None:
                        ada_mod(v)

                chunk(0, 0, down=False)
                pairs = (count - 2) // 2
                if vec is None:
                    nv = 0
                else:
                    with dve.Fori(0, min(nv, pairs)) as i:
                        for half in range(2):
                            chunk(i * 2 + 1 + half, (1 + half) % 2, v=i + vec if half else None)
                if nv < pairs:
                    with dve.Fori(nv, pairs) as i:
                        for half in range(2):
                            chunk(i * 2 + 1 + half, (1 + half) % 2)
                for c in range(2 * pairs + 1, count):
                    chunk(c, c % 2, v=vec + nv - 1 if nv > pairs and c == 2 * nv else None,
                          last=(c == count - 1))
                for s in range(3):
                    turn[s] = b0[s] + count + (s < 2)

            def add_output(stage, scale=None, half=False, vectors=0):
                if half:
                    dve.wait_ge(sem("mod_ready"), vectors)
                    link(dve.tensor_scalar(ghalf[:, :], scale, 0.5, None, ALU.mult))
                    scale = ghalf
                for k in range(KT):
                    src = ps[:, 2 + k // 2, (k % 2) * T:(k % 2 + 1) * T]
                    if k in (0, 2, 4):
                        wait("out_pair")
                    elif k == 6:
                        dve.wait_ge(used[2], first[stage][2] + dict(STAGES)[stage])
                    if scale is None:
                        if k % 2 == 0:
                            continue
                        ins = dve.tensor_tensor(xT[:, k - 1:k + 1, :], ps[:, 2 + k // 2, :].rearrange("p (n t) -> p n t", n=2),
                                                xT[:, k - 1:k + 1, :], ALU.add)
                    else:
                        ins = stt(xT[:, k, :], src, scale[:, k:k + 1], xT[:, k, :])
                    if k % 2:
                        ins.then_inc(sem("x_ready"), 1)

            def add_units(stage, u0, gate):
                for j in range(4):
                    s, b = (u0 + j) % 3, (u0 + j) % 2 + (2 if stage == "blk2" else 0)
                    dve.wait_ge(used[s], first[stage][s] + (u0 + j) // 3 + 1)
                    if gate is None:
                        dve.tensor_tensor(xT[:, 2 * j:2 * j + 2, :], ps[:, b, :].rearrange("p (n t) -> p n t", n=2),
                                          xT[:, 2 * j:2 * j + 2, :], ALU.add).then_inc(sem("x_ready"), 1)
                    else:
                        stt(xT[:, 2 * j, :], ps[:, b, 0:T], gate[:, 2 * j:2 * j + 1], xT[:, 2 * j, :])
                        stt(xT[:, 2 * j + 1, :], ps[:, b, T:2 * T], gate[:, 2 * j + 1:2 * j + 2], xT[:, 2 * j + 1, :]).then_inc(sem("x_ready"), 1)
                    if j < 3:
                        refill(s)

            chunked("ffn0", 2)
            add_output("ffn0", mod(0, 2), half=True, vectors=3)
            norm(ng(0, 1), mod(0, 3), mod(0, 4), vectors=5)
            refill(2)

            def mix_low(sl):
                wait("mix_high")
                dve.tensor_tensor(mlo[:, sl, :], hf[:, sl, :], mhi[:, sl, :].bitcast(F32), ALU.subtract).then_inc(sem("mix_split"), 1)

            def qk_norm(i):
                wait("stat_read")
                link(dve.reciprocal(rstd[:, :], root[:, :]))
                dst = (q0 if i < 2 else k0)[:, 2 * (i % 2):2 * (i % 2) + 2, :]
                stt(dst, dst, qk_gain[:, i // 2:i // 2 + 1], rstd[:, :].rearrange("p (n t) -> p n t", n=2), ALU.mult, ALU.mult).then_inc(sem("qk_ready"), 1)

            qk_gain = col("qk_g", 0, 2)
            link(dve.tensor_scalar(qk_gain[:, 0:1], qk_gain[:, 0:1], 64 ** -0.5, None, ALU.mult))
            causal = c_("causal")

            def negative_max(i):
                wait("scores_ready")
                e, b = i % 4, 2 + i % 4
                diag = ps[:, b, :].rearrange("p (j n) -> p j n", j=2)[:, :, 0:P]
                link(dve.tensor_tensor(diag, diag, causal.rearrange("p (o n) -> p o n", o=1).to_broadcast([P, 2, P]), ALU.add))
                dve.tensor_reduce(negmax[:, e, 0:1], ps[:, b, 0:P], AX_X, ALU.max, negate=True)
                dve.tensor_reduce(negmax[:, e, 1:2], ps[:, b, P:3 * P], AX_X, ALU.max, negate=True).then_inc(sem("negmax_ready"), 1)

            def difference(h):
                e = (2 * h) % 4
                wait("exp_done", 2)
                link(dve.reciprocal(zinv[:, e:e + 2, :], zsum[:, e:e + 2, :]))
                link(dve.tensor_scalar(zinv[:, e + 1, :], zinv[:, e + 1, :], lam[:, 4:5], None, ALU.mult))
                pa = [exps[:, e, 0:P], exps[:, e, P:3 * P]]
                pb = [exps[:, e + 1, 0:P], exps[:, e + 1, P:3 * P]]
                dve.tensor_scalar(pa[0], pa[0], zinv[:, e, 0:1], None, ALU.mult)
                link(dve.tensor_scalar(pa[1], pa[1], zinv[:, e, 1:2], None, ALU.mult))
                stt(pa[0], pb[0], zinv[:, e + 1, 0:1], pa[0])
                stt(pa[1], pb[1], zinv[:, e + 1, 1:2], pa[1]).then_inc(sem("probs_ready"), 1)

            for u in range(8):
                if u == 7:
                    negative_max(0)
                    negative_max(1)
                refill(u % 3)
                if u == 3:
                    ada_rows(7)
                if u == 4:
                    ada_mod(7)
                if u == 7:
                    ada_rows(8)
                if 1 <= u <= 4:
                    qk_norm(u - 1)
            for h in range(4):
                difference(h)
                if h < 3:
                    negative_max(2 * h + 2)
                    negative_max(2 * h + 3)
                if h == 0:
                    ada_mod(8)
            mix_low(slice(4, 6))
            mix_low(slice(6, 8))
            for j in range(2):
                wait("stat_read")
                link(dve.reciprocal(rstd[:, :], root[:, :]))
                stt(hf[:, 2 * j:2 * j + 2, :], hf[:, 2 * j:2 * j + 2, :], col("subln"), rstd[:, :].rearrange("p (n t) -> p n t", n=2),
                    ALU.mult, ALU.mult).then_inc(sem("o_normed"), 1)
            mix_low(slice(0, 2))
            mix_low(slice(2, 4))
            add_units("mix0", 8, mod(0, 5))
            norm(ng(0, 2), mod(0, 6), mod(0, 7), vectors=8)
            refill(2)
            chunked("ffn1", 9)
            add_output("ffn1", mod(0, 8), half=True, vectors=9)
            norm(ng(1, 0), mod(1, 0), mod(1, 1), vectors=11)
            refill(2)
            chunked("ffn2", 14, 4)
            add_output("ffn2", mod(1, 2), half=True, vectors=12)

            norm(ng(1, 1), mod(1, 3), mod(1, 4), vectors=18)
            refill(2)
            link(dve.memset(vconv[:, :, 0:2], 0.0))
            for j in range(4):
                refill(0)
                u = 3 * j + 1
                wait("evacuated")
                dve.wait_ge(used[1], first["mix1"][1] + j + 1)
                dve.tensor_tensor(vconv[:, :, 2:T + 2], cgate.rearrange("p (n t) -> p n t", n=2),
                                  ps[:, u % 2, :].rearrange("p (n t) -> p n t", n=2), ALU.mult).then_inc(sem("v_done"), 1)
                refill(1)
                dve.wait_ge(sem("v_done"), j + 1)
                for tap in range(3):
                    for m in range(2):
                        w = col("conv_w", tap * KT + 2 * j + m)
                        if tap == 0:
                            ins = dve.tensor_scalar(yconv[:, m, :], vconv[:, m, 0:T], w, None, ALU.mult)
                        else:
                            ins = stt(yconv[:, m, :], vconv[:, m, tap:tap + T], w, yconv[:, m, :])
                        if m:
                            link(ins)
                dve.wait_ge(used[2], first["mix1"][2] + j + 1)
                dve.tensor_tensor(hf[:, 2 * j:2 * j + 2, :], yconv, ps[:, (u + 1) % 2, :].rearrange("p (n t) -> p n t", n=2),
                                  ALU.mult).then_inc(sem("y_done"), 1)
                refill(2)
                mix_low(slice(2 * j, 2 * j + 2))
            add_units("mix1", 12, mod(1, 5))
            norm(ng(1, 2), mod(1, 6), mod(1, 7), vectors=18, slot=0)
            chunked("ffn3")
            add_output("ffn3", mod(1, 8), half=True, vectors=18)

            norm(col("attn_norm", 0, KT), None)
            refill(2)
            cos_b, sin_b, cos_a, sin_a = (c_(x) for x in ("cos_moba", "sin_moba", "cos_mla", "sin_mla"))

            def both(t, rows):
                return t[rows, :].rearrange("p (o t) -> p o t", o=1).to_broadcast([rows.stop - rows.start, 2, T])

            def rope(r):
                wait("rope_swapped")
                if r:
                    dve.wait_ge(sem("roped"), r)
                b = (7, 6)[r % 2]
                if r == 0:
                    rows = slice(64, 96)
                    dve.tensor_tensor(swapped[rows, 0, :], ps[rows, b, 0:T], sin_a[rows, :], ALU.mult).then_inc(sem("rope_read"), 1)
                    link(dve.tensor_tensor(krope[rows, :], krope[rows, :], cos_a[rows, :], ALU.mult))
                    dve.wait_ge(sem("rope_read"), r + 1)
                    link(dve.tensor_tensor(krope[rows, :], krope[rows, :], swapped[rows, 0, :], ALU.add))
                    dve.tensor_copy(kA[rows, :, :], krope[rows, :].rearrange("p (o t) -> p o t", o=1).to_broadcast([32, MLA_H, T])).then_inc(sem("roped"), 1)
                    return
                if r < 5:
                    rows, c, s = slice(0, P), cos_b, sin_b
                    x = q0[:, 2 * (r - 1):2 * r, :] if r < 3 else k0[:, 2 * (r - 3):2 * (r - 2), :]
                else:
                    rows, c, s = slice(64, 96), cos_a, sin_a
                    x = qA[rows, 2 * (r - 5):2 * (r - 4), :]
                sw = swapped[rows, :, :]
                dve.tensor_tensor(sw, ps[rows, b, :].rearrange("p (n t) -> p n t", n=2), both(s, rows), ALU.mult).then_inc(sem("rope_read"), 1)
                link(dve.tensor_tensor(x, x, both(c, rows), ALU.mult))
                dve.wait_ge(sem("rope_read"), r + 1)
                dve.tensor_tensor(x, x, sw, ALU.add).then_inc(sem("roped"), 1)

            def latent(j):
                wait("stat_read")
                sl = slice(j * T, (j + 1) * T)
                link(dve.reciprocal(rstd[:, sl], root[:, sl]))
                for k in range(*((0, 6) if j == 0 else (6, 8))):
                    g = col("q_norm", k) if j == 0 else col("kv_norm", k - 6)
                    ins = stt(hf[:, k, :], hf[:, k, :], g, rstd[:, sl], ALU.mult, ALU.mult)
                ins.then_inc(sem("latent_normed"), 1)

            def latent_low(j):
                wait("latent_high")
                sl = slice(0, 6) if j == 0 else slice(6, 8)
                dve.tensor_tensor(mlo[:, sl, :], hf[:, sl, :], mhi[:, sl, :].bitcast(F32), ALU.subtract).then_inc(sem("latent_split"), 1)

            for u in range(11):
                refill(u % 3)
                if u == 4:
                    latent(0)
                if u == 5:
                    latent(1)
                    rope(0)
                if 6 <= u < 10:
                    rope(u - 5)
                if u == 8:
                    latent_low(0)
                    latent_low(1)
            refill(2)
            for u in UQ_UNITS:
                refill(u % 3)
                if u > UQ_UNITS[0]:
                    rope(5 + u - UQ_UNITS[0] - 1)
            rope(8)

            def normalised(i):
                e = i % 4
                wait("exp_done")
                link(dve.reciprocal(zinv[:, e, :], zsum[:, e, :]))
                dve.tensor_scalar(exps[:, e, 0:P], exps[:, e, 0:P], zinv[:, e, 0:1], None, ALU.mult)
                dve.tensor_scalar(exps[:, e, P:3 * P], exps[:, e, P:3 * P], zinv[:, e, 1:2], None, ALU.mult).then_inc(sem("probs_ready"), 1)

            def o_low(j):
                tile_ = 4 + j if j < 4 else j - 4
                wait("o_high")
                dve.tensor_tensor(mlo[:, tile_, :], ps[:, 6, 0:T], mhi[:, tile_, :].bitcast(F32), ALU.subtract).then_inc(sem("o_split"), 1)

            negative_max(0)
            negative_max(1)
            normalised(0)
            for i in range(16):
                if i + 2 < 16:
                    negative_max(i + 2)
                if i + 1 < 16:
                    normalised(i + 1)
                if i % 2:
                    if i > 1:
                        o_low(i // 2 - 1)
                    refill((16 + i // 2) % 3)
            o_low(7)
            for j in range(2):
                banks = ((2, 4), (0, 6))[j]
                for which in range(2 - j):
                    refill((24 + 2 * j + which) % 3)
                for which in range(2):
                    u = 24 + 2 * j + which
                    dve.wait_ge(used[u % 3], first["blk2"][u % 3] + u // 3 + 1)
                    if which == 0:
                        wait("gates_ready")
                    g = gates[:, which, 4 * j:4 * j + 4, :]
                    src = ps[:, banks[which]:banks[which] + 2, :].rearrange("p b (n t) -> p (b n) t", n=2)
                    link(dve.tensor_tensor(hf[:, 4 * j:4 * j + 4, :] if which == 0 else g, g, src, ALU.mult))
                dve.tensor_tensor(hf[:, 4 * j:4 * j + 4, :], hf[:, 4 * j:4 * j + 4, :], gates[:, 1, 4 * j:4 * j + 4, :], ALU.add).then_inc(sem("mixed"), 1)
                wait("mixed_high")
                dve.tensor_tensor(hlo[:, 4 * j:4 * j + 4, :], hf[:, 4 * j:4 * j + 4, :], hhi[:, 4 * j:4 * j + 4, :].bitcast(F32),
                                  ALU.subtract).then_inc(sem("mixed_split"), 1)
            refill(27 % 3)
            add_units("blk2", 28, None)

            norm(col("ffn_norm", 0, KT), None, final=True)
            refill(1)

            def htok_low(j):
                wait("htok_high", 2)
                for t in range(2):
                    sl = slice(j * 512, (j + 1) * 512)
                    ins = dve.tensor_tensor(htok_lo[:, t, sl], ps[:, 2 * t + j, :], htok_hi[:, t, sl].bitcast(F32), ALU.subtract)
                ins.then_inc(sem("htok_split"), 1)

            htok_low(0)
            wait("logits_ready")
            dve.tensor_copy(adarow[0:NG + NE, :], ps[0:NG + NE, 7, 0:T]).then_inc(sem("logits_copied"), 1)
            wait("logits_turned")
            link(dve.tensor_copy(logit[:, :, :], ps[:, 6, 0:P].rearrange("p (t n) -> p t n", t=2)[:, :, 0:NG + NE]))
            rank = c_("rank")

            def r_(o, n):
                return rt[:, o:o + 2 * n].rearrange("p (t n) -> p t n", t=2)

            def spread(x, n):
                return x.to_broadcast([P, 2, n])

            def first_best(x, best, cand, hot, n):
                link(dve.tensor_reduce(best, x, AX_X, ALU.max))
                link(dve.tensor_tensor(cand, x, spread(best, n), ALU.is_equal))
                link(dve.tensor_tensor(cand, cand, rank[:, 8 - n:8].rearrange("p (o n) -> p o n", o=1).to_broadcast([P, 2, n]), ALU.mult))
                link(dve.tensor_reduce(r_(252, 1), cand, AX_X, ALU.max))
                link(dve.tensor_tensor(hot, cand, spread(r_(252, 1), n), ALU.is_equal))

            gl = logit[:, :, 0:NG]
            el = logit[:, :, NG:NG + NE].rearrange("p t (g e) -> p t g e", g=NG)
            gbest, ghot, gcand = r_(0, 1), r_(2, NG), r_(10, NG)
            first_best(gl, gbest, gcand, ghot, NG)
            dve.tensor_tensor(r_(56, NG), gl, spread(gbest, NG), ALU.subtract).then_inc(sem("router_max"), 1)
            htok_low(1)

            wait("ranked")
            in_group = place[:, 0:2 * NG].rearrange("p (t n) -> p t n", t=2)
            before, beyond = place[:, 8:10], place[:, 10:12]
            link(dve.tensor_tensor(in_group, ps[:, 4, 0:2 * NG].rearrange("p (t n) -> p t n", t=2), ghot, ALU.mult))
            link(dve.tensor_reduce(before.rearrange("p (t o) -> p t o", t=2), in_group, AX_X, ALU.add))
            link(dve.tensor_scalar(beyond, before, float(P), None, ALU.subtract))
            over = place[:, 12:16]
            link(dve.tensor_scalar(over, ps[:, 4, 2 * NG:3 * NG], float(P), None, ALU.is_gt))
            for t in range(2):
                for b in range(NG):
                    dve.tensor_scalar(pick[:, t, b, :], c_("iota"), before[:, t:t + 1], ghot[:, t, b:b + 1],
                                      ALU.is_equal, ALU.mult)
                ins = dve.tensor_scalar(pick[:, t, NG, :], c_("iota"), beyond[:, t:t + 1], None, ALU.is_equal)
            ins.then_inc(sem("picked"), 1)
            link(dve.tensor_reduce(place[:, 16:17], over, AX_X, ALU.add))
            link(dve.tensor_tensor(over, over, c_("group_base"), ALU.mult))
            link(dve.tensor_reduce(place[:, 17:18], over, AX_X, ALU.add))
            dve.tensor_copy(overflow[:, :], place[:, 16:18]).then_inc(sem("overflow_known"), 1)
            wait("router_exp")
            pg = r_(18, 1)
            link(dve.tensor_reduce(pg, r_(64, NG), AX_X, ALU.add))
            link(dve.reciprocal(pg, pg))
            picked = r_(72, EG)
            link(dve.tensor_tensor(picked, el[:, :, 0, :], spread(ghot[:, :, 0:1], EG), ALU.mult))
            tmp = r_(88, EG)
            for g in range(1, NG):
                link(dve.tensor_tensor(tmp, el[:, :, g, :], spread(ghot[:, :, g:g + 1], EG), ALU.mult))
                link(dve.tensor_tensor(picked, picked, tmp, ALU.add))
            best1, hot1 = r_(20, 1), r_(104, EG)
            first_best(picked, best1, tmp, hot1, EG)
            rest = r_(136, EG)
            link(dve.tensor_scalar(rest, hot1, BIG, None, ALU.mult))
            link(dve.tensor_tensor(rest, rest, picked, ALU.add))
            best2, hot2 = r_(22, 1), r_(152, EG)
            first_best(rest, best2, tmp, hot2, EG)
            dve.tensor_tensor(r_(128, 1), best2, best1, ALU.subtract).then_inc(sem("router_two"), 1)
            for k in range(KT):
                wait("gathered_high")
                dve.tensor_tensor(hlo[:, k, :], ps[:, k, 0:T], hhi[:, k, :].bitcast(F32), ALU.subtract)
                dve.tensor_tensor(mlo[:, k, :], ps[:, k, T:2 * T], mhi[:, k, :].bitcast(F32), ALU.subtract).then_inc(sem("gathered_split"), 1)
            wait("router_exp")
            w1, w2 = r_(24, 1), r_(26, 1)
            link(dve.tensor_scalar(w1, r_(130, 1), 1.0, None, ALU.add))
            link(dve.reciprocal(w1, w1))
            link(dve.tensor_tensor(w1, w1, pg, ALU.mult))
            link(dve.tensor_tensor(w2, w1, r_(130, 1), ALU.mult))
            link(dve.tensor_tensor(hot1, hot1, spread(w1, EG), ALU.mult))
            link(dve.tensor_tensor(hot2, hot2, spread(w2, EG), ALU.mult))
            dve.tensor_tensor(hot1, hot1, hot2, ALU.add).then_inc(sem("slot_weights"), 1)

            def expert_low(s, e, p):
                dve.wait_ge(high[s], e + (b_moe[s] + 1))
                dve.tensor_tensor(wlo[s][:, :], weights_of(s, p), whi[s][:, :].bitcast(F32), ALU.subtract).then_inc(split[s], 1)

            def expert_hidden(e, p):
                dve.wait_ge(sem("moe_silu"), e + 1)
                if not isinstance(e, int) or e >= 2:
                    dve.wait_ge(sem("moe_turned"), e - 1)
                w = slot_w[:, bass.ds(e, 1)] if not isinstance(e, int) else slot_w[:, e:e + 1]
                stt(hid2[:, p, :], silu2[:, p, :], w, ps[:, p, CH:2 * CH], ALU.mult, ALU.mult).then_inc(sem("moe_hidden"), 1)

            def hidden_low(e, p):
                dve.wait_ge(sem("moe_high"), e + 1)
                dve.tensor_tensor(hidlo[p][:, 0, :], ps[:, 2, p * T:(p + 1) * T], hidhi[p][:, 0, :].bitcast(F32),
                                  ALU.subtract).then_inc(sem("moe_split"), 1)

            def output_low(g):
                dve.wait_ge(sem("y_high"), g + 1)
                dve.tensor_tensor(y_lo[:, :].rearrange("p (b n) -> p b n", b=2), ps[:, 6:8, :],
                                  y_hi[:, :].bitcast(F32).rearrange("p (b n) -> p b n", b=2), ALU.subtract).then_inc(sem("y_split"), 1)

            def output_add(g, pairs=range(4)):
                for pr in pairs:
                    q = 4 * g + pr
                    dve.wait_ge(sem("scattered"), q + 1)
                    if g:
                        dve.wait_ge(sem("x_added"), q - 3)
                    x = xT[:, 2 * pr:2 * pr + 2, :]
                    dve.tensor_tensor(x, ps[:, 3 + q % 3, :].rearrange("p (n t) -> p n t", n=2), x, ALU.add).then_inc(sem("x_added"), 1)

            def expert_block(g, ends):
                def step(e, p, j):
                    hidden_low(e, p)
                    if follows(j, ends, 2):
                        expert_low(0, e + 2, p)
                    if follows(j, ends, 1):
                        expert_hidden(e + 1, 1 - p)
                    if follows(j, ends, 2):
                        expert_low(1, e + 2, p)
                    if j in BESIDE and 0 < g < NG:
                        output_add(g - 1, BESIDE[j])
                    if j == EG - 1:
                        output_low(g)
                    if follows(j, ends, 1):
                        expert_low(2, e + 1, 1 - p)

                experts_of(dve, g, step, ends)
                if ends:
                    output_add(g)

            expert_low(0, 1, 1)
            wait("slot_weights_out")
            link(dve.tensor_copy(slot_w, ps[:, 7, 0:(NG + 1) * EG]))
            expert_hidden(0, 0)
            expert_low(1, 1, 1)
            for g in range(NG):
                expert_block(g, g == NG - 1)
            dve.wait_ge(sem("overflow_known"), 1)
            has_fifth = dve.value_load(overflow[0:1, 0:1], min_val=0, max_val=1)
            with dve.If(has_fifth > 0):
                for j in range(2):
                    dve.wait_ge(sem("fifth_high"), j + 1)
                    sl = slice(4 * j, 4 * j + 4)
                    dve.tensor_tensor(hlo[:, sl, 0:P], ps[:, j, :].rearrange("p (k n) -> p k n", k=4),
                                      hhi[:, sl, 0:P].bitcast(F32), ALU.subtract).then_inc(sem("fifth_split"), 1)
                for s in range(3):
                    expert_low(s, NE, 0)
                expert_low(0, NE + 1, 1)
                expert_hidden(NE, 0)
                expert_low(1, NE + 1, 1)
                expert_block(NG, True)
                dve.wait_ge(sem("x_added"), 4 * (NG + 1))
            dve.wait_ge(sem("x_added"), 4 * NG)
            dve.memset(place[:, 0:1], 0.0).then_inc(sem("x_ready"), 4)
            norm(col("final_norm", 0, KT), None, final=True)


_INS = ["x", "c", "norm_g", "w_ada", "b_ada", "ffn_wg", "ffn_wu", "ffn_wd", "w_in_ab", "qk_norm_g", "lambda_q1",
        "lambda_k1", "lambda_q2", "lambda_k2", "subln_g", "pool_w", "pool_scale", "w_out_ab", "w_in_c", "conv_w",
        "w_out_c", "attn_norm_2", "w_in_2", "q_norm_2", "w_uq_2", "kv_norm_2", "w_ukv_2", "w_o_mla_2", "w_o_moba_2",
        "w_out_2", "ffn_norm_2", "w_router_group_2", "b_router_group_2", "w_router_expert_2", "b_router_expert_2",
        "w_exp_gate_2", "w_exp_up_2", "w_exp_down_2", "final_norm_2"]


def kernel(**inputs):
    import concourse.bacc as _bacc
    from concourse.bass_utils import run_bass_kernel_spmd as _run

    nc = _bacc.Bacc("TRN2", target_bir_lowering=False, num_devices=1)
    arrays, aps = {}, {}
    for name in _INS:
        a = np.ascontiguousarray(inputs[name])
        arrays[f"in_{name}_dram"] = a
        aps[name] = nc.dram_tensor(f"in_{name}_dram", a.shape, mybir.dt.from_np(a.dtype), kind="ExternalInput").ap()
    table, _ = constants()
    arrays["const_dram"] = table
    const_dram = nc.dram_tensor("const_dram", table.shape, F32, kind="ExternalInput").ap()
    out = nc.dram_tensor("out_0_dram", (1, T, D), F32, kind="ExternalOutput").ap()
    build(nc, aps, const_dram, out)
    r = _run(nc, [arrays], core_ids=[0])
    return r.results[0]["out_0_dram"]
```
